# Optimizing a Trainium2 kernel written in Bass

```python
import math
import jax, jax.numpy as jnp
from jax import lax
import numpy as np

"""One inference step (DEPTH layers) of a hybrid decoder trunk with parallel head groups.

Each layer: one combined input projection whose columns feed two head groups reading the same input:
  group A: chunked gMLP spatial gating (4 heads x 128 ch, causal 128x128 lower-triangular W_s per head)
  group B: S5 diagonal complex state-space layer (32 channel groups of 16, one 64-dim complex state each,
           ZOH discretisation, associative scan), output Re(C h) + D x, then GELU + GLU
  concat -> one output projection -> DeepNorm post-LN residual -> grouped top-2 MoE with a router shared
  by all layers -> DeepNorm post-LN residual.

Inputs:
  x_prompt (BATCH, SEQ, D_MODEL), x_sample (DEC_BATCH, DEC_SEQ, D_MODEL)
  state_ssm_re / state_ssm_im (DEPTH, DEC_BATCH, G_B, N_STATE): carried S5 state of the sample group
  weights (see setup_inputs).
Outputs (tuple):
  y_prompt (BATCH, SEQ, D_MODEL)
  y_sample (DEC_BATCH, DEC_SEQ, D_MODEL)
  new_ssm_re_prompt, new_ssm_im_prompt (DEPTH, BATCH, G_B, N_STATE)
  new_ssm_re_sample, new_ssm_im_sample (DEPTH, DEC_BATCH, G_B, N_STATE)
  new_chunk_v_sample (DEPTH, DEC_BATCH, DEC_SEQ, W_A): normalised v rows of the new chunk
"""

D_MODEL = 1024
BATCH = 1
SEQ = 2048
DEPTH = 1
DEC_BATCH = 8
DEC_SEQ = 1
PAST_LEN = 16384
PAGE_SIZE = 128

D_MIX = D_MODEL
W_A = D_MIX // 2
W_B = D_MIX - W_A
CHUNK = 128
H_A = 4
P_A = W_A // H_A
GROUP_B = 16
G_B = W_B // GROUP_B
N_STATE = 64
D_IN = 2 * W_A + W_B
N_EXPERTS = 16
N_EXPERT_GROUPS = 4
EXPERTS_PER_GROUP = N_EXPERTS // N_EXPERT_GROUPS
TOP_K = 2
D_FF_EXPERT = D_MODEL // 4
DEEPNORM_ALPHA = (2 * DEPTH) ** 0.25
DEEPNORM_BETA = (8 * DEPTH) ** -0.25
LN_EPS = 1e-5
DT_MIN = 1e-3
DT_MAX = 1e-1

kernel_name = "hymba_gmlp_s5_sharedrouter_moe_step"

def layer_norm(x, g, b):
    xf = x.astype(jnp.float32)
    mu = xf.mean(-1, keepdims=True)
    var = jnp.square(xf - mu).mean(-1, keepdims=True)
    y = (xf - mu) * lax.rsqrt(var + LN_EPS) * g.astype(jnp.float32) + b.astype(jnp.float32)
    return y.astype(x.dtype)

def cmul(ar, ai, br, bi):
    return ar * br - ai * bi, ar * bi + ai * br

def chunk_spatial_gate(v, w_s, b_s):
    bt, s = v.shape[:2]
    l = min(s, CHUNK)
    vc = v.reshape(bt, s // l, l, H_A, P_A)
    w = jnp.tril(w_s[:, :l, :l])
    out = jnp.einsum('hlm,bcmhp->bclhp', w, vc) + b_s[:, :l].T[:, :, None]
    return out.reshape(bt, s, H_A, P_A)

def s5_mixer(xs, h0_re, h0_im, a_re, a_im, log_dt, b_re, b_im, c_re, c_im, d_skip, w_glu, b_glu):
    f32 = jnp.float32
    xf = xs.astype(f32)
    a_re = a_re.astype(f32)
    a_im = a_im.astype(f32)
    dt = jnp.exp(log_dt.astype(f32))[:, None]
    decay = jnp.exp(a_re * dt)
    lb_re, lb_im = decay * jnp.cos(a_im * dt), decay * jnp.sin(a_im * dt)
    den = a_re * a_re + a_im * a_im
    nr, ni = lb_re - 1.0, lb_im
    zr = (nr * a_re + ni * a_im) / den
    zi = (ni * a_re - nr * a_im) / den
    bb_re, bb_im = cmul(zr[..., None], zi[..., None], b_re.astype(f32), b_im.astype(f32))
    bu_re = jnp.einsum('bsgp,gnp->bsgn', xf, bb_re)
    bu_im = jnp.einsum('bsgp,gnp->bsgn', xf, bb_im)
    s = xs.shape[1]
    la_re = jnp.broadcast_to(lb_re, (1, s) + lb_re.shape)
    la_im = jnp.broadcast_to(lb_im, (1, s) + lb_im.shape)

    def combine(e1, e2):
        a1r, a1i, b1r, b1i = e1
        a2r, a2i, b2r, b2i = e2
        ar, ai = cmul(a2r, a2i, a1r, a1i)
        br, bi = cmul(a2r, a2i, b1r, b1i)
        return ar, ai, br + b2r, bi + b2i

    ac_re, ac_im, h_re, h_im = lax.associative_scan(combine, (la_re, la_im, bu_re, bu_im), axis=1)
    ir, ii = cmul(ac_re, ac_im, h0_re.astype(f32)[:, None], h0_im.astype(f32)[:, None])
    h_re = h_re + ir
    h_im = h_im + ii
    y = (jnp.einsum('bsgn,gpn->bsgp', h_re, c_re.astype(f32))
         - jnp.einsum('bsgn,gpn->bsgp', h_im, c_im.astype(f32))
         + d_skip.astype(f32) * xf)
    y = jax.nn.gelu(y)
    z = y * jax.nn.sigmoid(jnp.einsum('bsgp,gpq->bsgq', y, w_glu.astype(f32)) + b_glu.astype(f32))
    return z.astype(xs.dtype), h_re[:, -1], h_im[:, -1]

def grouped_moe(x, w_router, router_bias, w_gate, w_up, w_down):
    f32 = jnp.float32
    bt, s, d = x.shape
    xt = x.reshape(bt * s, d)
    scores = jax.nn.sigmoid((xt @ w_router).astype(f32))
    biased = scores + router_bias.astype(f32)
    grouped = biased.reshape(-1, N_EXPERT_GROUPS, EXPERTS_PER_GROUP)
    group_score = lax.top_k(grouped, TOP_K)[0].sum(-1)
    sel_group = jnp.argmax(group_score, axis=-1)
    expert_group = jnp.arange(N_EXPERTS) // EXPERTS_PER_GROUP
    masked = jnp.where(expert_group[None, :] == sel_group[:, None], biased, -jnp.inf)
    _, top_idx = lax.top_k(masked, TOP_K)
    top_s = jnp.take_along_axis(scores, top_idx, axis=-1)
    gates = top_s / top_s.sum(-1, keepdims=True)
    comb = (jax.nn.one_hot(top_idx, N_EXPERTS, dtype=f32) * gates[..., None]).sum(1)
    out = jnp.zeros(xt.shape, f32)
    for e in range(N_EXPERTS):
        h = jax.nn.silu(xt @ w_gate[e]) * (xt @ w_up[e])
        out = out + comb[:, e:e + 1] * (h @ w_down[e]).astype(f32)
    return out.astype(x.dtype).reshape(bt, s, d)

def hybrid_layer(x, h0_re, h0_im, w_in, w_out, ln_v_g, ln_v_b, w_s, b_s, ssm_a_re, ssm_a_im,
                 ssm_log_dt, ssm_b_re, ssm_b_im, ssm_c_re, ssm_c_im, ssm_d, w_glu, b_glu,
                 ln1_g, ln1_b, ln2_g, ln2_b, w_router, router_bias, w_gate, w_up, w_down):
    bt, s, _ = x.shape
    proj = x @ w_in
    u = jax.nn.gelu(proj[..., :W_A])
    v = layer_norm(jax.nn.gelu(proj[..., W_A:2 * W_A]), ln_v_g, ln_v_b)
    xs = proj[..., 2 * W_A:].reshape(bt, s, G_B, GROUP_B)
    y_a = u * chunk_spatial_gate(v.reshape(bt, s, H_A, P_A), w_s, b_s).reshape(bt, s, W_A)
    y_b, h_re, h_im = s5_mixer(xs, h0_re, h0_im, ssm_a_re, ssm_a_im, ssm_log_dt, ssm_b_re, ssm_b_im,
                               ssm_c_re, ssm_c_im, ssm_d, w_glu, b_glu)
    mix = jnp.concatenate([y_a, y_b.reshape(bt, s, W_B)], axis=-1) @ w_out
    x = layer_norm(DEEPNORM_ALPHA * x + mix, ln1_g, ln1_b)
    x = layer_norm(DEEPNORM_ALPHA * x + grouped_moe(x, w_router, router_bias, w_gate, w_up, w_down), ln2_g, ln2_b)
    return x, h_re, h_im, v

def setup_inputs(seed: int = 0) -> dict:
    key = jax.random.key(seed)
    ks = jax.random.split(key, 32)
    nrm = jax.random.normal
    f32 = jnp.float32
    x_prompt = nrm(ks[0], (BATCH, SEQ, D_MODEL), f32)
    x_sample = nrm(ks[1], (DEC_BATCH, DEC_SEQ, D_MODEL), f32)
    state_ssm_re = 0.5 * nrm(ks[2], (DEPTH, DEC_BATCH, G_B, N_STATE), f32)
    state_ssm_im = 0.5 * nrm(ks[3], (DEPTH, DEC_BATCH, G_B, N_STATE), f32)
    w_in = nrm(ks[4], (DEPTH, D_MODEL, D_IN), f32) * D_MODEL ** -0.5
    w_out = nrm(ks[5], (DEPTH, D_MIX, D_MODEL), f32) * (D_MIX ** -0.5 * DEEPNORM_BETA)
    ln_v_g = 1.0 + 0.05 * nrm(ks[6], (DEPTH, W_A), f32)
    ln_v_b = 0.02 * nrm(ks[7], (DEPTH, W_A), f32)
    w_s = nrm(ks[8], (DEPTH, H_A, CHUNK, CHUNK), f32) * CHUNK ** -0.5
    b_s = 1.0 + 0.1 * nrm(ks[9], (DEPTH, H_A, CHUNK), f32)
    ssm_a_re = -0.5 + 0.01 * nrm(ks[10], (DEPTH, G_B, N_STATE), f32)
    ssm_a_im = (jnp.pi * jnp.arange(N_STATE, dtype=f32))[None, None, :] + 0.01 * nrm(ks[11], (DEPTH, G_B, N_STATE), f32)
    ssm_log_dt = math.log(DT_MIN) + jax.random.uniform(ks[12], (DEPTH, G_B), f32) * (math.log(DT_MAX) - math.log(DT_MIN))
    ssm_b_re = nrm(ks[13], (DEPTH, G_B, N_STATE, GROUP_B), f32) * (2 * GROUP_B) ** -0.5
    ssm_b_im = nrm(ks[14], (DEPTH, G_B, N_STATE, GROUP_B), f32) * (2 * GROUP_B) ** -0.5
    ssm_c_re = nrm(ks[15], (DEPTH, G_B, GROUP_B, N_STATE), f32) * (2 * N_STATE) ** -0.5
    ssm_c_im = nrm(ks[16], (DEPTH, G_B, GROUP_B, N_STATE), f32) * (2 * N_STATE) ** -0.5
    ssm_d = nrm(ks[17], (DEPTH, G_B, GROUP_B), f32)
    w_glu = nrm(ks[18], (DEPTH, G_B, GROUP_B, GROUP_B), f32) * GROUP_B ** -0.5
    b_glu = 0.02 * nrm(ks[19], (DEPTH, G_B, GROUP_B), f32)
    ln1_g = 1.0 + 0.05 * nrm(ks[20], (DEPTH, D_MODEL), f32)
    ln1_b = 0.02 * nrm(ks[21], (DEPTH, D_MODEL), f32)
    ln2_g = 1.0 + 0.05 * nrm(ks[22], (DEPTH, D_MODEL), f32)
    ln2_b = 0.02 * nrm(ks[23], (DEPTH, D_MODEL), f32)
    w_router = nrm(ks[24], (D_MODEL, N_EXPERTS), f32) * D_MODEL ** -0.5
    router_bias = 0.01 * nrm(ks[25], (N_EXPERTS,), f32)
    w_gate = nrm(ks[26], (DEPTH, N_EXPERTS, D_MODEL, D_FF_EXPERT), f32) * D_MODEL ** -0.5
    w_up = nrm(ks[27], (DEPTH, N_EXPERTS, D_MODEL, D_FF_EXPERT), f32) * D_MODEL ** -0.5
    w_down = nrm(ks[28], (DEPTH, N_EXPERTS, D_FF_EXPERT, D_MODEL), f32) * (D_FF_EXPERT ** -0.5 * DEEPNORM_BETA)
    return {"x_prompt": x_prompt, "x_sample": x_sample, "state_ssm_re": state_ssm_re,
            "state_ssm_im": state_ssm_im, "w_in": w_in, "w_out": w_out, "ln_v_g": ln_v_g,
            "ln_v_b": ln_v_b, "w_s": w_s, "b_s": b_s, "ssm_a_re": ssm_a_re, "ssm_a_im": ssm_a_im,
            "ssm_log_dt": ssm_log_dt, "ssm_b_re": ssm_b_re, "ssm_b_im": ssm_b_im,
            "ssm_c_re": ssm_c_re, "ssm_c_im": ssm_c_im, "ssm_d": ssm_d, "w_glu": w_glu,
            "b_glu": b_glu, "ln1_g": ln1_g, "ln1_b": ln1_b, "ln2_g": ln2_g, "ln2_b": ln2_b,
            "w_router": w_router, "router_bias": router_bias, "w_gate": w_gate, "w_up": w_up,
            "w_down": w_down}

def reference(x_prompt, x_sample, state_ssm_re, state_ssm_im, w_in, w_out, ln_v_g, ln_v_b, w_s, b_s,
              ssm_a_re, ssm_a_im, ssm_log_dt, ssm_b_re, ssm_b_im, ssm_c_re, ssm_c_im, ssm_d,
              w_glu, b_glu, ln1_g, ln1_b, ln2_g, ln2_b, w_router, router_bias, w_gate, w_up, w_down):
    h0_zero = jnp.zeros((x_prompt.shape[0], G_B, N_STATE), jnp.float32)
    xp = x_prompt
    xsm = x_sample
    pr_re, pr_im, sm_re, sm_im, sm_v = [], [], [], [], []
    for l in range(DEPTH):
        p = dict(w_in=w_in[l], w_out=w_out[l], ln_v_g=ln_v_g[l], ln_v_b=ln_v_b[l], w_s=w_s[l],
                 b_s=b_s[l], ssm_a_re=ssm_a_re[l], ssm_a_im=ssm_a_im[l], ssm_log_dt=ssm_log_dt[l],
                 ssm_b_re=ssm_b_re[l], ssm_b_im=ssm_b_im[l], ssm_c_re=ssm_c_re[l],
                 ssm_c_im=ssm_c_im[l], ssm_d=ssm_d[l], w_glu=w_glu[l], b_glu=b_glu[l],
                 ln1_g=ln1_g[l], ln1_b=ln1_b[l], ln2_g=ln2_g[l], ln2_b=ln2_b[l],
                 w_router=w_router, router_bias=router_bias, w_gate=w_gate[l], w_up=w_up[l],
                 w_down=w_down[l])
        xp, hr, hi, _ = hybrid_layer(xp, h0_zero, h0_zero, **p)
        pr_re.append(hr)
        pr_im.append(hi)
        xsm, hr, hi, v_new = hybrid_layer(xsm, state_ssm_re[l], state_ssm_im[l], **p)
        sm_re.append(hr)
        sm_im.append(hi)
        sm_v.append(v_new)
    return (xp, xsm, jnp.stack(pr_re), jnp.stack(pr_im), jnp.stack(sm_re), jnp.stack(sm_im), jnp.stack(sm_v))


_drawn_inputs = setup_inputs


def setup_inputs(seed=0):
    import zlib

    import numpy as np

    out = dict(_drawn_inputs(seed))
    spreads = {}
    factors = {'ln_v_b': 2.859, 'ssm_a_re': 4.026, 'b_glu': 8.0, 'ln2_b': 2.912}
    for name, (base, spread) in spreads.items():
        noise = np.random.default_rng([zlib.crc32(name.encode()), seed]).standard_normal(out[name].shape)
        drawn = base * np.exp(spread * noise) if base else spread * noise
        out[name] = __import__('jax').numpy.asarray(drawn.astype(out[name].dtype))
    for name, factor in factors.items():
        out[name] = (out[name] * factor).astype(out[name].dtype)
    return out
```

```python
from contextlib import ExitStack, contextmanager

import concourse.bass as bass
from concourse import mybir

P = 128
F32 = mybir.dt.float32
I32 = mybir.dt.int32
U32 = mybir.dt.uint32
ACT = mybir.ActivationFunctionType
ALU = mybir.AluOpType
AX = mybir.AxisListType.X

D = 1024
KD = D // P
SEQ = 2048
NS = 8
WA = 512
FT = WA // P
HA = 4
G, Q, N = 32, 16, 64
PAIRS = G // 2
L = 16
HALF = L // 2
K = SEQ // L
SUP = 512
NSUP = SEQ // SUP
KS = SUP // L
CH = SEQ // P
E = 16
EG = 4
FF = 256
ALPHA = 2.0 ** 0.25
EPS = 1e-5
TWO_PI_HI, TWO_PI_MID, TWO_PI_LO = 6.28125, 0.0019350051879882812, 3.0199159819e-07
ROUND = 12582912.0
PI_IN = 3.1415925


class Place:

    END = 229344

    def __init__(self, nc, at):
        self.nc, self.at = nc, at

    def __call__(self, name, shape, dt=F32):
        size = 4
        for n in shape[1:]:
            size *= n
        assert self.at + size <= self.END, f"{name} ends at {self.at + size}"
        tensor = self.nc.alloc_sbuf_tensor_at(name, shape, dt, offset=self.at)
        self.at += -(-size // 32) * 32
        return tensor


class Chain:

    def __init__(self, engine, sem):
        self.engine, self.sem, self.n, self.base = engine, sem, 0, None

    def value(self):
        return self.n if self.base is None else self.base + self.n

    def __call__(self, instruction):
        instruction.then_inc(self.sem, 1)
        self.n += 1
        self.engine.wait_ge(self.sem, self.value())

    def mark(self, instruction):
        instruction.then_inc(self.sem, 1)
        self.n += 1

    def settle(self):
        self.engine.wait_ge(self.sem, self.value())

    def enter(self, i, per):
        self.before, self.per = self.n, per
        self.base, self.n = i * per + self.before, 0

    def leave(self, times):
        assert self.n == self.per, f"{self.n} steps an iteration, not {self.per}"
        self.base, self.n = None, self.before + times * self.per


def cmul(mul, add, sub, out_re, out_im, ar, ai, br, bi, t):
    return [(mul, t[0], ar, br), (mul, t[1], ai, bi), (mul, t[2], ar, bi), (mul, t[3], ai, br)], [
        (sub, out_re, t[0], t[1]), (add, out_im, t[2], t[3])]


def hybrid_step(nc, a, o):
    ctx = ExitStack()
    with ctx, nc.allow_non_contiguous_dma(reason="small parameters are laid out by state"):
        KB = 1024
        keep = Place(nc, 17408)

        def sb(name, shape, dt=F32, where=keep):
            return where(name, shape, dt)

        held = []

        def phase_sem(name):
            held.append(nc.alloc_semaphore(name))
            return held[-1]

        def sems(names):
            return [phase_sem(n) for n in names.split()]

        @contextmanager
        def phase():
            with ExitStack() as ph:
                yield ph
            nc.clear_and_free_semaphores(held)
            held.clear()
            nc.all_engine_barrier()

        def dram(name, shape, dt=F32):
            return nc.dram_tensor(name, shape, dt).ap()

        u_dram = dram("u_blocks", [WA, L, K])
        us_dram = dram("u_sample", [NS, WA])
        sq_dram = dram("sq_mats", [PAIRS, P, 2, 4 * P])
        k_dram = dram("k_lags", [(L + HALF - 1) * Q, WA])
        x1_dram = dram("x1_rows", [SEQ + NS, D])
        acc_dram = dram("acc_rows", [SEQ + NS + P, D])

        ident = sb("ident", [P, P])
        ya = sb("ya", [P, FT, SEQ])
        p_re, p_im = sb("p_re", [P, L + 1, PAIRS]), sb("p_im", [P, L + 1, PAIRS])
        unit = sb("unit", [P, 2, PAIRS])
        r16 = sb("r16", [P, PAIRS])
        cb_re, cb_im = sb("cb_re", [P, PAIRS, 2, Q]), sb("cb_im", [P, PAIRS, 2, Q])
        k_lag = sb("k_lag", [P, 2, WA])
        xts = sb("xts", [P, KD, NS])
        mixs = sb("mixs", [NS, 2, WA])
        mixs_t = sb("mixs_t", [P, KD, NS])
        us = sb("us", [NS, 2, WA])

        base = keep.at
        pa = Place(nc, base)
        w_xs = sb("w_xs", [P, KD, WA], where=pa)
        xt = sb("xt", [P, KD, SEQ], where=pa)
        pb = Place(nc, base + 80 * KB)
        w_u = sb("w_u", [P, KD, WA], where=pb)
        xin = sb("xin", [P, 4, D], where=pb)
        ust = sb("ust", [P, 4, L, KS], where=pb)
        v_re, v_im = sb("v_re", [P, 4, L, Q], where=pb), sb("v_im", [P, 4, L, Q], where=pb)
        q_mat = sb("q_mat", [P, 2, 2, L, Q], where=pb)
        s_mat = sb("s_mat", [P, 2, 4 * P], where=pb)
        lv_re, lv_im = sb("lv_re", [P, PAIRS, L], where=pb), sb("lv_im", [P, PAIRS, L], where=pb)
        bb_re, bb_im = sb("bb_re", [P, PAIRS, Q], where=pb), sb("bb_im", [P, PAIRS, Q], where=pb)
        braw = sb("braw", [P, 2, PAIRS, Q], where=pb)
        craw = s_mat[:, 0, :].rearrange("p (m t n) -> p m t n", m=2, t=2)
        xsin = q_mat[0:NS].rearrange("p a b d q -> p (a b d q)")
        c_re, c_ni = sb("c_re", [P, PAIRS, Q], where=pb), sb("c_ni", [P, PAIRS, Q], where=pb)
        prm = sb("prm", [P, 3, PAIRS], where=pb)
        tm = sb("tm", [P, 16, PAIRS], where=pb)
        whole = sb("whole", [P, PAIRS], I32, where=pb)
        tv = sb("tv", [P, 4, L * Q], where=pb)
        tq = sb("tq", [P, 4, L * Q], where=pb)
        d_row = sb("d_row", [P, G, Q], where=pb)

        with phase() as ph:
            tp = [ph.enter_context(nc.psum_tensor(f"tp{i}", [P, SUP], F32)) for i in range(2)]
            pxs = [ph.enter_context(nc.psum_tensor(f"pxs{i}", [P, SUP], F32)) for i in range(2)]
            pu = [ph.enter_context(nc.psum_tensor(f"pu{i}", [P, SUP], F32)) for i in range(2)]
            pst = ph.enter_context(nc.psum_tensor("pst", [P, 4 * P], F32))
            pkv = ph.enter_context(nc.psum_tensor("pkv", [P, 2, 2 * Q], F32))
            (id_zero, id_ready, w_xs_in, w_u_in, w_v_in, xs_in, prm_in, b_in, c_in, d_in,
             xt_act, xt_dve, xs_prod, u_prod, xs_out, u_out, c_turned, c_copied, st_prod,
             st_out, kv_prod, kv_out, v_ready, q_ready, par3, sin1, lam_ready, cq_ready, ust_ready,
             dch, ach, gch, xsT_prod, xsT_out, k_stored, d_masked, kz, us_prod, us_out) = sems("""id_zero id_ready w_xs_in w_u_in w_v_in
             xs_in prm_in b_in c_in d_in xt_act xt_dve xs_prod u_prod xs_out
             u_out c_turned c_copied st_prod st_out kv_prod kv_out v_ready q_ready par3 sin1 lam_ready
             cq_ready ust_ready dch ach gch xsT_prod xsT_out k_stored d_masked kz us_prod us_out""")
            load_x = [phase_sem(f"x_loaded{i}") for i in range(4)]
            turned = [phase_sem(f"tile_turned{i}") for i in range(4)]
            ust_stored = [phase_sem(f"ust_stored{i}") for i in range(4)]
            q_stored = [phase_sem(f"q_stored{i}") for i in range(2)]
            s_stored = [phase_sem(f"s_stored{i}") for i in range(2)]
            x_rows = a["x_prompt"][0]
            w_in = a["w_in"][0].rearrange("(k p) n -> p k n", p=P)
            block = ph.enter_context(nc.Block())

            @block.sync
            def _(sp):
                for c in range(4):
                    sp.dma_start(xin[:, c, :], x_rows[c * P:(c + 1) * P, :]).then_inc(load_x[c], 16)
                    if c == 0:
                        sp.dma_start(w_xs[:], w_in[:, :, 2 * WA:3 * WA]).then_inc(w_xs_in, 16)
                sp.dma_start(w_u[:], w_in[:, :, 0:WA]).then_inc(w_u_in, 16)

                def stores(s):
                    for f in range(FT):
                        sp.wait_ge(xs_out, s * FT + f + 1)
                        sp.dma_start(u_dram[f * P:(f + 1) * P, :, bass.ds(s * KS, KS)], ust[:, f]).then_inc(ust_stored[f], 16)
                    for f in range(4):
                        sp.wait_ge(st_out, s * 4 + f + 1)
                        sp.dma_start(sq_dram[s * 4 + f, :, 0, :], s_mat[:, f % 2, :]).then_inc(s_stored[f % 2], 16)

                with sp.Fori(0, NSUP - 1) as s:
                    for c in range(4):
                        sp.wait_ge(turned[c], s + 1)
                        sp.dma_start(xin[:, c, :], x_rows[bass.ds((s * 4 + 4 + c) * P, P), :]).then_inc(load_x[c], 16)
                    stores(s)
                stores(NSUP - 1)
                sp.wait_ge(us_prod, 1)
                sp.dma_start(w_xs[:], w_in[:, :, WA:2 * WA]).then_inc(w_v_in, 16)
                sp.wait_ge(us_out, 2)
                sp.dma_start(us_dram, us[:, 1, :]).then_inc(k_stored, 16)
                sp.wait_ge(kz, 1)
                for h in range(2):
                    sp.dma_start(k_dram[h * P:(h + 1) * P, :], k_lag[:, h, :]).then_inc(k_stored, 16)
                sp.dma_start(k_dram[2 * P:, :], tv[0:(HALF - 1) * Q].rearrange("p a b -> p (a b)")[:, 0:WA]).then_inc(k_stored, 16)
                sp.wait_ge(k_stored, 64)
                sp.wait_ge(w_v_in, 16)
                for f in range(FT):
                    sp.wait_ge(ust_stored[f], NSUP * 16)
                for b in range(2):
                    sp.wait_ge(s_stored[b], PAIRS // 2 * 16)
                    sp.wait_ge(q_stored[b], PAIRS // 2 * 16)

            @block.gpsimd
            def _(gp):
                gp.memset(ident[:], 0.0).then_inc(id_zero, 1)
                gp.wait_ge(id_zero, 1)
                gp.affine_select(out=ident[:], in_=ident[:], compare_op=ALU.not_equal, fill=1.0, base=0,
                                 pattern=[[-1, P]], channel_multiplier=1).then_inc(id_ready, 1)
                gp.dma_start(braw[:, 0], bass.AP(tensor=a["ssm_b_re"].tensor, offset=0,
                             ap=[[Q, P], [2 * N * Q, PAIRS], [1, Q]])).then_inc(b_in, 16)
                gp.dma_start(braw[:, 1], bass.AP(tensor=a["ssm_b_im"].tensor, offset=0,
                             ap=[[Q, P], [2 * N * Q, PAIRS], [1, Q]])).then_inc(b_in, 16)
                gp.dma_start(d_row[:], bass.AP(tensor=a["ssm_d"].tensor, offset=0,
                             ap=[[0, P], [Q, G], [1, Q]])).then_inc(d_in, 16)
                gp.wait_ge(d_in, 16)
                gp.affine_select(out=d_row[:], in_=d_row[:], compare_op=ALU.is_equal, fill=0.0, base=Q - P,
                                 pattern=[[0, G], [-1, Q]], channel_multiplier=1).then_inc(d_masked, 1)
                ch = Chain(gp, gch)
                gp.wait_ge(lam_ready, 1)
                gp.wait_ge(cq_ready, 1)
                lag_re = p_re[:, 1:L + 1, :].rearrange("p d c -> p c d")
                lag_im = p_im[:, 1:L + 1, :].rearrange("p d c -> p c d")

                def q_pair(pair, b):
                    sh = [P, L, Q]
                    lr = lag_re[:, pair, :].unsqueeze(2).broadcast_to(sh)
                    li = lag_im[:, pair, :].unsqueeze(2).broadcast_to(sh)
                    cr = c_re[:, pair, :].unsqueeze(1).broadcast_to(sh)
                    cn = c_ni[:, pair, :].unsqueeze(1).broadcast_to(sh)
                    t = [tq[:, k, :].rearrange("p (d q) -> p d q", q=Q) for k in range(4)]
                    for k, (x, y) in enumerate([(cr, lr), (cn, li), (cn, lr), (cr, li)]):
                        ch.mark(gp.tensor_tensor(t[k], x, y, ALU.mult))
                    ch.settle()
                    gp.tensor_tensor(q_mat[:, b, 0], t[0], t[1], ALU.add).then_inc(q_ready, 1)
                    gp.tensor_tensor(q_mat[:, b, 1], t[2], t[3], ALU.subtract).then_inc(q_ready, 1)

                gp.wait_ge(xsT_prod, 1)
                for b in range(2):
                    q_pair(b, b)
                    gp.wait_ge(q_ready, 2 * (b + 1))
                    gp.dma_start(sq_dram[b, :, 1, :], q_mat[:, b].rearrange("p a d q -> p (a d q)")).then_inc(q_stored[b], 16)
                with gp.Fori(0, PAIRS // 2 - 1) as i:
                    ch.enter(i, 8)
                    for b in range(2):
                        gp.wait_ge(q_stored[b], i * 16 + 16)
                        q_pair(i * 2 + 2 + b, b)
                        gp.wait_ge(q_ready, i * 4 + 4 + 2 * (b + 1))
                        gp.dma_start(sq_dram[i * 2 + 2 + b, :, 1, :], q_mat[:, b].rearrange("p a d q -> p (a d q)")).then_inc(q_stored[b], 16)
                    ch.leave(PAIRS // 2 - 1)

            @block.scalar
            def _(act):
                act.dma_start(prm[:, 0, :], bass.AP(tensor=a["ssm_a_re"].tensor, offset=0,
                              ap=[[1, P], [P, PAIRS]])).then_inc(prm_in, 16)
                act.dma_start(prm[:, 1, :], bass.AP(tensor=a["ssm_a_im"].tensor, offset=0,
                              ap=[[1, P], [P, PAIRS]])).then_inc(prm_in, 16)
                for h in range(2):
                    act.dma_start(prm[h * N:(h + 1) * N, 2, :], bass.AP(tensor=a["ssm_log_dt"].tensor, offset=h,
                                  ap=[[0, N], [2, PAIRS]])).then_inc(prm_in, 16)
                for m, name in enumerate(("ssm_c_re", "ssm_c_im")):
                    for t in range(2):
                        for h in range(2):
                            act.dma_start(craw[:, m, t, h * N:(h + 1) * N],
                                          bass.AP(tensor=a[name].tensor, offset=(t * 16 + h) * Q * N,
                                                  ap=[[2 * Q * N, 8], [N, Q], [1, N]])).then_inc(c_in, 16)
                act.dma_start(xsin[:], a["x_sample"][:, 0, :]).then_inc(xs_in, 16)
                act.wait_ge(par3, 2)
                nc.scalar.activation(unit[:, 1, :], tm[:, 6, :], ACT.Sin).then_inc(sin1, 1)
                nc.scalar.activation(unit[:, 0, :], tm[:, 7, :], ACT.Sin).then_inc(sin1, 1)
                act.wait_ge(c_turned, 1)
                pc = pst[:, :].rearrange("p (m c) -> p m c", m=2)
                nc.scalar.copy(c_re[:].rearrange("p a b -> p (a b)"), pc[:, 0, :]).then_inc(c_copied, 1)
                nc.scalar.mul(c_ni[:].rearrange("p a b -> p (a b)"), pc[:, 1, :], -1.0).then_inc(c_copied, 1)
                act.wait_ge(xsT_prod, 1)
                nc.scalar.copy(xts[:], tp[0][:, 0:KD * NS].rearrange("p (k n) -> p k n", n=NS)).then_inc(xsT_out, 1)
                with act.Fori(0, NSUP) as s:
                    for c in range(4):
                        act.wait_ge(turned[c], s + 1)
                        nc.scalar.copy(xt[:, 0:4, bass.ds(s * SUP + c * P, P)],
                                       tp[0][:, :].rearrange("p (k n) -> p k n", k=4)).then_inc(xt_act, 1)
                    for f in range(FT):
                        act.wait_ge(u_prod, s * FT + f + 1)
                        nc.scalar.activation(ya[:, f, bass.ds(s * SUP, SUP)], pu[f % 2][:, :],
                                             ACT.Gelu_apprx_tanh).then_inc(u_out, 1)
                act.wait_ge(us_prod, 2)
                nc.scalar.activation(us[:, 0, :], pu[0][0:NS, :], ACT.Gelu_apprx_tanh).then_inc(us_out, 1)

            @block.vector
            def _(dve):
                v = nc.vector
                ch = Chain(dve, dch)
                T = [tm[:, k, :] for k in range(16)]
                are, aim, dt, ad, ang = prm[:, 0, :], prm[:, 1, :], T[0], T[1], T[5]
                ch(v.memset(cb_re[:], 0.0))
                ch(v.memset(cb_im[:], 0.0))

                def exp(out, x, k, r, whole):
                    ch(v.tensor_scalar(k, x, 1.4426950408889634, ROUND, ALU.mult, ALU.add))
                    ch(v.tensor_scalar(k, k, -ROUND, None, ALU.add))
                    ch(v.tensor_scalar(k, k, -126.0, 127.0, ALU.max, ALU.min))
                    ch(v.scalar_tensor_tensor(r, k, -0.693359375, x, ALU.mult, ALU.add))
                    ch(v.scalar_tensor_tensor(r, k, 2.12194440e-4, r, ALU.mult, ALU.add))
                    ch(v.tensor_scalar(out, r, 1.0 / 5040, None, ALU.mult))
                    for c in (720, 120, 24, 6, 2, 1):
                        ch(v.scalar_tensor_tensor(out, out, 1.0 / c, r, ALU.add, ALU.mult))
                    ch(v.tensor_scalar(k, k, 127.0, None, ALU.add))
                    ch(v.tensor_copy(whole, k))
                    ch(v.tensor_scalar(whole, whole, 23, None, ALU.logical_shift_left))
                    ch(v.scalar_tensor_tensor(out, out, 1.0, whole.bitcast(F32), ALU.add, ALU.mult))

                dve.wait_ge(prm_in, 64)
                exp(dt, prm[:, 2, :], T[8], T[9], whole[:])
                ch(v.tensor_tensor(ad, are, dt, ALU.mult))
                ch(v.tensor_tensor(ang, aim, dt, ALU.mult))
                exp(T[4], ad, T[8], T[9], whole[:])
                ch(v.tensor_tensor(r16[:], T[4], T[4], ALU.mult))
                for _ in range(3):
                    ch(v.tensor_tensor(r16[:], r16[:], r16[:], ALU.mult))
                ch(v.tensor_scalar(T[8], ang, 1.0 / 6.283185307179586, ROUND, ALU.mult, ALU.add))
                ch(v.tensor_scalar(T[8], T[8], -ROUND, None, ALU.add))
                for part in (TWO_PI_HI, TWO_PI_MID, TWO_PI_LO):
                    ch(v.scalar_tensor_tensor(ang, T[8], -part, ang, ALU.mult, ALU.add))
                v.tensor_scalar(T[6], ang, PI_IN, -PI_IN, ALU.min, ALU.max).then_inc(par3, 1)
                dve.wait_ge(par3, 1)
                ch(v.tensor_scalar(T[9], T[6], -1.0, None, ALU.mult))
                ch(v.tensor_tensor(T[9], T[9], T[6], ALU.max))
                v.tensor_scalar(T[7], T[9], -1.0, 1.5707963267948966, ALU.mult, ALU.add).then_inc(par3, 1)
                dve.wait_ge(sin1, 2)
                for part, pw in ((0, p_re), (1, p_im)):
                    ch.mark(v.tensor_tensor(pw[:, 1, :], T[4], unit[:, part, :], ALU.mult))
                ch.mark(v.memset(p_re[:, 0, :], 1.0))
                ch.mark(v.memset(p_im[:, 0, :], 0.0))
                ch.settle()
                have = 1
                while have < L:
                    sh = [P, have, PAIRS]
                    br, bi = (x[:, have, :].unsqueeze(1).broadcast_to(sh) for x in (p_re, p_im))
                    ar, ai = p_re[:, 1:have + 1, :], p_im[:, 1:have + 1, :]
                    t = [tv[:, k, 0:have * PAIRS].rearrange("p (a b) -> p a b", b=PAIRS) for k in range(4)]
                    for k, (x, y) in enumerate([(ar, br), (ai, bi), (ar, bi), (ai, br)]):
                        ch.mark(v.tensor_tensor(t[k], x, y, ALU.mult))
                    ch.settle()
                    ch.mark(v.tensor_tensor(p_re[:, have + 1:2 * have + 1, :], t[0], t[1], ALU.subtract))
                    ch.mark(v.tensor_tensor(p_im[:, have + 1:2 * have + 1, :], t[2], t[3], ALU.add))
                    ch.settle()
                    have *= 2
                for r in range(L):
                    ch.mark(v.tensor_copy(lv_re[:, :, r], p_re[:, L - 1 - r, :]))
                    ch.mark(v.tensor_copy(lv_im[:, :, r], p_im[:, L - 1 - r, :]))
                ch(v.tensor_tensor(T[10], are, are, ALU.mult))
                ch(v.tensor_tensor(T[11], aim, aim, ALU.mult))
                ch(v.tensor_tensor(T[10], T[10], T[11], ALU.add))
                ch(v.reciprocal(T[10], T[10]))
                ch(v.tensor_scalar(T[11], p_re[:, 1, :], -1.0, None, ALU.add))
                nr, ni = T[11], p_im[:, 1, :]
                for k, (x, y) in enumerate([(nr, are), (ni, aim), (ni, are), (nr, aim)]):
                    ch.mark(v.tensor_tensor(T[12 + k], x, y, ALU.mult))
                ch.settle()
                ch(v.tensor_tensor(T[12], T[12], T[13], ALU.add))
                ch(v.tensor_tensor(T[14], T[14], T[15], ALU.subtract))
                ch(v.tensor_tensor(T[12], T[12], T[10], ALU.mult))
                ch(v.tensor_tensor(T[14], T[14], T[10], ALU.mult))
                dve.wait_ge(b_in, 32)
                sh = [P, PAIRS, Q]
                zr, zi = (x.unsqueeze(2).broadcast_to(sh) for x in (T[12], T[14]))
                t = [tv[:, k, :].rearrange("p (a b) -> p a b", b=Q) for k in range(4)]
                for k, (x, y) in enumerate([(zr, braw[:, 0]), (zi, braw[:, 1]), (zr, braw[:, 1]), (zi, braw[:, 0])]):
                    ch.mark(v.tensor_tensor(t[k], x, y, ALU.mult))
                ch.settle()
                ch.mark(v.tensor_tensor(bb_re[:], t[0], t[1], ALU.subtract))
                ch.mark(v.tensor_tensor(bb_im[:], t[2], t[3], ALU.add))
                ch.settle()
                v.memset(tm[:, 2, :], 0.0).then_inc(lam_ready, 1)
                dve.wait_ge(c_copied, 2)
                for src, dst in ((c_re, cb_re), (c_ni, cb_im)):
                    for h in range(2):
                        ch.mark(v.tensor_copy(dst[h * N:(h + 1) * N, :, h, :], src[h * N:(h + 1) * N, :, :]))
                ch.settle()
                v.memset(tm[:, 2, :], 0.0).then_inc(cq_ready, 1)

                def v_pair(pair, b):
                    sh = [P, L, Q]
                    lr, li = (x[:, pair, :].unsqueeze(2).broadcast_to(sh) for x in (lv_re, lv_im))
                    br, bi = (x[:, pair, :].unsqueeze(1).broadcast_to(sh) for x in (bb_re, bb_im))
                    t = [tv[:, k, :].rearrange("p (d q) -> p d q", q=Q) for k in range(4)]
                    for k, (x, y) in enumerate([(lr, br), (li, bi), (lr, bi), (li, br)]):
                        ch.mark(v.tensor_tensor(t[k], x, y, ALU.mult))
                    ch.settle()
                    v.tensor_tensor(v_re[:, b], t[0], t[1], ALU.subtract).then_inc(v_ready, 1)
                    v.tensor_tensor(v_im[:, b], t[2], t[3], ALU.add).then_inc(v_ready, 1)

                def super_tile(s, first):
                    for c in range(4):
                        dve.wait_ge(turned[c], s + 1)
                        v.tensor_copy(xt[:, 4:8, bass.ds(s * SUP + c * P, P)],
                                      tp[1][:, :].rearrange("p (k n) -> p k n", k=4)).then_inc(xt_dve, 1)
                    for f in range(FT):
                        dve.wait_ge(xs_prod, s * FT + f + 1)
                        if not first:
                            dve.wait_ge(ust_stored[f], s * 16)
                        v.tensor_copy(ust[:, f].rearrange("p j k -> p k j"),
                                      pxs[f % 2][:, :].rearrange("p (k j) -> p k j", j=L)).then_inc(xs_out, 1)
                        if not first or f:
                            dve.wait_ge(v_ready, s * 8 + 2 * f)
                        v_pair(s * 4 + f, f)
                    for f in range(4):
                        b = f % 2
                        dve.wait_ge(st_prod, s * 4 + f + 1)
                        if not first or f > 1:
                            dve.wait_ge(s_stored[b], (s * 2 + f // 2) * 16)
                        v.tensor_copy(s_mat[:, b, :], pst[:, :]).then_inc(st_out, 1)
                        dve.wait_ge(kv_prod, s * 4 + f + 1)
                        v.tensor_copy(k_lag[:, :, bass.ds((s * 4 + f) * 2 * Q, 2 * Q)], pkv[:, :, :]).then_inc(kv_out, 1)

                super_tile(0, True)
                with dve.Fori(1, NSUP) as s:
                    ch.enter(s - 1, 16)
                    super_tile(s, False)
                    ch.leave(NSUP - 1)
                dve.wait_ge(us_prod, 1)
                v.tensor_copy(us[:, 1, :], pxs[0][0:NS, :]).then_inc(us_out, 1)
                dve.wait_ge(d_masked, 1)
                dve.wait_ge(kv_out, PAIRS)
                ch(v.tensor_tensor(k_lag[96:P, 1, :], k_lag[96:P, 1, :],
                                   d_row[96:P].rearrange("p g q -> p (g q)"), ALU.add))
                ch(v.memset(tv[:], 0.0))
                v.memset(tm[:, 2, :], 0.0).then_inc(kz, 1)

            @block.tensor
            def _(pe):
                t = nc.tensor
                pe.wait_ge(id_ready, 1)
                pe.wait_ge(c_in, 128)
                for m in range(2):
                    for h in range(2):
                        mm = t.transpose(pst[:, (2 * m + h) * P:(2 * m + h + 1) * P], craw[:, m, h, :], ident[:])
                mm.then_inc(c_turned, 1)
                pe.wait_ge(xs_in, 16)
                for k in range(KD):
                    mm = t.transpose(tp[0][:, k * NS:(k + 1) * NS], xsin[:, k * P:(k + 1) * P], ident[0:NS, 0:NS])
                mm.then_inc(xsT_prod, 1)
                pe.wait_ge(xsT_out, 1)
                pe.wait_ge(c_copied, 2)

                def super_tile(s, first):
                    for c in range(4):
                        pe.wait_ge(load_x[c], s * 16 + 16)
                        for h in range(2):
                            if not first or c:
                                pe.wait_ge((xt_act, xt_dve)[h], s * 4 + c)
                            for k in range(4):
                                kk = 4 * h + k
                                mm = t.transpose(tp[h][:, k * P:(k + 1) * P], xin[:, c, kk * P:(kk + 1) * P], ident[:])
                        mm.then_inc(turned[c], 1)
                    pe.wait_ge(xt_act, s * 4 + 4)
                    pe.wait_ge(xt_dve, s * 4 + 4)
                    if first:
                        pe.wait_ge(w_xs_in, 16)
                    for f in range(FT):
                        for w, banks, prod, out in ((w_xs, pxs, xs_prod, xs_out), (w_u, pu, u_prod, u_out)):
                            if first and f == 0 and w is w_u:
                                pe.wait_ge(w_u_in, 16)
                            if not first or f > 1:
                                pe.wait_ge(out, s * FT + f - 1)
                            for k in range(KD):
                                mm = t.matmul(banks[f % 2][:, :], w[:, k, f * P:(f + 1) * P],
                                              xt[:, k, bass.ds(s * SUP, SUP)], start=(k == 0), stop=(k == KD - 1))
                            mm.then_inc(prod, 1)
                    for f in range(4):
                        pair = s * 4 + f
                        pe.wait_ge(v_ready, s * 8 + 2 * f + 2)
                        if not first or f:
                            pe.wait_ge(st_out, s * 4 + f)
                        for h in range(2):
                            for m, vm in enumerate((v_re, v_im)):
                                win = vm[:, f].rearrange("p d q -> p (d q)")[:, h * P:(h + 1) * P]
                                mm = t.transpose(pst[:, (2 * h + m) * P:(2 * h + m + 1) * P], win, ident[:])
                        mm.then_inc(st_prod, 1)
                        if first and f == 0:
                            pe.wait_ge(cq_ready, 1)
                        if not first or f:
                            pe.wait_ge(kv_out, s * 4 + f)
                        for h in range(2):
                            for m, (vm, cm) in enumerate(((v_re, cb_re), (v_im, cb_im))):
                                win = vm[:, f].rearrange("p d q -> p (d q)")[:, h * P:(h + 1) * P]
                                mm = t.matmul(pkv[:, h, :], win, cm[:, pair].rearrange("p h q -> p (h q)"),
                                              start=(m == 0), stop=(m == 1))
                        mm.then_inc(kv_prod, 1)

                super_tile(0, True)
                with pe.Fori(1, NSUP) as s:
                    super_tile(s, False)
                for w, banks, out in ((w_xs, pxs, xs_out), (w_u, pu, u_out)):
                    pe.wait_ge(out, NSUP * FT)
                    for k in range(KD):
                        mm = t.matmul(banks[0][0:NS, :], xts[:, k, :], w[:, k, :], start=(k == 0), stop=(k == KD - 1))
                    mm.then_inc(us_prod, 1)

        pc = Place(nc, base + 80 * KB)
        cos_k, sin_k = sb("cos_k", [P, PAIRS, K], where=pc), sb("sin_k", [P, PAIRS, K], where=pc)
        us1 = sb("us1", [P, G, NS], where=Place(nc, Place.END - G * NS * 4))
        toep = sb("toep", [P, L, WA], where=pc)
        with phase() as ph:
            pt = Place(nc, base + 128 * KB)
            wst = sb("wst", [P, HA, P], where=pt)
            bs_row = sb("bs_row", [P, HA, P], where=pt)
            gate_b = sb("gate_b", [P, HA, P], where=pt)
            ones = sb("ones", [P, P], where=pt)
            g_col, b_col = sb("g_col", [P, HA], where=pt), sb("b_col", [P, HA], where=pt)
            vg = sb("vg", [P, 4, WA], where=pt)
            vn = sb("vn", [P, 4, WA], where=pt)
            wsr = vg[:, 3, :].rearrange("p (h m) -> p h m", h=HA)
            gt = k_lag
            st = sb("st", [P, 4, 6], where=pt)
            spare = sb("spare_b", [P, 1], where=pt)
            ag = sb("ag", [P, 4, 2], where=pt)
            rs = sb("rs", [P, 4, 2], where=pt)
            half_n = sb("half_n", [P, 1], where=pt)
            w16 = sb("w16", [P, 2, 2, PAIRS], where=pt)
            tw = sb("tw", [P, 4, PAIRS], where=pt)
            tb = toep[:, 0:2 * 4].rearrange("p a b -> p (a b)").rearrange("p (t c k) -> p t c k", t=4, c=PAIRS)
            gs_row, bs8 = mixs[:, 1, :], sb("bs8", [NS, WA], where=pt)
            w00 = sb("w00", [NS, 2, HA], where=pt)
            pv = [ph.enter_context(nc.psum_tensor(f"pv{i}", [P, WA], F32)) for i in range(2)]
            pg = [ph.enter_context(nc.psum_tensor(f"pg{i}", [P, HA, P], F32)) for i in range(2)]
            pw = ph.enter_context(nc.psum_tensor("pw", [P, HA, P], F32))
            pr = ph.enter_context(nc.psum_tensor("pr", [P, HA, P], F32))
            psv = ph.enter_context(nc.psum_tensor("psv", [NS, WA], F32))
            pmt = ph.enter_context(nc.psum_tensor("pmt", [P, 4 * NS], F32))
            (ws_in, row_in, col_in, smp_in, ones_set, w_turned, w_copied, w_masked, rowsum, gate_b_set, v_prod, v_gelu,
             var_set, rstd_set, v_norm, gate_prod, gated, toep_in, bdch, vs_prod, vs_gelu, vs_var, vs_rstd, vs_set,
             mixa_set, vs_stored, tables_set, us_zero, us_in) = sems("""ws_in row_in col_in smp_in ones_set w_turned w_copied w_masked rowsum
             gate_b_set v_prod v_gelu var_set rstd_set v_norm gate_prod gated toep_in bdch vs_prod vs_gelu vs_var
             vs_rstd vs_set mixa_set vs_stored tables_set us_zero us_in""")
            LAG = 3
            block = ph.enter_context(nc.Block())

            @block.sync
            def _(sp):
                sp.dma_start(wsr, a["w_s"][0].rearrange("h l m -> l h m")).then_inc(ws_in, 16)
                sp.dma_start(bs_row[:], bass.AP(tensor=a["b_s"].tensor, offset=0,
                             ap=[[0, P], [P, HA], [1, P]])).then_inc(row_in, 16)
                sp.dma_start(gs_row, bass.AP(tensor=a["ln_v_g"].tensor, offset=0, ap=[[0, NS], [1, WA]])).then_inc(smp_in, 16)
                sp.dma_start(bs8[:], bass.AP(tensor=a["ln_v_b"].tensor, offset=0, ap=[[0, NS], [1, WA]])).then_inc(smp_in, 16)
                sp.dma_start(w00[:, 0, :], bass.AP(tensor=a["w_s"].tensor, offset=0, ap=[[0, NS], [P * P, HA]])).then_inc(smp_in, 16)
                sp.dma_start(w00[:, 1, :], bass.AP(tensor=a["b_s"].tensor, offset=0, ap=[[0, NS], [P, HA]])).then_inc(smp_in, 16)
                sp.wait_ge(tables_set, 1)
                for j in range(L):
                    sp.dma_start(toep[:, j, :], k_dram[(L - 1 - j) * Q:(L - 1 - j) * Q + P, :]).then_inc(toep_in, 16)
                sp.wait_ge(vs_set, 1)
                sp.dma_start(o["v_sample"][0, :, 0, :], gt[0:NS, 0, :]).then_inc(vs_stored, 16)
                sp.wait_ge(vs_stored, 16)
                sp.wait_ge(toep_in, L * 16)

            @block.gpsimd
            def _(gp):
                gp.dma_start(g_col[:], bass.AP(tensor=a["ln_v_g"].tensor, offset=0, ap=[[1, P], [P, HA]])).then_inc(col_in, 16)
                gp.dma_start(b_col[:], bass.AP(tensor=a["ln_v_b"].tensor, offset=0, ap=[[1, P], [P, HA]])).then_inc(col_in, 16)
                gp.memset(us1[:], 0.0).then_inc(us_zero, 1)
                gp.wait_ge(us_zero, 1)
                for n in range(NS):
                    gp.dma_start(us1[P - Q:P, :, n], us_dram[n].rearrange("(g q) -> q g", q=Q)).then_inc(us_in, 16)
                gp.memset(ones[:], 1.0).then_inc(ones_set, 1)
                gp.memset(half_n[:], -0.5).then_inc(ones_set, 1)
                gp.wait_ge(w_copied, 1)
                gp.affine_select(out=wst[:], in_=wst[:], compare_op=ALU.is_ge, fill=0.0, base=0,
                                 pattern=[[0, HA], [1, P]], channel_multiplier=-1).then_inc(w_masked, 1)
                gp.wait_ge(ones_set, 2)
                with gp.Fori(0, CH // 4) as i:
                    for b in range(4):
                        gp.wait_ge(var_set, i * 4 + b + 1)
                        gp.tensor_tensor(rs[:, b, 1:2], rs[:, b, 0:1], half_n[:], ALU.pow).then_inc(rstd_set, 1)
                gp.wait_ge(vs_var, 1)
                gp.tensor_tensor(rs[0:NS, 0, 1:2], rs[0:NS, 0, 0:1], half_n[0:NS], ALU.pow).then_inc(vs_rstd, 1)
                gp.wait_ge(us_in, NS * 16)

            @block.scalar
            def _(act):
                act.wait_ge(w_turned, 1)
                nc.scalar.copy(wst[:], pw[:, :, :]).then_inc(w_copied, 1)

                def gelus(i, first):
                    for b in range(4):
                        act.wait_ge(v_prod, i * 4 + b + 1)
                        if not first:
                            act.wait_ge(v_norm, i * 4 + b - 3)
                        nc.scalar.activation(vg[:, b, :], pv[b % 2][:, :], ACT.Gelu_apprx_tanh).then_inc(v_gelu, 1)

                gelus(0, True)
                with act.Fori(1, CH // 4) as i:
                    gelus(i, False)
                act.wait_ge(vs_prod, 1)
                act.wait_ge(v_norm, CH)
                nc.scalar.activation(vg[0:NS, 0, :], psv[:, :], ACT.Gelu_apprx_tanh).then_inc(vs_gelu, 1)

            @block.vector
            def _(dve):
                v = nc.vector
                ch = Chain(dve, bdch)
                src, cur = (unit[:, 0, :], unit[:, 1, :]), 0

                def square(xr, xi, yr, yi):
                    ch.mark(v.tensor_tensor(tw[:, 0], xr, xr, ALU.mult))
                    ch.mark(v.tensor_tensor(tw[:, 1], xi, xi, ALU.mult))
                    ch.mark(v.tensor_tensor(tw[:, 2], xr, xi, ALU.mult))
                    ch.settle()
                    ch.mark(v.tensor_tensor(yr, tw[:, 0], tw[:, 1], ALU.subtract))
                    ch.mark(v.tensor_scalar(yi, tw[:, 2], 2.0, None, ALU.mult))
                    ch.settle()
                    unit_length(yr, yi)

                def unit_length(yr, yi):
                    ch.mark(v.tensor_tensor(tw[:, 0], yr, yr, ALU.mult))
                    ch.mark(v.tensor_tensor(tw[:, 1], yi, yi, ALU.mult))
                    ch.settle()
                    ch(v.tensor_tensor(tw[:, 0], tw[:, 0], tw[:, 1], ALU.add))
                    ch(v.tensor_scalar(tw[:, 0], tw[:, 0], -0.5, 1.5, ALU.mult, ALU.add))
                    ch.mark(v.tensor_tensor(yr, yr, tw[:, 0], ALU.mult))
                    ch.mark(v.tensor_tensor(yi, yi, tw[:, 0], ALU.mult))
                    ch.settle()

                for _ in range(4):
                    dst = (w16[:, cur, 0, :], w16[:, cur, 1, :])
                    square(*src, *dst)
                    src, cur = dst, 1 - cur
                ch.mark(v.memset(cos_k[:, :, 0:1], 1.0))
                ch.mark(v.memset(sin_k[:, :, 0:1], 0.0))
                ch.settle()
                have = 1
                while have < K:
                    sh = [P, PAIRS, have]
                    br, bi = (x.unsqueeze(2).broadcast_to(sh) for x in src)
                    t = [tb[:, k, :, 0:have] for k in range(4)]
                    ar, ai = cos_k[:, :, 0:have], sin_k[:, :, 0:have]
                    for k, (x, y) in enumerate([(ar, br), (ai, bi), (ar, bi), (ai, br)]):
                        ch.mark(v.tensor_tensor(t[k], x, y, ALU.mult))
                    ch.settle()
                    ch.mark(v.tensor_tensor(cos_k[:, :, have:2 * have], t[0], t[1], ALU.subtract))
                    ch.mark(v.tensor_tensor(sin_k[:, :, have:2 * have], t[2], t[3], ALU.add))
                    ch.settle()
                    have *= 2
                    if have < K:
                        dst = (w16[:, cur, 0, :], w16[:, cur, 1, :])
                        square(*src, *dst)
                        src, cur = dst, 1 - cur
                v.memset(tw[:, 3], 0.0).then_inc(tables_set, 1)
                dve.wait_ge(rowsum, 1)
                dve.wait_ge(row_in, 16)
                dve.wait_ge(col_in, 32)
                for h in range(HA):
                    v.scalar_tensor_tensor(gate_b[:, h, :], pr[:, h, :], b_col[:, h:h + 1], bs_row[:, h, :],
                                           ALU.mult, ALU.add).then_inc(gate_b_set, 1)
                dve.wait_ge(gate_b_set, HA)

                def normalise(src, n, b, var, rstd, ready, out):
                    ch.mark(v.bn_stats(st[0:n, b, :], src))
                    ch.settle()
                    v.memset(spare[:], 0.0)
                    ch(v.bn_aggr(ag[0:n, b, :], st[0:n, b, :]))
                    v.tensor_scalar(rs[0:n, b, 0:1], ag[0:n, b, 1:2], EPS, None, ALU.add).then_inc(var, 1)
                    dve.wait_ge(rstd, ready)
                    return v.tensor_scalar(out, src, ag[0:n, b, 0:1], rs[0:n, b, 1:2], ALU.subtract, ALU.mult)

                def norm_tile(c, b, first=False):
                    dve.wait_ge(v_gelu, c + 1)
                    if not first:
                        dve.wait_ge(gate_prod, c - 3)
                    normalise(vg[:, b, :], P, b, var_set, rstd_set, c + 1, vn[:, b, :]).then_inc(v_norm, 1)

                def gate_tile(c, b):
                    dve.wait_ge(gate_prod, c + 1)
                    for h in range(HA):
                        ch.mark(v.scalar_tensor_tensor(gt[:, b % 2, h * P:(h + 1) * P], pg[b % 2][:, h, :], g_col[:, h:h + 1],
                                                       gate_b[:, h, :], ALU.mult, ALU.add))
                    ch.settle()
                    part = ya[:, :, bass.ds(c * P, P)]
                    v.tensor_tensor(part, gt[:, b % 2, :].rearrange("p (h l) -> p h l", h=HA), part, ALU.mult).then_inc(gated, 1)

                for c in range(4):
                    norm_tile(c, c, True)
                with dve.Fori(0, CH // 4 - 1) as i:
                    ch.enter(i, 4 * 6)
                    for b in range(4):
                        gate_tile(i * 4 + b, b)
                        norm_tile(i * 4 + 4 + b, b)
                    ch.leave(CH // 4 - 1)
                for c in range(CH - 4, CH):
                    gate_tile(c, c % 4)
                dve.wait_ge(vs_gelu, 1)
                dve.wait_ge(smp_in, 64)
                dve.wait_ge(gated, CH)
                ch(normalise(vg[0:NS, 0, :], NS, 0, vs_var, vs_rstd, 1, vn[0:NS, 0, :]))
                ch(v.tensor_tensor(vn[0:NS, 0, :], vn[0:NS, 0, :], gs_row, ALU.mult))
                v.tensor_tensor(gt[0:NS, 0, :], vn[0:NS, 0, :], bs8[:], ALU.add).then_inc(vs_set, 1)
                dve.wait_ge(vs_set, 1)
                for h in range(HA):
                    ch.mark(v.tensor_scalar(gt[0:NS, 1, h * P:(h + 1) * P], gt[0:NS, 0, h * P:(h + 1) * P],
                                            w00[:, 0, h:h + 1], w00[:, 1, h:h + 1], ALU.mult, ALU.add))
                ch.settle()
                v.tensor_tensor(mixs[:, 0, :], gt[0:NS, 1, :], us[:, 0, :], ALU.mult).then_inc(mixa_set, 1)
                dve.wait_ge(w_turned, 2)
                v.tensor_copy(mixs_t[:, 0:FT, :], pmt[:, :].rearrange("p (f s) -> p f s", s=NS)).then_inc(mixa_set, 1)

            @block.tensor
            def _(pe):
                t = nc.tensor
                pe.wait_ge(ws_in, 16)
                for h in range(HA):
                    mm = t.transpose(pw[:, h, :], wsr[:, h, :], ident[:])
                mm.then_inc(w_turned, 1)

                def gate(c):
                    pe.wait_ge(v_norm, c + 1)
                    if c >= 2:
                        pe.wait_ge(gated, c - 1)
                    for h in range(HA):
                        mm = t.matmul(pg[c % 2][:, h, :], vn[:, c % 4, h * P:(h + 1) * P], wst[:, h, :], start=True, stop=True)
                    mm.then_inc(gate_prod, 1)

                for c in range(CH + LAG):
                    if c < CH:
                        if c >= 2:
                            pe.wait_ge(v_gelu, c - 1)
                        for k in range(KD):
                            mm = t.matmul(pv[c % 2][:, :], xt[:, k, c * P:(c + 1) * P], w_xs[:, k, :],
                                          start=(k == 0), stop=(k == KD - 1))
                        mm.then_inc(v_prod, 1)
                    if c == 0:
                        pe.wait_ge(w_masked, 1)
                        pe.wait_ge(ones_set, 2)
                        t.matmul(pr[:, :, :].rearrange("p h l -> p (h l)"), ones[:], wst[:].rearrange("p h l -> p (h l)"),
                                 start=True, stop=True).then_inc(rowsum, 1)
                    if c >= LAG:
                        gate(c - LAG)
                for k in range(KD):
                    mm = t.matmul(psv[:, :], xts[:, k, :], w_xs[:, k, :], start=(k == 0), stop=(k == KD - 1))
                mm.then_inc(vs_prod, 1)
                pe.wait_ge(mixa_set, 1)
                for f in range(FT):
                    mm = t.transpose(pmt[:, f * NS:(f + 1) * NS], mixs[:, 0, f * P:(f + 1) * P], ident[0:NS, 0:NS])
                mm.then_inc(w_turned, 1)


        yb = sb("yb", [P, FT, SEQ], where=Place(nc, base))
        w_out = sb("w_out", [P, KD, D], where=Place(nc, base + 32 * KB))
        w_out_in = nc.alloc_semaphore("w_out_in")
        with phase() as ph:
            PS = 4
            ps_ = Place(nc, base + 32 * KB)
            umat = sb("umat", [P, PS, 2, 2, K + NS], where=ps_)
            sq = sb("sq", [P, PS, 2, 4 * P], where=ps_)
            smat = sq[:, :, 0, :].rearrange("p s (h r c) -> p s h r c", h=2, r=2)
            qmat = sq[:, :, 1, :].rearrange("p s (r c) -> p s r c", r=2)
            ps_.at = base + 64 * KB
            hst = sb("hst", [P, 2, 2, K + 1], where=ps_)
            pt = Place(nc, base + 128 * KB)
            ytok = sb("ytok", [P, L, 8, Q], where=pt)
            pt.at = base + 144 * KB
            h_rows = sb("h_rows", [NS, 2, G * N], where=Place(nc, base + 128 * KB))
            rot = sb("rot", [P, 8, K], where=pt)
            sg = sb("sg", [P, 2, SUP], where=ps_)
            bus = sb("bus", [P, 2, PAIRS, NS], where=pt)
            h0 = sb("h0", [P, 2, PAIRS, NS], where=ps_)
            ts = sb("ts", [P, 4, PAIRS, NS], where=ps_)
            ys_row = sb("ys_row", [NS, WA], where=ps_)
            assert ps_.at <= base + 80 * KB
            fin = sb("fin", [P, 2, PAIRS], where=pt)
            fin_t = sb("fin_t", [PAIRS, 2, P], where=pt)
            wglu = sb("wglu", [P, FT, Q], where=pt)
            wbd = k_lag[:, 0, :].rearrange("p (f g q) -> p f g q", f=FT, g=8)
            bglu = sb("bglu", [P, FT], where=pt)
            d8 = k_lag[0:NS, 1, :]
            yts = sb("yts", [P, 2, FT, NS], where=pt)
            pst = [ph.enter_context(nc.psum_tensor(f"p_state{i}", [P, 2, P + NS], F32)) for i in range(2)]
            py = [[ph.enter_context(nc.psum_tensor(f"p_y{i}{g}", [P, 2, L, Q], F32)) for g in range(2)] for i in range(2)]
            ptr = [ph.enter_context(nc.psum_tensor(f"p_turn{i}", [P, 4, P], F32)) for i in range(2)]
            pgl = [py[1][g][:].rearrange("p g j q -> p (g j q)") for g in range(2)]
            (wg_in, wg_set, col_in, s_prod, y_prod, w_rot, h_set, bus_set, y_gelu, y_turned, yb_set,
             glu_prod, glu_sig, glu_set, cdch, h0_in, h0_turned, h0_set, hs_set, ys_prod, ys_set, ys_gelu, ys_turned,
             ys_copied, gs_prod, gs_sig, mix_set, st_turned, st_copied, out_stored, fin_set, fin_turned,
             fin_copied, v_zero) = sems("""wg_in wg_set c_col_in s_prod y_prod w_rot h_set bus_set
             y_gelu y_turned yb_set glu_prod glu_sig glu_set cdch h0_in h0_turned h0_set hs_set ys_prod ys_set ys_gelu
             ys_turned ys_copied gs_prod gs_sig mix_set st_turned st_copied out_stored fin_set fin_turned fin_copied
             v_zero""")
            pair_in = [phase_sem(f"pair_in{i}") for i in range(PS)]
            QUADS = PAIRS // 4
            psy = py[0][0][0:NS].rearrange("p g j q -> p (g j q)")
            block = ph.enter_context(nc.Block())

            @block.sync
            def _(sp):
                def u_view(pair, h, g):
                    return u_dram[bass.ds((pair * 2 + g) * Q, Q), h * HALF:(h + 1) * HALF, :].rearrange("q j k -> j q k")

                def load(pair, b):
                    for h in range(2):
                        for g in range(2):
                            sp.dma_start(umat[:, b, h, g, 0:K], u_view(pair, h, g)).then_inc(pair_in[b], 16)
                    sp.dma_start(umat[:, b, 1, :, K:K + NS], us1[:, bass.ds(pair * 2, 2), :]).then_inc(pair_in[b], 16)
                    sp.dma_start(sq[:, b], sq_dram[pair]).then_inc(pair_in[b], 16)

                for b in range(PS):
                    load(b, b)
                with sp.Fori(0, PAIRS // PS - 1) as i:
                    for b in range(PS):
                        sp.wait_ge(y_prod, i * PS + b + 1)
                        load(i * PS + PS + b, b)
                sp.wait_ge(y_prod, PAIRS)
                sp.dma_start(w_out[:], a["w_out"][0].rearrange("(k p) n -> p k n", p=P)).then_inc(w_out_in, 16)
                sp.wait_ge(y_turned, 4 * QUADS)
                sp.dma_start(h_rows[:, 0, :], a["state_ssm_re"][0].rearrange("s g n -> s (g n)")).then_inc(h0_in, 16)
                sp.dma_start(h_rows[:, 1, :], a["state_ssm_im"][0].rearrange("s g n -> s (g n)")).then_inc(h0_in, 16)
                sp.wait_ge(fin_copied, 1)
                sp.dma_start(o["re_prompt"][0, 0].rearrange("(c g) n -> c (g n)", g=2), fin_t[:, 0, :]).then_inc(out_stored, 16)
                sp.dma_start(o["im_prompt"][0, 0].rearrange("(c g) n -> c (g n)", g=2), fin_t[:, 1, :]).then_inc(out_stored, 16)
                sp.wait_ge(st_copied, 8)
                sp.dma_start(o["re_sample"][0].rearrange("s g n -> s (g n)"), h_rows[:, 0, :]).then_inc(out_stored, 16)
                sp.dma_start(o["im_sample"][0].rearrange("s g n -> s (g n)"), h_rows[:, 1, :]).then_inc(out_stored, 16)
                sp.wait_ge(out_stored, 64)

            @block.gpsimd
            def _(gp):
                gp.dma_start(wglu[:], bass.AP(tensor=a["w_glu"].tensor, offset=0,
                             ap=[[Q, P], [P * Q, FT], [1, Q]])).then_inc(wg_in, 16)
                gp.dma_start(bglu[:], bass.AP(tensor=a["b_glu"].tensor, offset=0, ap=[[1, P], [P, FT]])).then_inc(col_in, 16)
                gp.dma_start(d8, bass.AP(tensor=a["ssm_d"].tensor, offset=0, ap=[[0, NS], [1, WA]])).then_inc(col_in, 16)
                gp.wait_ge(wg_in, 16)
                gp.tensor_copy(wbd, wglu[:].unsqueeze(2).broadcast_to([P, FT, 8, Q])).then_inc(wg_set, 1)
                gp.wait_ge(wg_set, 1)
                gp.affine_select(out=wbd, in_=wbd, compare_op=ALU.is_ge, fill=0.0, base=0,
                                 pattern=[[0, FT], [-Q, 8], [0, Q]], channel_multiplier=1).then_inc(wg_set, 1)
                gp.wait_ge(wg_set, 2)
                gp.affine_select(out=wbd, in_=wbd, compare_op=ALU.is_ge, fill=0.0, base=Q - 1,
                                 pattern=[[0, FT], [Q, 8], [0, Q]], channel_multiplier=-1).then_inc(wg_set, 1)

            @block.scalar
            def _(act):
                def quad(i):
                    for b in range(4):
                        act.wait_ge(y_prod, i * 4 + b + 1)
                        for g in range(2):
                            nc.scalar.activation(ytok[:, :, 2 * b + g, :], py[b % 2][g][:, 0],
                                                 ACT.Gelu_apprx_tanh).then_inc(y_gelu, 1)
                    for j in range(4):
                        act.wait_ge(y_turned, i * 4 + j + 1)
                        nc.scalar.copy(yb[:, i, :].rearrange("p (k j) -> p j k", j=L)[:, 4 * j:4 * j + 4, :],
                                       ptr[j % 2][:, :, :]).then_inc(yb_set, 1)

                with act.Fori(0, QUADS) as i:
                    quad(i)
                act.wait_ge(ys_set, 1)
                nc.scalar.activation(mixs[:, 1, :], ys_row[:, 0:WA], ACT.Gelu_apprx_tanh).then_inc(ys_gelu, 1)
                act.wait_ge(ys_turned, 1)
                nc.scalar.copy(yts[:, 0], pst[1][:, 0, 0:FT * NS].rearrange("p (f s) -> p f s", s=NS)).then_inc(ys_copied, 1)
                act.wait_ge(col_in, 32)
                for n in range(4 * FT):
                    act.wait_ge(glu_prod, n + 1)
                    if n >= 2:
                        act.wait_ge(glu_set, n - 1)
                    nc.scalar.activation(sg[:, n % 2, :], pgl[n % 2], ACT.Sigmoid, bias=bglu[:, n // 4:n // 4 + 1]).then_inc(glu_sig, 1)
                act.wait_ge(gs_prod, 1)
                for f in range(FT):
                    nc.scalar.activation(yts[:, 1, f, :], pst[1][:, 0, 64 + f * NS:64 + (f + 1) * NS], ACT.Sigmoid,
                                         bias=bglu[:, f:f + 1]).then_inc(gs_sig, 1)

            @block.vector
            def _(dve):
                v = nc.vector
                ch = Chain(dve, cdch)
                for b in range(2):
                    ch.mark(v.memset(hst[:, b, :, 0:1], 0.0))
                ch.settle()

                def scan_pair(pair, b, first):
                    dve.wait_ge(s_prod, pair + 1)
                    c, s = cos_k[:, pair, :], sin_k[:, pair, :]
                    sr, si = pst[b][:, 0, 0:K], pst[b][:, 1, 0:K]
                    t = [rot[:, k, :] for k in range(8)]
                    for k, (x, y) in enumerate([(c, sr), (s, si), (c, si), (s, sr)]):
                        ch.mark(v.tensor_tensor(t[k], x, y, ALU.mult))
                    v.tensor_copy(bus[:, :, pair, :], pst[b][:, :, K:K + NS]).then_inc(bus_set, 1)
                    ch.settle()
                    ch.mark(v.tensor_tensor(t[4], t[0], t[1], ALU.add))
                    v.tensor_tensor(t[5], t[2], t[3], ALU.subtract).then_inc(w_rot, 1)
                    ch.settle()
                    dve.wait_ge(w_rot, pair + 1)
                    decay = r16[:, pair:pair + 1] if isinstance(pair, int) else r16[:, bass.ds(pair, 1)]
                    decay = decay.broadcast_to([P, K])
                    ch.mark(v.tensor_tensor_scan(t[6], decay, t[4], 0.0, ALU.mult, ALU.add))
                    ch.mark(v.tensor_tensor_scan(t[7], decay, t[5], 0.0, ALU.mult, ALU.add))
                    ch.settle()
                    for k, (x, y) in enumerate([(c, t[6]), (s, t[7]), (c, t[7]), (s, t[6])]):
                        ch.mark(v.tensor_tensor(t[k], x, y, ALU.mult))
                    ch.settle()
                    if not first:
                        dve.wait_ge(y_prod, pair - 1)
                    ch.mark(v.tensor_tensor(hst[:, b, 0, 1:K + 1], t[0], t[1], ALU.subtract))
                    v.tensor_tensor(hst[:, b, 1, 1:K + 1], t[2], t[3], ALU.add).then_inc(h_set, 1)
                    ch.settle()
                    dve.wait_ge(h_set, pair + 1)
                    fp = fin[:, :, pair:pair + 1] if isinstance(pair, int) else fin[:, :, bass.ds(pair, 1)]
                    ch(v.tensor_copy(fp, hst[:, b, :, K:K + 1]))

                for b in range(2):
                    scan_pair(b, b, True)
                with dve.Fori(1, PAIRS // 2) as i:
                    ch.enter(i - 1, 26)
                    for b in range(2):
                        scan_pair(i * 2 + b, b, False)
                    ch.leave(PAIRS // 2 - 1)
                v.memset(rot[:, 0, :], 0.0).then_inc(fin_set, 1)
                dve.wait_ge(fin_turned, 1)
                v.tensor_copy(fin_t[:], ptr[0][0:PAIRS, 0:2, :]).then_inc(fin_copied, 1)
                dve.wait_ge(bus_set, PAIRS)
                dve.wait_ge(h0_turned, 1)
                v.tensor_copy(h0[:], ptr[1][:, :, :].rearrange("p a b -> p (a b)")[:, 0:2 * PAIRS * NS]
                              .rearrange("p (r c s) -> p r c s", r=2, c=PAIRS)).then_inc(h0_set, 1)
                dve.wait_ge(h0_set, 1)
                sh = [P, PAIRS, NS]
                lr, li = (x[:, 1, :].unsqueeze(2).broadcast_to(sh) for x in (p_re, p_im))
                for k, (x, y) in enumerate([(lr, h0[:, 0]), (li, h0[:, 1]), (lr, h0[:, 1]), (li, h0[:, 0])]):
                    ch.mark(v.tensor_tensor(ts[:, k], x, y, ALU.mult))
                ch.settle()
                ch.mark(v.tensor_tensor(ts[:, 0], ts[:, 0], ts[:, 1], ALU.subtract))
                ch.mark(v.tensor_tensor(ts[:, 2], ts[:, 2], ts[:, 3], ALU.add))
                ch.settle()
                v.tensor_tensor(h0[:, 0], ts[:, 0], bus[:, 0], ALU.add).then_inc(hs_set, 1)
                v.tensor_tensor(h0[:, 1], ts[:, 2], bus[:, 1], ALU.add).then_inc(hs_set, 1)
                dve.wait_ge(col_in, 32)
                ch(v.tensor_tensor(ys_row[:], d8, us[:, 1, :], ALU.mult))
                dve.wait_ge(ys_prod, 1)
                v.tensor_tensor(ys_row[:], psy[:, :], ys_row[:], ALU.add).then_inc(ys_set, 1)
                for n in range(8):
                    dve.wait_ge(st_turned, n + 1)
                    v.tensor_copy(h_rows[:, n // 4, (n % 4) * 512:(n % 4 + 1) * 512],
                                  ptr[n % 2][0:NS].rearrange("p a b -> p (a b)")).then_inc(st_copied, 1)
                for n in range(4 * FT):
                    dve.wait_ge(glu_sig, n + 1)
                    part = yb[:, n // 4, (n % 4) * SUP:(n % 4 + 1) * SUP]
                    v.tensor_tensor(part, part, sg[:, n % 2, :], ALU.mult).then_inc(glu_set, 1)
                dve.wait_ge(gs_sig, FT)
                v.tensor_tensor(mixs_t[:, FT:KD, :], yts[:, 0], yts[:, 1], ALU.mult).then_inc(mix_set, 1)

            @block.tensor
            def _(pe):
                t = nc.tensor

                def states(pair, slot, first, count):
                    b = slot % 2
                    pe.wait_ge(pair_in[slot], count * 96)
                    if not first:
                        pe.wait_ge(w_rot, pair - 1)
                        pe.wait_ge(bus_set, pair - 1)
                    for r in range(2):
                        for g in range(2):
                            lhs = [smat[:, slot, h, r, g * N:(g + 1) * N] for h in range(2)]
                            dst = pst[b][g * N:(g + 1) * N, r, :]
                            for h in range(2):
                                t.matmul(dst[:, 0:K], lhs[h], umat[:, slot, h, g, 0:K], start=(h == 0), stop=(h == 1))
                            mm = t.matmul(dst[:, K:K + NS], lhs[1], umat[:, slot, 1, g, K:K + NS], start=True, stop=True)
                    mm.then_inc(s_prod, 1)

                def outputs(pair, slot, first):
                    b = slot % 2
                    if not first:
                        pe.wait_ge(y_gelu, pair * 2 - 2)
                    for g in range(2):
                        dst = py[b][g][:, 0]
                        col = (pair * 2 + g) * Q
                        t.matmul(dst, umat[:, slot, 0, g, 0:K], toep[:, :, bass.ds(col, Q)], start=True, stop=False)
                        t.matmul(dst[:, HALF:L, :], umat[:, slot, 1, g, 0:K], toep[:, 0:HALF, bass.ds(col, Q)],
                                 start=False, stop=False)
                    pe.wait_ge(h_set, pair + 1)
                    for r in range(2):
                        for g in range(2):
                            rows = slice(g * N, (g + 1) * N)
                            mm = t.matmul(py[b][g][:, 0].rearrange("p j q -> p (j q)"), hst[rows, b, r, 0:K],
                                          qmat[rows, slot, r, :], start=False, stop=(r == 1))
                    mm.then_inc(y_prod, 1)

                def quad(i, first, last):
                    for b in range(4):
                        if not (last and b == 3):
                            states(i * 4 + b + 1, (b + 1) % PS, first and b == 0, i + (b + 1) // PS + 1)
                        outputs(i * 4 + b, b, first and b < 2)
                    pe.wait_ge(y_gelu, i * 8 + 8)
                    for j in range(L):
                        if j % 4 == 0 and not (first and j < 8):
                            pe.wait_ge(yb_set, i * 4 + j // 4 - 1)
                        mm = t.transpose(ptr[j // 4 % 2][:, j % 4, :], ytok[:, j].rearrange("p g q -> p (g q)"), ident[:])
                        if j % 4 == 3:
                            mm.then_inc(y_turned, 1)

                states(0, 0, True, 1)
                quad(0, True, False)
                with pe.Fori(1, QUADS - 1) as i:
                    quad(i, False, False)
                quad(QUADS - 1, False, True)
                pe.wait_ge(fin_set, 1)
                pe.wait_ge(yb_set, 4 * QUADS)
                for r in range(2):
                    mm = t.transpose(ptr[0][0:PAIRS, r, :], fin[:, r, :], ident[:])
                mm.then_inc(fin_turned, 1)
                pe.wait_ge(h0_in, 32)
                flat = ptr[1][:, :, :].rearrange("p a b -> p (a b)")
                for r in range(2):
                    for c in range(PAIRS):
                        mm = t.transpose(flat[:, (r * PAIRS + c) * NS:(r * PAIRS + c + 1) * NS],
                                         h_rows[:, r, c * P:(c + 1) * P], ident[0:NS, 0:NS])
                mm.then_inc(h0_turned, 1)
                pe.wait_ge(hs_set, 2)
                for c in range(PAIRS):
                    dst = psy[:, c * 2 * Q:(c + 1) * 2 * Q]
                    t.matmul(dst, h0[:, 0, c, :], cb_re[:, c].rearrange("p h q -> p (h q)"), start=True, stop=False)
                    mm = t.matmul(dst, h0[:, 1, c, :], cb_im[:, c].rearrange("p h q -> p (h q)"), start=False, stop=True)
                mm.then_inc(ys_prod, 1)
                pe.wait_ge(fin_copied, 1)
                for n in range(8):
                    if n >= 2:
                        pe.wait_ge(st_copied, n - 1)
                    for c in range(4):
                        mm = t.transpose(ptr[n % 2][0:NS, c, :], h0[:, n // 4, (n % 4) * 4 + c, :], ident[:])
                    mm.then_inc(st_turned, 1)
                pe.wait_ge(ys_gelu, 1)
                for f in range(FT):
                    mm = t.transpose(pst[1][:, 0, f * NS:(f + 1) * NS], mixs[:, 1, f * P:(f + 1) * P], ident[0:NS, 0:NS])
                mm.then_inc(ys_turned, 1)
                pe.wait_ge(wg_set, 3)
                for n in range(4 * FT):
                    if n >= 2:
                        pe.wait_ge(glu_sig, n - 1)
                    f = n // 4
                    t.matmul(pgl[n % 2], wbd[:, f].rearrange("p g q -> p (g q)"), yb[:, f, (n % 4) * SUP:(n % 4 + 1) * SUP],
                             start=True, stop=True).then_inc(glu_prod, 1)
                pe.wait_ge(ys_copied, 1)
                for f in range(FT):
                    mm = t.matmul(pst[1][:, 0, 64 + f * NS:64 + (f + 1) * NS], wbd[:, f].rearrange("p g q -> p (g q)"),
                                  yts[:, 0, f, :], start=True, stop=True)
                mm.then_inc(gs_prod, 1)

        TILES = CH + 1
        late = Place(nc, base + 150 * KB)
        scores = sb("scores", [P, TILES, E], where=late)
        w_slots = sb("w_slots", [P, 4, 3 * KD * FF], where=Place(nc, base + 53 * KB))
        with phase() as ph:
            pt = Place(nc, base + 64 * KB)
            xres = sb("xres", [P, 2, D], where=pt)
            z = sb("z", [P, 2, D], where=pt)
            x1 = sb("x1", [P, 2, D], where=pt)
            ax1 = sb("ax1", [P, 2, D], where=pt)
            x1t = sb("x1t", [P, 2, KD, P], where=pt)
            mixt = sb("mixt", [P, 2, KD, P], where=pt)
            g1_row, b1_row = sb("g1_row", [P, D], where=pt), sb("b1_row", [P, D], where=pt)
            w_r = sb("w_r", [P, KD, E], where=pt)
            st = sb("st1", [P, 2, 2, 6], where=pt)
            spare = sb("spare_d", [P, 1], where=pt)
            ag = sb("ag1", [P, 2, 2], where=pt)
            rs = sb("rs1", [P, 2, 2], where=pt)
            neg_half = sb("neg_half", [P, 1], where=pt)
            po = [[ph.enter_context(nc.psum_tensor(f"p_out{i}{n}", [P, SUP], F32)) for n in range(2)] for i in range(2)]
            ptr = [ph.enter_context(nc.psum_tensor(f"p_x1t{i}", [P, 4, P], F32)) for i in range(2)]
            prt = ph.enter_context(nc.psum_tensor("p_router", [P, E], F32))
            (row_in, half_set, mix_copied, o_prod, z_set, var_set, rstd_set, x1_set, ax1_set, x1_turned, x1t_act,
             x1t_dve, r_prod, r_set, sc_zero, ddch) = sems("""row1_in half_set mix_copied o_prod z_set var1_set
             rstd1_set x1_set ax1_set x1_turned x1t_act x1t_dve r_prod r_set sc_zero ddch""")
            xres_in = [phase_sem(f"xres_in{i}") for i in range(2)]
            x1_stored = [phase_sem(f"x1_stored{i}") for i in range(2)]
            ax1_stored = [phase_sem(f"ax1_stored{i}") for i in range(2)]
            block = ph.enter_context(nc.Block())

            @block.sync
            def _(sp):
                for b in range(2):
                    sp.dma_start(xres[:, b, :], a["x_prompt"][0, b * P:(b + 1) * P, :]).then_inc(xres_in[b], 16)
                for dst, name in ((g1_row, "ln1_g"), (b1_row, "ln1_b")):
                    sp.dma_start(dst[:], bass.AP(tensor=a[name].tensor, offset=0, ap=[[0, P], [1, D]])).then_inc(row_in, 16)
                sp.dma_start(w_r[:], a["w_router"].rearrange("(k p) e -> p k e", p=P)).then_inc(row_in, 16)

                def stores(c, b):
                    rows = bass.ds(c * P, P)
                    sp.wait_ge(x1_set, c + 1)
                    sp.dma_start(x1_dram[rows, :], x1[:, b, :]).then_inc(x1_stored[b], 16)
                    sp.wait_ge(ax1_set, c + 1)
                    sp.dma_start(acc_dram[rows, :], ax1[:, b, :]).then_inc(ax1_stored[b], 16)

                with sp.Fori(0, CH // 2 - 1) as i:
                    for b in range(2):
                        sp.wait_ge(z_set, i * 4 + 2 * b + 2)
                        sp.dma_start(xres[:, b, :], a["x_prompt"][0, bass.ds((i * 2 + 2 + b) * P, P), :]).then_inc(xres_in[b], 16)
                        stores(i * 2 + b, b)
                sp.wait_ge(z_set, 2 * CH - 2)
                sp.dma_start(xres[0:NS, 0, :], a["x_sample"][:, 0, :]).then_inc(xres_in[0], 16)
                for b in range(2):
                    stores(CH - 2 + b, b)
                sp.wait_ge(x1_set, CH + 1)
                sp.dma_start(x1_dram[SEQ:, :], x1[0:NS, 0, :]).then_inc(x1_stored[0], 16)
                sp.wait_ge(ax1_set, CH + 1)
                sp.dma_start(acc_dram[SEQ:SEQ + NS, :], ax1[0:NS, 0, :]).then_inc(ax1_stored[0], 16)
                sp.dma_start(acc_dram[SEQ + NS:, :], ax1[:, 1, :]).then_inc(ax1_stored[1], 16)
                for s in (x1_stored, ax1_stored):
                    sp.wait_ge(s[0], (CH // 2 + 1) * 16)
                sp.wait_ge(x1_stored[1], CH // 2 * 16)
                sp.wait_ge(ax1_stored[1], (CH // 2 + 1) * 16)

            @block.gpsimd
            def _(gp):
                gp.memset(scores[:], 0.0).then_inc(sc_zero, 1)
                gp.memset(neg_half[:], -0.5).then_inc(half_set, 1)
                gp.wait_ge(half_set, 1)

                def copies(c, b, first):
                    if not first:
                        gp.wait_ge(o_prod, c - 1)
                    cols = bass.ds(c * P, P)
                    gp.tensor_copy(mixt[:, b, 0:FT], ya[:, :, cols]).then_inc(mix_copied, 1)
                    gp.tensor_copy(mixt[:, b, FT:KD], yb[:, :, cols]).then_inc(mix_copied, 1)

                def root(c, b, n=P):
                    gp.wait_ge(var_set, c + 1)
                    gp.tensor_tensor(rs[0:n, b, 1:2], rs[0:n, b, 0:1], neg_half[0:n], ALU.pow).then_inc(rstd_set, 1)

                for b in range(2):
                    copies(b, b, True)
                with gp.Fori(0, CH // 2 - 1) as i:
                    for b in range(2):
                        copies(i * 2 + 2 + b, b, False)
                        root(i * 2 + b, b)
                for b in range(2):
                    root(CH - 2 + b, b)
                root(CH, 0, NS)

            @block.scalar
            def _(act):
                def tile(c, b, half, n=P):
                    act.wait_ge(x1_set, c + 1)
                    if half is not None:
                        act.wait_ge(ax1_stored[b], half * 16)
                    nc.scalar.mul(ax1[0:n, b, :], x1[0:n, b, :], ALPHA).then_inc(ax1_set, 1)
                    act.wait_ge(x1_turned, c + 1)
                    if half is not None:
                        act.wait_ge(r_prod, c - 1)
                    nc.scalar.copy(x1t[:, b, 0:4, 0:n], ptr[0][:, :, 0:n]).then_inc(x1t_act, 1)

                def score(c, n=P):
                    act.wait_ge(r_prod, c + 1)
                    nc.scalar.activation(scores[0:n, c, :], prt[0:n, :], ACT.Sigmoid).then_inc(r_set, 1)

                act.wait_ge(sc_zero, 1)
                tile(0, 0, None)
                tile(1, 1, None)
                score(0)
                with act.Fori(1, CH // 2) as i:
                    for b in range(2):
                        tile(i * 2 + b, b, i)
                        score(i * 2 + b - 1)
                tile(CH, 0, CH // 2, NS)
                score(CH - 1)
                score(CH, NS)

            @block.vector
            def _(dve):
                v = nc.vector
                ch = Chain(dve, ddch)

                def norm(c, b, first, half, n=P):
                    dve.wait_ge(xres_in[b], (half + 1) * 16)
                    dve.wait_ge(o_prod, c + 1)
                    for m in range(2):
                        cols = slice(m * SUP, (m + 1) * SUP)
                        v.scalar_tensor_tensor(z[0:n, b, cols], xres[0:n, b, cols], ALPHA, po[b][m][0:n, :], ALU.mult,
                                               ALU.add).then_inc(z_set, 1)
                    dve.wait_ge(z_set, c * 2 + 2)
                    for m in range(2):
                        ch.mark(v.bn_stats(st[0:n, b, m, :], z[0:n, b, m * SUP:(m + 1) * SUP]))
                    ch.settle()
                    v.memset(spare[:], 0.0)
                    ch(v.bn_aggr(ag[0:n, b, :], st[0:n, b]))
                    v.tensor_scalar(rs[0:n, b, 0:1], ag[0:n, b, 1:2], EPS, None, ALU.add).then_inc(var_set, 1)
                    if not first:
                        dve.wait_ge(x1_stored[b], half * 16)
                        dve.wait_ge(ax1_set, c - 1)
                        dve.wait_ge(x1_turned, c - 1)
                    ch(v.scalar_tensor_tensor(z[0:n, b, :], z[0:n, b, :], ag[0:n, b, 0:1], g1_row[0:n, :], ALU.subtract, ALU.mult))
                    dve.wait_ge(rstd_set, c + 1)
                    v.scalar_tensor_tensor(x1[0:n, b, :], z[0:n, b, :], rs[0:n, b, 1:2], b1_row[0:n, :], ALU.mult,
                                           ALU.add).then_inc(x1_set, 1)

                def turn(c, b, first=False, n=P):
                    dve.wait_ge(x1_turned, c + 1)
                    if not first:
                        dve.wait_ge(r_prod, c - 1)
                    v.tensor_copy(x1t[:, b, 4:8, 0:n], ptr[1][:, :, 0:n]).then_inc(x1t_dve, 1)

                dve.wait_ge(row_in, 48)
                for b in range(2):
                    norm(b, b, True, 0)
                    if b:
                        turn(0, 0, True)
                for b in range(2):
                    norm(2 + b, b, False, 1)
                    turn(1 + b, 1 - b, b == 0)
                with dve.Fori(2, CH // 2) as i:
                    ch.enter(i - 2, 8)
                    for b in range(2):
                        norm(i * 2 + b, b, False, i)
                        turn(i * 2 + b - 1, (b + 1) % 2)
                    ch.leave(CH // 2 - 2)
                norm(CH, 0, False, CH // 2, NS)
                turn(CH - 1, 1)
                turn(CH, 0, False, NS)

            @block.tensor
            def _(pe):
                t = nc.tensor

                def out(c, b, first):
                    pe.wait_ge(mix_copied, c * 2 + 2)
                    if not first:
                        pe.wait_ge(z_set, c * 2 - 2)
                    for m in range(2):
                        for k in range(KD):
                            mm = t.matmul(po[b][m][:, :], mixt[:, b, k, :], w_out[:, k, m * SUP:(m + 1) * SUP],
                                          start=(k == 0), stop=(k == KD - 1))
                    mm.then_inc(o_prod, 1)

                def turn(c, b, first, n=P):
                    pe.wait_ge(x1_set, c + 1)
                    if not first:
                        pe.wait_ge(x1t_act, c)
                        pe.wait_ge(x1t_dve, c)
                    for k in range(KD):
                        mm = t.transpose(ptr[k // 4][:, k % 4, 0:n], x1[0:n, b, k * P:(k + 1) * P], ident[0:n, 0:n])
                    mm.then_inc(x1_turned, 1)

                def router(c, b, first, n=P):
                    pe.wait_ge(x1t_act, c + 1)
                    pe.wait_ge(x1t_dve, c + 1)
                    if not first:
                        pe.wait_ge(r_set, c)
                    for k in range(KD):
                        mm = t.matmul(prt[0:n, :], x1t[:, b, k, 0:n], w_r[:, k, :], start=(k == 0), stop=(k == KD - 1))
                    mm.then_inc(r_prod, 1)

                pe.wait_ge(w_out_in, 16)
                pe.wait_ge(row_in, 48)
                out(0, 0, True)
                out(1, 1, True)
                turn(0, 0, True)
                out(2, 0, False)
                turn(1, 1, False)
                router(0, 0, True)
                out(3, 1, False)
                turn(2, 0, False)
                router(1, 1, False)
                with pe.Fori(2, CH // 2) as i:
                    for b in range(2):
                        out(i * 2 + b, b, False)
                        turn(i * 2 + b - 1, (b + 1) % 2, False)
                        router(i * 2 + b - 2, b, False)
                pe.wait_ge(z_set, CH * 2 - 2)
                for m in range(2):
                    for k in range(KD):
                        mm = t.matmul(po[0][m][0:NS, :], mixs_t[:, k, :], w_out[:, k, m * SUP:(m + 1) * SUP],
                                      start=(k == 0), stop=(k == KD - 1))
                mm.then_inc(o_prod, 1)
                turn(CH - 1, 1, False)
                router(CH - 2, 0, False)
                turn(CH, 0, False, NS)
                router(CH - 1, 1, False)
                router(CH, 0, False, NS)

        ROWS = SEQ + NS
        NT = (2 * ROWS + E * (P - 1)) // P
        GS = 4
        NT += -NT % GS
        BIG = 1e30
        with phase() as ph:
            pt = Place(nc, base)
            def tmp(name, shape, dt=F32):
                return sb(name, shape, dt, where=pt)

            bi, m1, oh1, oh2, msk, tot, pos, bas = (tmp(n, [P, TILES, E]) for n in
                                                    ("bi", "m1", "oh1", "oh2", "msk", "tot", "pos", "bas"))
            tot_e, inc_e, reset = (tmp(n, [P, E, TILES]) for n in ("tot_e", "inc_e", "reset"))
            pairs6 = tmp("pairs6", [P, TILES * EG, 6])
            gs, gq = tmp("gs", [P, TILES, EG]), tmp("gq", [P, TILES, EG])
            red, s1, s2, den, gw1, gw2 = (tmp(n, [P, TILES]) for n in ("red", "s1", "s2", "den", "gw1", "gw2"))
            rowf, tilef, gate_k = (tmp(n, [P, 2, TILES]) for n in ("rowf", "tilef", "gate_k"))
            posi, posj = tmp("posi", [P, TILES], I32), tmp("posj", [P, TILES], I32)
            w4, w16_, i48, i128 = tmp("w4", [P, EG]), tmp("w16r", [P, E]), tmp("i48", [P, NT]), tmp("i128", [P, P])
            thr, id1, valid, padrow = tmp("thr", [P, TILES]), tmp("id1", [P, TILES]), tmp("valid", [P, TILES]), tmp("padrow", [P, 1])
            below, ones2 = tmp("below", [P, P]), tmp("ones2", [P, P])
            rb = tmp("rb", [P, E])
            nt, te, ones_e = tmp("nt", [P, E]), tmp("te", [P, E]), tmp("ones_e", [P, E])
            cmp_, tix, tfl, tsl = tmp("cmp", [P, NT, E]), tmp("tix", [P, NT]), tmp("tfl", [P, NT]), tmp("tsl", [P, NT])
            lst, pad = tmp("lst", [P, NT]), tmp("pad", [P, NT])
            rowhot, tilehot = tmp("rowhot", [P, 2, P]), tmp("tilehot", [P, 2, 2, NT])
            assert pt.at <= base + 34 * KB, pt.at - base
            gates = sb("gates", [P, NT], where=late)
            g_idx, s_idx = sb("g_idx", [P, NT], U32, where=late), sb("s_idx", [P, NT], U32, where=late)
            tab = sb("tab", [P, 2, NT], I32, where=late)
            tab_e = sb("tab_e", [P, E], I32, where=late)
            spare, nothing = sb("spare_e", [P, 1], where=late), sb("nothing", [P, 1], where=late)
            gi, si = sb("gi", [P, GS], U32, where=late), sb("si", [P, 2], U32, where=late)
            pt = Place(nc, base)
            xgt = sb("xgt", [P, 2, KD, P], where=pt)
            yo = sb("yo", [P, 2, D], where=pt)
            sl = sb("sl", [P, 2, FF], where=pt)
            hh = sb("hh", [P, 2, FF], where=pt)
            ht = sb("ht", [P, 2, 2, P], where=pt)
            pt = Place(nc, base + 34 * KB)
            xg = sb("xg", [P, GS, D], where=pt)
            assert pt.at <= base + 53 * KB
            pg = [ph.enter_context(nc.psum_tensor(f"p_gu{i}", [P, 2, FF], F32)) for i in range(2)]
            pt_x = [ph.enter_context(nc.psum_tensor(f"p_xt{i}", [P, 4, P], F32)) for i in range(2)]
            pt_h = ph.enter_context(nc.psum_tensor("p_ht", [P, 2, P], F32))
            pd = [ph.enter_context(nc.psum_tensor(f"p_d{i}", [P, SUP], F32)) for i in range(2)]
            p_ls = ph.enter_context(nc.psum_tensor("p_list", [P, 2, NT], F32))
            (nothing_set, consts, rb_in, oh_set, cnt_prod, tables_set, hot_set, hot_used, list_prod, lists_set, w_dma, weights_ready,
             edch, gi_set, si_set, x_turned, xt_act, xt_dve, gu_prod, silu_set, h_set, h_turned, ht_set, d_prod, yo_act,
             yo_dve, added, te_set) = sems("""nothing_set consts rb_in oh_set cnt_prod tables_set2 hot_set hot_used list_prod
             lists_set w_dma weights_ready edch gi_set si_set xg_turned xg_act xg_dve gu_prod silu_set hh_set h_turned
             ht_set d_prod yo_act yo_dve added te_set""")
            xg_in = [phase_sem(f"xg_in{i}") for i in range(GS)]
            block = ph.enter_context(nc.Block())

            @block.sync
            def _(sp):
                def load(e, slot):
                    for n, (name, at) in enumerate((("w_gate", 0), ("w_up", KD * FF), ("w_down", 2 * KD * FF))):
                        sp.dma_start(w_slots[:, slot, at:at + KD * FF],
                                     a[name][0, e].rearrange("(p k) f -> p (k f)", p=P)).then_inc(w_dma, 16)

                for e in range(4):
                    load(e, 3 - e)
                sp.wait_ge(w_dma, 4 * 48)
                sp.sem_inc(weights_ready, 4)
                sp.wait_ge(te_set, 1)
                with sp.Fori(1, E // 4) as i:
                    for b in range(4):
                        free = sp.value_load(tab_e[0:1, bass.ds(i * 4 + b - 4, 1)], min_val=1, max_val=NT + 1)
                        sp.wait_ge(d_prod, free)
                        load(i * 4 + b, 3 - b)
                        sp.wait_ge(w_dma, (i * 4 + b + 1) * 48)
                        sp.sem_inc(weights_ready, 1)

            @block.gpsimd
            def _(gp):
                io = dict(allow_small_or_imprecise_dtypes=True)
                gp.dma_start(rb[:], bass.AP(tensor=a["router_bias"].tensor, offset=0, ap=[[0, P], [1, E]])).then_inc(rb_in, 16)
                gp.iota(w4[:], [[-1, EG]], base=EG, channel_multiplier=0, **io).then_inc(consts, 1)
                gp.iota(w16_[:], [[-1, E]], base=E, channel_multiplier=0, **io).then_inc(consts, 1)
                gp.iota(i48[:], [[1, NT]], base=0, channel_multiplier=0, **io).then_inc(consts, 1)
                gp.iota(i128[:], [[1, P]], base=0, channel_multiplier=0, **io).then_inc(consts, 1)
                gp.iota(thr[:], [[P, TILES]], base=0, channel_multiplier=0, **io).then_inc(consts, 1)
                gp.iota(id1[:], [[P, TILES]], base=1, channel_multiplier=1, **io).then_inc(consts, 1)
                gp.iota(padrow[:], [[0, 1]], base=ROWS + 1, channel_multiplier=1, **io).then_inc(consts, 1)
                gp.memset(valid[:], 1.0).then_inc(consts, 1)
                gp.memset(ones2[:], 1.0).then_inc(consts, 1)
                gp.memset(ones_e[:], 1.0).then_inc(consts, 1)
                gp.memset(reset[:], 1.0).then_inc(consts, 1)
                gp.wait_ge(consts, 11)
                gp.memset(nothing[:], 0.0).then_inc(nothing_set, 1)
                gp.wait_ge(nothing_set, 1)
                gp.memset(reset[:, :, 0:1], 0.0).then_inc(consts, 1)
                gp.affine_select(out=valid[:, CH:CH + 1], in_=valid[:, CH:CH + 1], compare_op=ALU.is_ge, fill=0.0,
                                 base=NS - 1, pattern=[[0, 1]], channel_multiplier=-1).then_inc(consts, 1)
                gp.affine_select(out=below[:], in_=ones2[:], compare_op=ALU.is_gt, fill=0.0, base=0,
                                 pattern=[[1, P]], channel_multiplier=-1).then_inc(consts, 1)


                def gather(i, b, first):
                    if not first:
                        gp.wait_ge(xg_in[b], (i - b) * (16 // GS))
                        gp.wait_ge(x_turned, i - GS + 1)
                    gp.tensor_copy(gi[:, b:b + 1], g_idx[:, bass.ds(i, 1)]).then_inc(gi_set, 1)
                    gp.wait_ge(gi_set, i + 1)
                    gp.tensor_tensor(spare[:], nothing[:], nothing[:], ALU.add)
                    gp.indirect_dma_start(xg[:, b, :], None, x1_dram,
                                          bass.IndirectOffsetOnAxis(ap=gi[:, b:b + 1], axis=0)).then_inc(xg_in[b], 16)

                def add(i, b, first):
                    if not first:
                        gp.wait_ge(added, i * 16)
                    gp.tensor_copy(si[:, b:b + 1], s_idx[:, bass.ds(i, 1)]).then_inc(si_set, 1)
                    gp.wait_ge(si_set, i + 1)
                    gp.wait_ge(yo_act, i + 1)
                    gp.wait_ge(yo_dve, i + 1)
                    gp.tensor_tensor(spare[:], nothing[:], nothing[:], ALU.add)
                    gp.indirect_dma_start(acc_dram, bass.IndirectOffsetOnAxis(ap=si[:, b:b + 1], axis=0),
                                          yo[:, b, :], None, compute_op=ALU.add).then_inc(added, 16)

                gp.wait_ge(lists_set, 1)
                for b in range(GS):
                    gather(b, b, True)
                for b in range(GS):
                    gather(GS + b, b, False)
                    add(b, b % 2, b == 0)
                with gp.Fori(1, NT // GS - 1) as i:
                    for b in range(GS):
                        gather(i * GS + GS + b, b, False)
                        add(i * GS + b, b % 2, False)
                for b in range(GS):
                    add(NT - GS + b, b % 2, False)
                gp.wait_ge(added, NT * 16)

            @block.vector
            def _(dve):
                v = nc.vector
                ch = Chain(dve, edch)
                tt, ts, stt, rd = v.tensor_tensor, v.tensor_scalar, v.scalar_tensor_tensor, v.tensor_reduce
                dve.wait_ge(consts, 14)
                dve.wait_ge(rb_in, 16)
                full = [P, TILES, E]
                ch(tt(bi[:], scores[:], rb[:].unsqueeze(1).broadcast_to(full), ALU.add))
                q4 = bi[:].rearrange("p t (g e) -> p (t g) e", e=EG)
                ch.mark(tt(pairs6[:, :, 0:3], q4[:, :, 0:3], q4[:, :, 1:4], ALU.add))
                ch.mark(tt(pairs6[:, :, 3:5], q4[:, :, 0:2], q4[:, :, 2:4], ALU.add))
                ch.mark(tt(pairs6[:, :, 5:6], q4[:, :, 0:1], q4[:, :, 3:4], ALU.add))
                ch.settle()
                ch(rd(gs[:].rearrange("p t g -> p (t g)"), pairs6[:], axis=AX, op=ALU.max))

                def first_max(x, weight, out, n):
                    sh = [P, TILES, n]
                    ch(rd(red[:], x, axis=AX, op=ALU.max))
                    ch(tt(out, x, red[:].unsqueeze(2).broadcast_to(sh), ALU.is_equal))
                    ch(tt(out, out, weight[:].unsqueeze(1).broadcast_to(sh), ALU.mult))
                    ch(rd(red[:], out, axis=AX, op=ALU.max))
                    ch(tt(out, out, red[:].unsqueeze(2).broadcast_to(sh), ALU.is_equal))

                first_max(gs[:], w4, gq[:], EG)
                by_group = [P, TILES, EG, E // EG]
                m4, b4 = (x[:].rearrange("p t (g e) -> p t g e", e=EG) for x in (m1, bi))
                ch(tt(m4, b4, gq[:].unsqueeze(3).broadcast_to(by_group), ALU.mult))
                ch(ts(gq[:], gq[:], BIG, -BIG, ALU.mult, ALU.add))
                ch(tt(m4, m4, gq[:].unsqueeze(3).broadcast_to(by_group), ALU.add))
                first_max(m1[:], w16_, oh1[:], E)
                ch(stt(m1[:], oh1[:], -2 * BIG, m1[:], ALU.mult, ALU.add))
                first_max(m1[:], w16_, oh2[:], E)
                vb = valid[:].unsqueeze(2).broadcast_to(full)
                for oh, s in ((oh1, s1), (oh2, s2)):
                    ch(tt(oh[:], oh[:], vb, ALU.mult))
                    ch(tt(msk[:], oh[:], scores[:], ALU.mult))
                    ch(rd(s[:], msk[:], axis=AX, op=ALU.add))
                ch(tt(den[:], s1[:], s2[:], ALU.add))
                ch(tt(den[:], den[:], valid[:], ALU.subtract))
                ch(ts(den[:], den[:], 1.0, None, ALU.add))
                ch(v.reciprocal(den[:], den[:]))
                ch(tt(gate_k[:, 0, :], s1[:], den[:], ALU.mult))
                ch(tt(gate_k[:, 1, :], s2[:], den[:], ALU.mult))
                tt(msk[:], oh1[:], oh2[:], ALU.add).then_inc(oh_set, 1)
                dve.wait_ge(cnt_prod, 1)
                cnt = pd[1][:, 0:TILES * E].rearrange("p (t e) -> p t e", e=E)
                pre = pd[0][:, 0:TILES * E].rearrange("p (t e) -> p t e", e=E)
                ch(v.tensor_copy(tot_e[:].rearrange("p e t -> p t e"), cnt))
                flat = "p e t -> p (e t)"
                ch(v.tensor_tensor_scan(inc_e[:].rearrange(flat), reset[:].rearrange(flat), tot_e[:].rearrange(flat), 0.0,
                                        ALU.mult, ALU.add))
                by_e = [P, E, TILES]
                ch(tt(reset[:], inc_e[:, :, TILES - 1:TILES].broadcast_to(by_e), thr[:].unsqueeze(1).broadcast_to(by_e), ALU.is_gt))
                ch(rd(nt[:], reset[:], axis=AX, op=ALU.add))
                ch(v.tensor_tensor_scan(te[:], ones_e[:], nt[:], 0.0, ALU.mult, ALU.add))
                ts(tab_e[:], te[:], 1.0, None, ALU.add).then_inc(te_set, 1)
                ch(tt(nt[:], te[:], nt[:], ALU.subtract))
                ch(tt(inc_e[:], inc_e[:], tot_e[:], ALU.subtract))
                ch(stt(inc_e[:], nt[:].unsqueeze(2).broadcast_to(by_e), float(P), inc_e[:], ALU.mult, ALU.add))
                ch(tt(pos[:], pre, inc_e[:].rearrange("p e t -> p t e"), ALU.add))
                for k, oh in enumerate((oh1, oh2)):
                    ch(tt(m1[:], oh[:], pos[:], ALU.mult))
                    ch(rd(red[:], m1[:], axis=AX, op=ALU.add))
                    ch(v.tensor_copy(posi[:], red[:]))
                    ch(ts(posj[:], posi[:], P - 1, None, ALU.bitwise_and))
                    ch(v.tensor_copy(rowf[:, k, :], posj[:]))
                    ch(ts(posj[:], posi[:], 7, None, ALU.logical_shift_right))
                    ch(v.tensor_copy(tilef[:, k, :], posj[:]))
                    ch(tt(gate_k[:, k, :], gate_k[:, k, :], valid[:], ALU.mult))
                ch(tt(id1[:], id1[:], valid[:], ALU.mult))
                by_t = [P, NT, E]
                ch(tt(cmp_[:], te[:].unsqueeze(1).broadcast_to(by_t), i48[:].unsqueeze(2).broadcast_to(by_t), ALU.is_le))
                ch(rd(tix[:], cmp_[:], axis=AX, op=ALU.add))
                ch(ts(tix[:], tix[:], float(E - 1), None, ALU.min))
                ch(ts(tfl[:], tix[:], 4.0, None, ALU.is_ge))
                for j in (8.0, 12.0):
                    ch(stt(tfl[:], tix[:], j, tfl[:], ALU.is_ge, ALU.add))
                ch(stt(tsl[:], tfl[:], 4.0, tix[:], ALU.mult, ALU.subtract))
                ch(ts(tsl[:], tsl[:], 3.0, None, ALU.add))
                v.tensor_copy(tab[:, 0, :], tsl[:]).then_inc(te_set, 1)
                ts(tab[:, 1, :], tix[:], 1.0, None, ALU.add).then_inc(te_set, 1)

                def hots(c, first):
                    for k in range(2):
                        if not first:
                            dve.wait_ge(hot_used, c * 2 + k - 1)
                        col = bass.ds(c, 1)
                        ch.mark(ts(rowhot[:, k, :], i128[:], rowf[:, k, col], None, ALU.is_equal))
                        ch.mark(ts(tilehot[:, k, 0, :], i48[:], tilef[:, k, col], id1[:, col], ALU.is_equal, ALU.mult))
                        ch.mark(ts(tilehot[:, k, 1, :], i48[:], tilef[:, k, col], gate_k[:, k, col], ALU.is_equal, ALU.mult))
                        ch.settle()
                        v.memset(lst[:, 0:1], 0.0).then_inc(hot_set, 1)

                hots(0, True)
                with dve.Fori(1, TILES) as c:
                    ch.enter(c - 1, 6)
                    hots(c, False)
                    ch.leave(TILES - 1)
                dve.wait_ge(list_prod, 1)
                dve.wait_ge(hot_set, 2 * TILES)
                ch(ts(lst[:], p_ls[:, 0, :], -1.0, None, ALU.add))
                ch(v.tensor_copy(gates[:], p_ls[:, 1, :]))
                ch(ts(pad[:], lst[:], 0.0, None, ALU.max))
                ch(v.tensor_copy(g_idx[:], pad[:]))
                ch(ts(pad[:], lst[:], 0.0, padrow[:, 0:1], ALU.is_lt, ALU.mult))
                ch(tt(pad[:], lst[:], pad[:], ALU.add))
                v.tensor_copy(s_idx[:], pad[:]).then_inc(lists_set, 1)
                dve.wait_ge(lists_set, 1)

                def turn(i, b):
                    dve.wait_ge(x_turned, i + 1)
                    v.tensor_copy(xgt[:, b, 4:8, :], pt_x[1][:, :, :]).then_inc(xt_dve, 1)

                def hidden(i, b, first):
                    dve.wait_ge(silu_set, i + 1)
                    if not first:
                        dve.wait_ge(h_turned, i - 1)
                    v.scalar_tensor_tensor(hh[:, b, :], pg[b][:, 1, :], gates[:, bass.ds(i, 1)], sl[:, b, :], ALU.mult,
                                           ALU.mult).then_inc(h_set, 1)

                def tail(i, b, first):
                    dve.wait_ge(h_turned, i + 1)
                    v.tensor_copy(ht[:, b], pt_h[:, :, :]).then_inc(ht_set, 1)

                def result(i, b, first):
                    dve.wait_ge(d_prod, i + 2)
                    if not first:
                        dve.wait_ge(added, i * 16 - 16)
                    v.tensor_copy(yo[:, b, SUP:D], pd[1][:, :]).then_inc(yo_dve, 1)

                def step(i, b, first, last):
                    hidden(i, b, first)
                    if not (first and b == 0):
                        tail(i - 1, 1 - b, False)
                    if not last:
                        turn(i + 1, 1 - b)
                    if not (first and b == 0):
                        result(i - 1, 1 - b, first)

                turn(0, 0)
                for b in range(2):
                    step(b, b, True, False)
                with dve.Fori(1, NT // 2 - 1) as i:
                    for b in range(2):
                        step(i * 2 + b, b, False, False)
                for b in range(2):
                    step(NT - 2 + b, b, False, b == 1)
                tail(NT - 1, 1, False)
                result(NT - 1, 1, False)

            @block.scalar
            def _(act):
                def turn(i):
                    act.wait_ge(x_turned, i + 1)

                def turn_b(i, b):
                    act.wait_ge(x_turned, i + 1)
                    nc.scalar.copy(xgt[:, b, 0:4, :], pt_x[0][:, :, :]).then_inc(xt_act, 1)

                def step(i, b, first, last):
                    act.wait_ge(gu_prod, i + 1)
                    if not first:
                        act.wait_ge(h_set, i - 1)
                    nc.scalar.activation(sl[:, b, :], pg[b][:, 0, :], ACT.Silu).then_inc(silu_set, 1)
                    if not last:
                        turn_b(i + 1, 1 - b)
                    if not (first and b == 0):
                        result(i - 1, 1 - b, first)

                def result(i, b, first):
                    act.wait_ge(d_prod, i + 2)
                    if not first:
                        act.wait_ge(added, i * 16 - 16)
                    nc.scalar.copy(yo[:, b, 0:SUP], pd[0][:, :]).then_inc(yo_act, 1)

                act.wait_ge(lists_set, 1)
                turn_b(0, 0)
                for b in range(2):
                    step(b, b, True, False)
                with act.Fori(1, NT // 2 - 1) as i:
                    for b in range(2):
                        step(i * 2 + b, b, False, False)
                for b in range(2):
                    step(NT - 2 + b, b, False, b == 1)
                result(NT - 1, 1, False)

            @block.tensor
            def _(pe):
                t = nc.tensor
                pe.sem_inc(d_prod, 1)
                pe.wait_ge(oh_set, 1)
                flat = msk[:].rearrange("p t e -> p (t e)")
                t.matmul(pd[0][:, 0:TILES * E], below[:], flat, start=True, stop=True)
                t.matmul(pd[1][:, 0:TILES * E], ones2[:], flat, start=True, stop=True).then_inc(cnt_prod, 1)

                def place(c, first, last):
                    for k in range(2):
                        pe.wait_ge(hot_set, c * 2 + k + 1)
                        mm = t.matmul(p_ls[:, :, :].rearrange("p a b -> p (a b)"), rowhot[:, k, :],
                                      tilehot[:, k].rearrange("p a b -> p (a b)"), start=(first and k == 0), stop=(last and k == 1))
                        mm.then_inc(hot_used, 1)
                    return mm

                place(0, True, False)
                with pe.Fori(1, TILES - 1) as c:
                    place(c, False, False)
                place(TILES - 1, False, True)
                pe.wait_ge(hot_used, 2 * TILES)
                pe.sem_inc(list_prod, 1)

                def turn(i, b, first):
                    pe.wait_ge(xg_in[b], (i - b) * (16 // GS) + 16)
                    if not first:
                        pe.wait_ge(xt_act, i)
                        pe.wait_ge(xt_dve, i)
                    for k in range(KD):
                        mm = t.transpose(pt_x[k // 4][:, k % 4, :], xg[:, b, k:D:KD], ident[:])
                    mm.then_inc(x_turned, 1)

                def gate_up(i, b, first):
                    expert = pe.value_load(tab[0:1, 1, bass.ds(i, 1)], min_val=1, max_val=E)
                    slot = pe.value_load(tab[0:1, 0, bass.ds(i, 1)], min_val=0, max_val=3)
                    pe.wait_ge(weights_ready, expert)
                    pe.wait_ge(xt_act, i + 1)
                    pe.wait_ge(xt_dve, i + 1)
                    if not first:
                        pe.wait_ge(h_set, i - 1)
                    w = w_slots[:, slot, 0:2 * KD * FF].rearrange("p (m k f) -> p k m f", m=2, k=KD)
                    for k in range(KD):
                        mm = t.matmul(pg[b][:, :, :], xgt[:, b, k, :], w[:, k], start=(k == 0), stop=(k == KD - 1))
                    mm.then_inc(gu_prod, 1)

                def turn_hidden(i, b, first):
                    pe.wait_ge(h_set, i + 1)
                    if not first:
                        pe.wait_ge(ht_set, i)
                    for k in range(2):
                        mm = t.transpose(pt_h[:, k, :], hh[:, b, k:FF:2], ident[:])
                    mm.then_inc(h_turned, 1)

                def down(i, b, first):
                    slot = pe.value_load(tab[0:1, 0, bass.ds(i, 1)], min_val=0, max_val=3)
                    pe.wait_ge(ht_set, i + 1)
                    if not first:
                        pe.wait_ge(yo_act, i)
                        pe.wait_ge(yo_dve, i)
                    w = w_slots[:, slot, 2 * KD * FF:].rearrange("p (k n) -> p k n", k=2)
                    for m in range(2):
                        for k in range(2):
                            mm = t.matmul(pd[m][:, :], ht[:, b, k, :], w[:, k, m * SUP:(m + 1) * SUP], start=(k == 0), stop=(k == 1))
                    mm.then_inc(d_prod, 1)

                def step(i, g, start=False, last=False):
                    b, begun = g % 2, not (start and g == 0)
                    gate_up(i, b, start and g < 2)
                    if begun:
                        turn_hidden(i - 1, 1 - b, start and g < 2)
                    if not last:
                        turn(i + 1, (g + 1) % GS, False)
                    if begun:
                        down(i - 1, 1 - b, start and g < 2)

                pe.wait_ge(te_set, 3)
                turn(0, 0, True)
                for g in range(GS):
                    step(g, g, start=True)
                with pe.Fori(1, NT // GS - 1) as i:
                    for g in range(GS):
                        step(i * GS + g, g)
                for g in range(GS):
                    step(NT - GS + g, g, last=(g == GS - 1))
                turn_hidden(NT - 1, 1, False)
                down(NT - 1, 1, False)

        with phase() as ph:
            pt = Place(nc, base)
            SL = 4
            zi = sb("zi", [P, SL, D], where=pt)
            zo = sb("zo", [P, SL, D], where=pt)
            g2_row, b2_row = sb("g2_row", [P, D], where=pt), sb("b2_row", [P, D], where=pt)
            st = sb("st2", [P, SL, 2, 6], where=pt)
            ag = sb("ag2", [P, SL, 2], where=pt)
            rs = sb("rs2", [P, SL, 2], where=pt)
            nh, spare = sb("nh", [P, 1], where=pt), sb("spare_g", [P, 1], where=pt)
            row_in, nh_set, var_set, rstd_set, out_set, gdch = sems("row2_in nh_set var2_set rstd2_set out_set gdch")
            acc_in = [phase_sem(f"acc_in{i}") for i in range(SL)]
            y_stored = [phase_sem(f"y_stored{i}") for i in range(SL)]
            block = ph.enter_context(nc.Block())

            @block.sync
            def _(sp):
                for dst, name in ((g2_row, "ln2_g"), (b2_row, "ln2_b")):
                    sp.dma_start(dst[:], bass.AP(tensor=a[name].tensor, offset=0, ap=[[0, P], [1, D]])).then_inc(row_in, 16)
                for b in range(SL):
                    sp.dma_start(zi[:, b, :], acc_dram[b * P:(b + 1) * P, :]).then_inc(acc_in[b], 16)
                with sp.Fori(0, CH // SL - 1) as i:
                    for b in range(SL):
                        sp.wait_ge(out_set, i * SL + b + 1)
                        sp.dma_start(zi[:, b, :], acc_dram[bass.ds((i * SL + SL + b) * P, P), :]).then_inc(acc_in[b], 16)
                sp.wait_ge(out_set, CH - SL + 1)
                sp.dma_start(zi[0:NS, 0, :], acc_dram[SEQ:SEQ + NS, :]).then_inc(acc_in[0], 16)

            @block.scalar
            def _(act):
                with act.Fori(0, CH // SL) as i:
                    for b in range(SL):
                        act.wait_ge(out_set, i * SL + b + 1)
                        act.dma_start(o["y_prompt"][0, bass.ds((i * SL + b) * P, P), :], zo[:, b, :]).then_inc(y_stored[b], 16)
                act.wait_ge(out_set, CH + 1)
                act.dma_start(o["y_sample"][:, 0, :], zo[0:NS, 0, :]).then_inc(y_stored[0], 16)
                act.wait_ge(y_stored[0], (CH // SL + 1) * 16)
                for b in range(1, SL):
                    act.wait_ge(y_stored[b], CH // SL * 16)

            @block.gpsimd
            def _(gp):
                gp.memset(nh[:], -0.5).then_inc(nh_set, 1)
                gp.wait_ge(nh_set, 1)
                with gp.Fori(0, CH // SL) as i:
                    for b in range(SL):
                        gp.wait_ge(var_set, i * SL + b + 1)
                        gp.tensor_tensor(rs[:, b, 1:2], rs[:, b, 0:1], nh[:], ALU.pow).then_inc(rstd_set, 1)
                gp.wait_ge(var_set, CH + 1)
                gp.tensor_tensor(rs[0:NS, 0, 1:2], rs[0:NS, 0, 0:1], nh[0:NS], ALU.pow).then_inc(rstd_set, 1)

            @block.vector
            def _(dve):
                v = nc.vector
                ch = Chain(dve, gdch)

                def norm(c, b, turn, n=P):
                    dve.wait_ge(acc_in[b], (turn + 1) * 16)
                    for m in range(2):
                        ch.mark(v.bn_stats(st[0:n, b, m, :], zi[0:n, b, m * SUP:(m + 1) * SUP]))
                    ch.settle()
                    v.memset(spare[:], 0.0)
                    ch(v.bn_aggr(ag[0:n, b, :], st[0:n, b]))
                    v.tensor_scalar(rs[0:n, b, 0:1], ag[0:n, b, 1:2], EPS, None, ALU.add).then_inc(var_set, 1)
                    ch(v.scalar_tensor_tensor(zi[0:n, b, :], zi[0:n, b, :], ag[0:n, b, 0:1], g2_row[0:n, :], ALU.subtract, ALU.mult))
                    dve.wait_ge(rstd_set, c + 1)
                    if not (isinstance(turn, int) and turn == 0):
                        dve.wait_ge(y_stored[b], turn * 16)
                    v.scalar_tensor_tensor(zo[0:n, b, :], zi[0:n, b, :], rs[0:n, b, 1:2], b2_row[0:n, :], ALU.mult,
                                           ALU.add).then_inc(out_set, 1)

                dve.wait_ge(row_in, 32)
                for b in range(SL):
                    norm(b, b, 0)
                with dve.Fori(1, CH // SL) as i:
                    ch.enter(i - 1, 4 * SL)
                    for b in range(SL):
                        norm(i * SL + b, b, i)
                    ch.leave(CH // SL - 1)
                norm(CH, 0, CH // SL, NS)


INS = ["x_prompt", "x_sample", "state_ssm_re", "state_ssm_im", "w_in", "w_out", "ln_v_g", "ln_v_b", "w_s", "b_s",
       "ssm_a_re", "ssm_a_im", "ssm_log_dt", "ssm_b_re", "ssm_b_im", "ssm_c_re", "ssm_c_im", "ssm_d", "w_glu",
       "b_glu", "ln1_g", "ln1_b", "ln2_g", "ln2_b", "w_router", "router_bias", "w_gate", "w_up", "w_down"]
OUTS = [("y_prompt", (1, SEQ, D)), ("y_sample", (NS, 1, D)), ("re_prompt", (1, 1, G, N)), ("im_prompt", (1, 1, G, N)),
        ("re_sample", (1, NS, G, N)), ("im_sample", (1, NS, G, N)), ("v_sample", (1, NS, 1, WA))]


def kernel(**inputs):
    import numpy as np
    from concourse import bacc
    from concourse.bass_utils import run_bass_kernel_spmd

    nc = bacc.Bacc("TRN2", target_bir_lowering=False, num_devices=1)
    arrays = {f"in_{n}": np.ascontiguousarray(inputs[n]) for n in INS}
    a = {n: nc.dram_tensor(f"in_{n}", arrays[f"in_{n}"].shape, F32, kind="ExternalInput").ap() for n in INS}
    o = {n: nc.dram_tensor(f"out_{n}", shape, F32, kind="ExternalOutput").ap() for n, shape in OUTS}
    hybrid_step(nc, a, o)
    r = run_bass_kernel_spmd(nc, [arrays], core_ids=[0])
    return tuple(r.results[0][f"out_{n}"] for n, _ in OUTS)
```

```python
from contextlib import ExitStack, contextmanager

import concourse.bass as bass
from concourse import mybir

P = 128
F32 = mybir.dt.float32
I32 = mybir.dt.int32
F32R = mybir.dt.float32r
HIGH = -4096
PARTS = ((0, 0), (0, 1), (1, 0))
U32 = mybir.dt.uint32
ACT = mybir.ActivationFunctionType
ALU = mybir.AluOpType
AX = mybir.AxisListType.X

D = 1024
KD = D // P
SEQ = 2048
NS = 8
WA = 512
FT = WA // P
HA = 4
G, Q, N = 32, 16, 64
PAIRS = G // 2
L = 16
HALF = L // 2
K = SEQ // L
SUP = 512
NSUP = SEQ // SUP
KS = SUP // L
CH = SEQ // P
E = 16
EG = 4
FF = 256
ALPHA = 2.0 ** 0.25
EPS = 1e-5
TWO_PI_HI, TWO_PI_MID, TWO_PI_LO = 6.28125, 0.0019350051879882812, 3.0199159819e-07
ROUND = 12582912.0
PI_IN = 3.1415925


class Place:

    END = 229344

    def __init__(self, nc, at):
        self.nc, self.at = nc, at

    def __call__(self, name, shape, dt=F32):
        size = 4
        for n in shape[1:]:
            size *= n
        assert self.at + size <= self.END, f"{name} ends at {self.at + size}"
        tensor = self.nc.alloc_sbuf_tensor_at(name, shape, dt, offset=self.at)
        self.at += -(-size // 32) * 32
        return tensor


class Chain:

    def __init__(self, engine, sem):
        self.engine, self.sem, self.n, self.base = engine, sem, 0, None

    def value(self):
        return self.n if self.base is None else self.base + self.n

    def __call__(self, instruction):
        instruction.then_inc(self.sem, 1)
        self.n += 1
        self.engine.wait_ge(self.sem, self.value())

    def mark(self, instruction):
        instruction.then_inc(self.sem, 1)
        self.n += 1

    def settle(self):
        self.engine.wait_ge(self.sem, self.value())

    def enter(self, i, per):
        self.before, self.per = self.n, per
        self.base, self.n = i * per + self.before, 0

    def leave(self, times):
        assert self.n == self.per, f"{self.n} steps an iteration, not {self.per}"
        self.base, self.n = None, self.before + times * self.per


def hybrid_step(nc, a, o):
    ctx = ExitStack()
    with ctx, nc.allow_non_contiguous_dma(reason="small parameters are laid out by state"):
        KB = 1024
        keep = Place(nc, 17408)

        def sb(name, shape, dt=F32, where=keep):
            return where(name, shape, dt)

        held = []

        def phase_sem(name):
            held.append(nc.alloc_semaphore(name))
            return held[-1]

        def sems(names):
            return [phase_sem(n) for n in names.split()]

        @contextmanager
        def phase():
            with ExitStack() as ph:
                yield ph
            nc.clear_and_free_semaphores(held)
            held.clear()
            nc.all_engine_barrier()

        def dram(name, shape, dt=F32):
            return nc.dram_tensor(name, shape, dt).ap()

        u_dram = dram("u_blocks", [WA, L, K])
        us_dram = dram("u_sample", [NS, WA])
        sq_dram = dram("sq_mats", [PAIRS, P, 2, 4 * P])
        k_dram = dram("k_lags", [(L + HALF - 1) * Q, WA])
        x1_dram = dram("x1_rows", [SEQ + NS, D])
        acc_dram = dram("acc_rows", [SEQ + NS + P, D])

        ident = sb("ident", [P, P])
        ya = sb("ya", [P, FT, SEQ])
        p_re, p_im = sb("p_re", [P, L + 1, PAIRS]), sb("p_im", [P, L + 1, PAIRS])
        unit = sb("unit", [P, 2, PAIRS])
        r16 = sb("r16", [P, PAIRS])
        cb_re, cb_im = sb("cb_re", [P, PAIRS, 2, Q]), sb("cb_im", [P, PAIRS, 2, Q])
        k_lag = sb("k_lag", [P, 2, WA])
        xts = sb("xts", [P, KD, NS])
        mixs = sb("mixs", [NS, 2, WA])
        mixs_t = sb("mixs_t", [P, KD, NS])
        us = sb("us", [NS, 2, WA])

        base = keep.at
        pa = Place(nc, base)
        w_xs = sb("w_xs", [P, KD, WA], where=pa)
        xt = sb("xt", [P, KD, SEQ], where=pa)
        pb = Place(nc, base + 80 * KB)
        w_u = sb("w_u", [P, KD, WA], where=pb)
        xin = sb("xin", [P, 4, D], where=pb)
        ust = sb("ust", [P, 4, L, KS], where=pb)
        v_re, v_im = sb("v_re", [P, 4, L, Q], where=pb), sb("v_im", [P, 4, L, Q], where=pb)
        q_mat = sb("q_mat", [P, 2, 2, L, Q], where=pb)
        s_mat = sb("s_mat", [P, 2, 4 * P], where=pb)
        lv_re, lv_im = sb("lv_re", [P, PAIRS, L], where=pb), sb("lv_im", [P, PAIRS, L], where=pb)
        bb_re, bb_im = sb("bb_re", [P, PAIRS, Q], where=pb), sb("bb_im", [P, PAIRS, Q], where=pb)
        braw = sb("braw", [P, 2, PAIRS, Q], where=pb)
        craw = s_mat[:, 0, :].rearrange("p (m t n) -> p m t n", m=2, t=2)
        xsin = q_mat[0:NS].rearrange("p a b d q -> p (a b d q)")
        c_re, c_ni = sb("c_re", [P, PAIRS, Q], where=pb), sb("c_ni", [P, PAIRS, Q], where=pb)
        prm = sb("prm", [P, 3, PAIRS], where=pb)
        tm = sb("tm", [P, 16, PAIRS], where=pb)
        whole = sb("whole", [P, PAIRS], I32, where=pb)
        tv = sb("tv", [P, 4, L * Q], where=pb)
        tq = sb("tq", [P, 4, L * Q], where=pb)
        d_row = sb("d_row", [P, G, Q], where=pb)

        with phase() as ph:
            tp = [ph.enter_context(nc.psum_tensor(f"tp{i}", [P, SUP], F32)) for i in range(2)]
            pxs = [ph.enter_context(nc.psum_tensor(f"pxs{i}", [P, SUP], F32)) for i in range(2)]
            pu = [ph.enter_context(nc.psum_tensor(f"pu{i}", [P, SUP], F32)) for i in range(2)]
            pst = ph.enter_context(nc.psum_tensor("pst", [P, 4 * P], F32))
            pkv = ph.enter_context(nc.psum_tensor("pkv", [P, 2, 2 * Q], F32))
            (id_zero, id_ready, w_v_in, xs_in, prm_in, b_in, c_in, d_in,
             xt_act, xt_dve, xs_prod, u_prod, xs_out, u_out, c_turned, c_copied, st_prod,
             st_out, kv_prod, kv_out, v_ready, q_ready, par3, sin1, lam_ready, cq_ready, ust_ready,
             dch, ach, gch, xsT_prod, xsT_out, k_stored, d_masked, kz, us_prod, us_out) = sems("""id_zero id_ready w_v_in
             xs_in prm_in b_in c_in d_in xt_act xt_dve xs_prod u_prod xs_out
             u_out c_turned c_copied st_prod st_out kv_prod kv_out v_ready q_ready par3 sin1 lam_ready
             cq_ready ust_ready dch ach gch xsT_prod xsT_out k_stored d_masked kz us_prod us_out""")
            w_in_f = [phase_sem(f"w_in_f{i}") for i in range(FT)]
            load_x = [phase_sem(f"x_loaded{i}") for i in range(4)]
            turned = [phase_sem(f"tile_turned{i}") for i in range(4)]
            ust_stored = [phase_sem(f"ust_stored{i}") for i in range(4)]
            q_stored = [phase_sem(f"q_stored{i}") for i in range(2)]
            s_stored = [phase_sem(f"s_stored{i}") for i in range(2)]
            x_rows = a["x_prompt"][0]
            w_in = a["w_in"][0].rearrange("(k p) n -> p k n", p=P)
            block = ph.enter_context(nc.Block())

            @block.sync
            def _(sp):
                for c in range(4):
                    sp.dma_start(xin[:, c, :], x_rows[c * P:(c + 1) * P, :]).then_inc(load_x[c], 16)
                for f in range(FT):
                    for w, at in ((w_xs, 2 * WA), (w_u, 0)):
                        sp.dma_start(w[:, :, f * P:(f + 1) * P], w_in[:, :, at + f * P:at + (f + 1) * P]).then_inc(w_in_f[f], 16)

                def stores(s):
                    for f in range(FT):
                        sp.wait_ge(xs_out, s * FT + f + 1)
                        sp.dma_start(u_dram[f * P:(f + 1) * P, :, bass.ds(s * KS, KS)], ust[:, f]).then_inc(ust_stored[f], 16)
                        sp.wait_ge(st_out, s * 4 + f + 1)
                        sp.dma_start(sq_dram[s * 4 + f, :, 0, :], s_mat[:, f % 2, :]).then_inc(s_stored[f % 2], 16)

                with sp.Fori(0, NSUP - 1) as s:
                    for c in range(4):
                        sp.wait_ge(turned[c], s + 1)
                        sp.dma_start(xin[:, c, :], x_rows[bass.ds((s * 4 + 4 + c) * P, P), :]).then_inc(load_x[c], 16)
                    stores(s)
                stores(NSUP - 1)
                sp.wait_ge(us_out, 2)
                sp.dma_start(us_dram, us[:, 1, :]).then_inc(k_stored, 16)
                sp.wait_ge(kz, 1)
                for h in range(2):
                    sp.dma_start(k_dram[h * P:(h + 1) * P, :], k_lag[:, h, :]).then_inc(k_stored, 16)
                sp.dma_start(k_dram[2 * P:, :], tv[0:(HALF - 1) * Q].rearrange("p a b -> p (a b)")[:, 0:WA]).then_inc(k_stored, 16)
                sp.wait_ge(k_stored, 64)
                sp.wait_ge(w_v_in, 16)
                for f in range(FT):
                    sp.wait_ge(ust_stored[f], NSUP * 16)
                for b in range(2):
                    sp.wait_ge(s_stored[b], PAIRS // 2 * 16)
                    sp.wait_ge(q_stored[b], PAIRS // 2 * 16)

            @block.gpsimd
            def _(gp):
                gp.memset(ident[:], 0.0).then_inc(id_zero, 1)
                gp.wait_ge(id_zero, 1)
                gp.affine_select(out=ident[:], in_=ident[:], compare_op=ALU.not_equal, fill=1.0, base=0,
                                 pattern=[[-1, P]], channel_multiplier=1).then_inc(id_ready, 1)
                gp.dma_start(braw[:, 0], bass.AP(tensor=a["ssm_b_re"].tensor, offset=0,
                             ap=[[Q, P], [2 * N * Q, PAIRS], [1, Q]])).then_inc(b_in, 16)
                gp.dma_start(braw[:, 1], bass.AP(tensor=a["ssm_b_im"].tensor, offset=0,
                             ap=[[Q, P], [2 * N * Q, PAIRS], [1, Q]])).then_inc(b_in, 16)
                gp.dma_start(d_row[:], bass.AP(tensor=a["ssm_d"].tensor, offset=0,
                             ap=[[0, P], [Q, G], [1, Q]])).then_inc(d_in, 16)
                gp.wait_ge(d_in, 16)
                gp.affine_select(out=d_row[:], in_=d_row[:], compare_op=ALU.is_equal, fill=0.0, base=Q - P,
                                 pattern=[[0, G], [-1, Q]], channel_multiplier=1).then_inc(d_masked, 1)
                ch = Chain(gp, gch)
                gp.wait_ge(lam_ready, 1)
                gp.wait_ge(cq_ready, 1)
                lag_re = p_re[:, 1:L + 1, :].rearrange("p d c -> p c d")
                lag_im = p_im[:, 1:L + 1, :].rearrange("p d c -> p c d")

                def q_pair(pair, b):
                    sh = [P, L, Q]
                    lr = lag_re[:, pair, :].unsqueeze(2).broadcast_to(sh)
                    li = lag_im[:, pair, :].unsqueeze(2).broadcast_to(sh)
                    cr = c_re[:, pair, :].unsqueeze(1).broadcast_to(sh)
                    cn = c_ni[:, pair, :].unsqueeze(1).broadcast_to(sh)
                    t = [tq[:, k, :].rearrange("p (d q) -> p d q", q=Q) for k in range(4)]
                    for k, (x, y) in enumerate([(cr, lr), (cn, li), (cn, lr), (cr, li)]):
                        ch.mark(gp.tensor_tensor(t[k], x, y, ALU.mult))
                    ch.settle()
                    gp.tensor_tensor(q_mat[:, b, 0], t[0], t[1], ALU.add).then_inc(q_ready, 1)
                    gp.tensor_tensor(q_mat[:, b, 1], t[2], t[3], ALU.subtract).then_inc(q_ready, 1)

                gp.wait_ge(xsT_prod, 1)
                for b in range(2):
                    q_pair(b, b)
                    gp.wait_ge(q_ready, 2 * (b + 1))
                    gp.dma_start(sq_dram[b, :, 1, :], q_mat[:, b].rearrange("p a d q -> p (a d q)")).then_inc(q_stored[b], 16)
                with gp.Fori(0, PAIRS // 2 - 1) as i:
                    ch.enter(i, 8)
                    for b in range(2):
                        gp.wait_ge(q_stored[b], i * 16 + 16)
                        q_pair(i * 2 + 2 + b, b)
                        gp.wait_ge(q_ready, i * 4 + 4 + 2 * (b + 1))
                        gp.dma_start(sq_dram[i * 2 + 2 + b, :, 1, :], q_mat[:, b].rearrange("p a d q -> p (a d q)")).then_inc(q_stored[b], 16)
                    ch.leave(PAIRS // 2 - 1)

            @block.scalar
            def _(act):
                act.dma_start(prm[:, 0, :], bass.AP(tensor=a["ssm_a_re"].tensor, offset=0,
                              ap=[[1, P], [P, PAIRS]])).then_inc(prm_in, 16)
                act.dma_start(prm[:, 1, :], bass.AP(tensor=a["ssm_a_im"].tensor, offset=0,
                              ap=[[1, P], [P, PAIRS]])).then_inc(prm_in, 16)
                for h in range(2):
                    act.dma_start(prm[h * N:(h + 1) * N, 2, :], bass.AP(tensor=a["ssm_log_dt"].tensor, offset=h,
                                  ap=[[0, N], [2, PAIRS]])).then_inc(prm_in, 16)
                def turned_x(s, c):
                    act.wait_ge(turned[c], s + 1)
                    nc.scalar.copy(xt[:, 0:4, bass.ds(s * SUP + c * P, P)],
                                   tp[0][:, :].rearrange("p (k n) -> p k n", k=4)).then_inc(xt_act, 1)

                def u_tile(s, f):
                    act.wait_ge(u_prod, s * FT + f + 1)
                    nc.scalar.activation(ya[:, f, bass.ds(s * SUP, SUP)], pu[f % 2][:, :],
                                         ACT.Gelu_apprx_tanh).then_inc(u_out, 1)

                for c in range(4):
                    turned_x(0, c)
                for m, name in enumerate(("ssm_c_re", "ssm_c_im")):
                    for t in range(2):
                        for h in range(2):
                            act.dma_start(craw[:, m, t, h * N:(h + 1) * N],
                                          bass.AP(tensor=a[name].tensor, offset=(t * 16 + h) * Q * N,
                                                  ap=[[2 * Q * N, 8], [N, Q], [1, N]])).then_inc(c_in, 16)
                act.dma_start(xsin[:], a["x_sample"][:, 0, :]).then_inc(xs_in, 16)
                act.wait_ge(par3, 2)
                nc.scalar.activation(unit[:, 1, :], tm[:, 6, :], ACT.Sin).then_inc(sin1, 1)
                nc.scalar.activation(unit[:, 0, :], tm[:, 7, :], ACT.Sin).then_inc(sin1, 1)
                act.wait_ge(c_turned, 1)
                pc = pst[:, :].rearrange("p (m c) -> p m c", m=2)
                nc.scalar.copy(c_re[:].rearrange("p a b -> p (a b)"), pc[:, 0, :]).then_inc(c_copied, 1)
                nc.scalar.mul(c_ni[:].rearrange("p a b -> p (a b)"), pc[:, 1, :], -1.0).then_inc(c_copied, 1)
                act.wait_ge(xsT_prod, 1)
                nc.scalar.copy(xts[:], tp[0][:, 0:KD * NS].rearrange("p (k n) -> p k n", n=NS)).then_inc(xsT_out, 1)
                for f in range(2):
                    u_tile(0, f)
                for f in range(2):
                    turned_x(1, f)
                for f in range(2, 4):
                    u_tile(0, f)
                    turned_x(1, f)
                with act.Fori(1, NSUP - 1) as s:
                    for f in range(FT):
                        u_tile(s, f)
                        turned_x(s + 1, f)
                act.wait_ge(us_prod, 2)
                nc.scalar.activation(us[:, 0, :], pu[0][0:NS, :], ACT.Gelu_apprx_tanh).then_inc(us_out, 1)
                for f in range(FT):
                    if f == FT - 1:
                        act.wait_ge(xs_prod, NSUP * FT)
                        act.dma_start(w_xs[:], w_in[:, :, WA:2 * WA]).then_inc(w_v_in, 16)
                    u_tile(NSUP - 1, f)

            @block.vector
            def _(dve):
                v = nc.vector
                ch = Chain(dve, dch)
                T = [tm[:, k, :] for k in range(16)]

                def turned_x(s, c):
                    dve.wait_ge(turned[c], s + 1)
                    v.tensor_copy(xt[:, 4:8, bass.ds(s * SUP + c * P, P)],
                                  tp[1][:, :].rearrange("p (k n) -> p k n", k=4)).then_inc(xt_dve, 1)

                for c in range(4):
                    turned_x(0, c)
                are, aim, dt, ad, ang = prm[:, 0, :], prm[:, 1, :], T[0], T[1], T[5]
                ch(v.memset(cb_re[:], 0.0))
                ch(v.memset(cb_im[:], 0.0))

                def exp(out, x, k, r, whole):
                    ch(v.tensor_scalar(k, x, 1.4426950408889634, ROUND, ALU.mult, ALU.add))
                    ch(v.tensor_scalar(k, k, -ROUND, None, ALU.add))
                    ch(v.tensor_scalar(k, k, -126.0, 127.0, ALU.max, ALU.min))
                    ch(v.scalar_tensor_tensor(r, k, -0.693359375, x, ALU.mult, ALU.add))
                    ch(v.scalar_tensor_tensor(r, k, 2.12194440e-4, r, ALU.mult, ALU.add))
                    ch(v.tensor_scalar(out, r, 1.0 / 5040, None, ALU.mult))
                    for c in (720, 120, 24, 6, 2, 1):
                        ch(v.scalar_tensor_tensor(out, out, 1.0 / c, r, ALU.add, ALU.mult))
                    ch(v.tensor_scalar(k, k, 127.0, None, ALU.add))
                    ch(v.tensor_copy(whole, k))
                    ch(v.tensor_scalar(whole, whole, 23, None, ALU.logical_shift_left))
                    ch(v.scalar_tensor_tensor(out, out, 1.0, whole.bitcast(F32), ALU.add, ALU.mult))

                dve.wait_ge(prm_in, 64)
                exp(dt, prm[:, 2, :], T[8], T[9], whole[:])
                ch(v.tensor_tensor(ad, are, dt, ALU.mult))
                ch(v.tensor_tensor(ang, aim, dt, ALU.mult))
                exp(T[4], ad, T[8], T[9], whole[:])
                ch(v.tensor_tensor(r16[:], T[4], T[4], ALU.mult))
                for _ in range(3):
                    ch(v.tensor_tensor(r16[:], r16[:], r16[:], ALU.mult))
                ch(v.tensor_scalar(T[8], ang, 1.0 / 6.283185307179586, ROUND, ALU.mult, ALU.add))
                ch(v.tensor_scalar(T[8], T[8], -ROUND, None, ALU.add))
                for part in (TWO_PI_HI, TWO_PI_MID, TWO_PI_LO):
                    ch(v.scalar_tensor_tensor(ang, T[8], -part, ang, ALU.mult, ALU.add))
                v.tensor_scalar(T[6], ang, PI_IN, -PI_IN, ALU.min, ALU.max).then_inc(par3, 1)
                dve.wait_ge(par3, 1)
                ch(v.tensor_scalar(T[9], T[6], -1.0, None, ALU.mult))
                ch(v.tensor_tensor(T[9], T[9], T[6], ALU.max))
                v.tensor_scalar(T[7], T[9], -1.0, 1.5707963267948966, ALU.mult, ALU.add).then_inc(par3, 1)
                dve.wait_ge(sin1, 2)
                for part, pw in ((0, p_re), (1, p_im)):
                    ch.mark(v.tensor_tensor(pw[:, 1, :], T[4], unit[:, part, :], ALU.mult))
                ch.mark(v.memset(p_re[:, 0, :], 1.0))
                ch.mark(v.memset(p_im[:, 0, :], 0.0))
                ch.settle()
                have = 1
                while have < L:
                    sh = [P, have, PAIRS]
                    br, bi = (x[:, have, :].unsqueeze(1).broadcast_to(sh) for x in (p_re, p_im))
                    ar, ai = p_re[:, 1:have + 1, :], p_im[:, 1:have + 1, :]
                    t = [tv[:, k, 0:have * PAIRS].rearrange("p (a b) -> p a b", b=PAIRS) for k in range(4)]
                    for k, (x, y) in enumerate([(ar, br), (ai, bi), (ar, bi), (ai, br)]):
                        ch.mark(v.tensor_tensor(t[k], x, y, ALU.mult))
                    ch.settle()
                    ch.mark(v.tensor_tensor(p_re[:, have + 1:2 * have + 1, :], t[0], t[1], ALU.subtract))
                    ch.mark(v.tensor_tensor(p_im[:, have + 1:2 * have + 1, :], t[2], t[3], ALU.add))
                    ch.settle()
                    have *= 2
                for r in range(L):
                    ch.mark(v.tensor_copy(lv_re[:, :, r], p_re[:, L - 1 - r, :]))
                    ch.mark(v.tensor_copy(lv_im[:, :, r], p_im[:, L - 1 - r, :]))
                ch(v.tensor_tensor(T[10], are, are, ALU.mult))
                ch(v.tensor_tensor(T[11], aim, aim, ALU.mult))
                ch(v.tensor_tensor(T[10], T[10], T[11], ALU.add))
                ch(v.reciprocal(T[10], T[10]))
                ch(v.tensor_scalar(T[11], p_re[:, 1, :], -1.0, None, ALU.add))
                nr, ni = T[11], p_im[:, 1, :]
                for k, (x, y) in enumerate([(nr, are), (ni, aim), (ni, are), (nr, aim)]):
                    ch.mark(v.tensor_tensor(T[12 + k], x, y, ALU.mult))
                ch.settle()
                ch(v.tensor_tensor(T[12], T[12], T[13], ALU.add))
                ch(v.tensor_tensor(T[14], T[14], T[15], ALU.subtract))
                ch(v.tensor_tensor(T[12], T[12], T[10], ALU.mult))
                ch(v.tensor_tensor(T[14], T[14], T[10], ALU.mult))
                dve.wait_ge(b_in, 32)
                sh = [P, PAIRS, Q]
                zr, zi = (x.unsqueeze(2).broadcast_to(sh) for x in (T[12], T[14]))
                t = [tv[:, k, :].rearrange("p (a b) -> p a b", b=Q) for k in range(4)]
                for k, (x, y) in enumerate([(zr, braw[:, 0]), (zi, braw[:, 1]), (zr, braw[:, 1]), (zi, braw[:, 0])]):
                    ch.mark(v.tensor_tensor(t[k], x, y, ALU.mult))
                ch.settle()
                ch.mark(v.tensor_tensor(bb_re[:], t[0], t[1], ALU.subtract))
                ch.mark(v.tensor_tensor(bb_im[:], t[2], t[3], ALU.add))
                ch.settle()
                v.memset(tm[:, 2, :], 0.0).then_inc(lam_ready, 1)
                dve.wait_ge(c_copied, 2)
                for src, dst in ((c_re, cb_re), (c_ni, cb_im)):
                    for h in range(2):
                        ch.mark(v.tensor_copy(dst[h * N:(h + 1) * N, :, h, :], src[h * N:(h + 1) * N, :, :]))
                ch.settle()
                v.memset(tm[:, 2, :], 0.0).then_inc(cq_ready, 1)

                def v_pair(pair, b):
                    sh = [P, L, Q]
                    lr, li = (x[:, pair, :].unsqueeze(2).broadcast_to(sh) for x in (lv_re, lv_im))
                    br, bi = (x[:, pair, :].unsqueeze(1).broadcast_to(sh) for x in (bb_re, bb_im))
                    t = [tv[:, k, :].rearrange("p (d q) -> p d q", q=Q) for k in range(4)]
                    for k, (x, y) in enumerate([(lr, br), (li, bi), (lr, bi), (li, br)]):
                        ch.mark(v.tensor_tensor(t[k], x, y, ALU.mult))
                    ch.settle()
                    v.tensor_tensor(v_re[:, b], t[0], t[1], ALU.subtract).then_inc(v_ready, 1)
                    v.tensor_tensor(v_im[:, b], t[2], t[3], ALU.add).then_inc(v_ready, 1)

                def xs_tile(s, f, first):
                    dve.wait_ge(xs_prod, s * FT + f + 1)
                    if not first:
                        dve.wait_ge(ust_stored[f], s * 16)
                    v.tensor_copy(ust[:, f].rearrange("p j k -> p k j"),
                                  pxs[f % 2][:, :].rearrange("p (k j) -> p k j", j=L)).then_inc(xs_out, 1)

                def v_tile(s, f, first):
                    if not first or f:
                        dve.wait_ge(v_ready, s * 8 + 2 * f)
                    v_pair(s * 4 + f, f)

                def results(s, f, first):
                    b = f % 2
                    dve.wait_ge(st_prod, s * 4 + f + 1)
                    if not first or f > 1:
                        dve.wait_ge(s_stored[b], (s * 2 + f // 2) * 16)
                    v.tensor_copy(s_mat[:, b, :], pst[:, :]).then_inc(st_out, 1)
                    dve.wait_ge(kv_prod, s * 4 + f + 1)
                    v.tensor_copy(k_lag[:, :, bass.ds((s * 4 + f) * 2 * Q, 2 * Q)], pkv[:, :, :]).then_inc(kv_out, 1)

                def super_tile(s, last):
                    for f in range(FT):
                        v_tile(s, f, False)
                        xs_tile(s, f, False)
                        if not last:
                            turned_x(s + 1, f)
                        results(s, f, False)

                for f in range(2):
                    xs_tile(0, f, True)
                for f in range(2):
                    turned_x(1, f)
                for f in range(2):
                    v_tile(0, f, True)
                for f in range(2, FT):
                    xs_tile(0, f, True)
                    turned_x(1, f)
                    v_tile(0, f, True)
                    if f == 2:
                        results(0, 0, True)
                        results(0, 1, True)
                results(0, 2, True)
                results(0, 3, True)
                with dve.Fori(1, NSUP - 1) as s:
                    ch.enter(s - 1, 16)
                    super_tile(s, False)
                    ch.leave(NSUP - 2)
                dve.wait_ge(us_prod, 1)
                v.tensor_copy(us[:, 1, :], pxs[0][0:NS, :]).then_inc(us_out, 1)
                super_tile(NSUP - 1, True)
                dve.wait_ge(v_ready, 2 * PAIRS)
                ch(v.memset(tv[:], 0.0))
                dve.wait_ge(d_masked, 1)
                dve.wait_ge(kv_out, PAIRS)
                ch(v.tensor_tensor(k_lag[96:P, 1, :], k_lag[96:P, 1, :],
                                   d_row[96:P].rearrange("p g q -> p (g q)"), ALU.add))
                v.memset(tm[:, 2, :], 0.0).then_inc(kz, 1)

            @block.tensor
            def _(pe):
                t = nc.tensor
                pe.wait_ge(id_ready, 1)

                def turn(s, c, first):
                    pe.wait_ge(load_x[c], s * 16 + 16)
                    for h in range(2):
                        if not first or c:
                            pe.wait_ge((xt_act, xt_dve)[h], s * 4 + c)
                        for k in range(4):
                            kk = 4 * h + k
                            mm = t.transpose(tp[h][:, k * P:(k + 1) * P], xin[:, c, kk * P:(kk + 1) * P], ident[:])
                    mm.then_inc(turned[c], 1)

                def project(s, f, first):
                    if f == 0:
                        pe.wait_ge(xt_act, s * 4 + 4)
                        pe.wait_ge(xt_dve, s * 4 + 4)
                    if first:
                        pe.wait_ge(w_in_f[f], 32)
                    for w, banks, prod, out in ((w_xs, pxs, xs_prod, xs_out), (w_u, pu, u_prod, u_out)):
                        if not first or f > 1:
                            pe.wait_ge(out, s * FT + f - 1)
                        for k in range(KD):
                            mm = t.matmul(banks[f % 2][:, :], w[:, k, f * P:(f + 1) * P],
                                          xt[:, k, bass.ds(s * SUP, SUP)], start=(k == 0), stop=(k == KD - 1))
                        mm.then_inc(prod, 1)

                def pair_mats(s, f, first):
                    pair = s * 4 + f
                    pe.wait_ge(v_ready, s * 8 + 2 * f + 2)
                    if not first or f:
                        pe.wait_ge(st_out, s * 4 + f)
                    for h in range(2):
                        for m, vm in enumerate((v_re, v_im)):
                            win = vm[:, f].rearrange("p d q -> p (d q)")[:, h * P:(h + 1) * P]
                            mm = t.transpose(pst[:, (2 * h + m) * P:(2 * h + m + 1) * P], win, ident[:])
                    mm.then_inc(st_prod, 1)
                    if first and f == 0:
                        pe.wait_ge(cq_ready, 1)
                    if not first or f:
                        pe.wait_ge(kv_out, s * 4 + f)
                    for h in range(2):
                        for m, (vm, cm) in enumerate(((v_re, cb_re), (v_im, cb_im))):
                            win = vm[:, f].rearrange("p d q -> p (d q)")[:, h * P:(h + 1) * P]
                            mm = t.matmul(pkv[:, h, :], win, cm[:, pair].rearrange("p h q -> p (h q)"),
                                          start=(m == 0), stop=(m == 1))
                    mm.then_inc(kv_prod, 1)

                for c in range(4):
                    turn(0, c, True)
                project(0, 0, True)
                project(0, 1, True)
                pe.wait_ge(c_in, 128)
                for m in range(2):
                    for h in range(2):
                        mm = t.transpose(pst[:, (2 * m + h) * P:(2 * m + h + 1) * P], craw[:, m, h, :], ident[:])
                mm.then_inc(c_turned, 1)
                pe.wait_ge(xs_in, 16)
                for k in range(KD):
                    mm = t.transpose(tp[0][:, k * NS:(k + 1) * NS], xsin[:, k * P:(k + 1) * P], ident[0:NS, 0:NS])
                mm.then_inc(xsT_prod, 1)
                pe.wait_ge(xsT_out, 1)
                pe.wait_ge(c_copied, 2)
                turn(1, 0, False)
                turn(1, 1, False)
                project(0, 2, True)
                turn(1, 2, False)
                pair_mats(0, 0, True)
                pair_mats(0, 1, True)
                project(0, 3, True)
                turn(1, 3, False)
                pair_mats(0, 2, True)
                pair_mats(0, 3, True)
                with pe.Fori(1, NSUP - 1) as s:
                    for f in range(FT):
                        project(s, f, False)
                        turn(s + 1, f, False)
                        pair_mats(s, f, False)
                for w, banks, out in ((w_xs, pxs, xs_out), (w_u, pu, u_out)):
                    pe.wait_ge(out, (NSUP - 1) * FT)
                    for k in range(KD):
                        mm = t.matmul(banks[0][0:NS, :], xts[:, k, :], w[:, k, :], start=(k == 0), stop=(k == KD - 1))
                    mm.then_inc(us_prod, 1)
                pe.wait_ge(us_out, 2)
                for f in range(FT):
                    project(NSUP - 1, f, False)
                    pair_mats(NSUP - 1, f, False)

        pc = Place(nc, base + 80 * KB)
        cos_k, sin_k = sb("cos_k", [P, PAIRS, K], where=pc), sb("sin_k", [P, PAIRS, K], where=pc)
        us1 = sb("us1", [P, G, NS], where=Place(nc, Place.END - G * NS * 4))
        toep = sb("toep", [P, L, WA], where=pc)
        PS = 4
        ps_ = Place(nc, base + 32 * KB)
        umat = sb("umat", [P, PS, 2, 2, K + NS], where=ps_)
        sq = sb("sq", [P, PS, 2, 4 * P], where=ps_)
        pair_in = [nc.alloc_semaphore(f"pair_in{i}") for i in range(PS)]

        def u_view(pair, h, g):
            return u_dram[bass.ds((pair * 2 + g) * Q, Q), h * HALF:(h + 1) * HALF, :].rearrange("q j k -> j q k")

        def load(sp, pair, b):
            for h in range(2):
                for g in range(2):
                    sp.dma_start(umat[:, b, h, g, 0:K], u_view(pair, h, g)).then_inc(pair_in[b], 16)
            sp.dma_start(umat[:, b, 1, :, K:K + NS], us1[:, bass.ds(pair * 2, 2), :]).then_inc(pair_in[b], 16)
            sp.dma_start(sq[:, b], sq_dram[pair]).then_inc(pair_in[b], 16)

        with phase() as ph:
            pt = Place(nc, base + 128 * KB)
            wst = sb("wst", [P, HA, P], where=pt)
            bs_row = sb("bs_row", [P, HA, P], where=pt)
            gate_b = bs_row
            ones = sb("ones", [P, P], where=pt)
            g_col, b_col = sb("g_col", [P, HA], where=pt), sb("b_col", [P, HA], where=pt)
            vg = sb("vg", [P, 4, WA], where=pt)
            vn = sb("vn", [P, 4, WA], where=pt)
            wsr = vg[:, 3, :].rearrange("p (h m) -> p h m", h=HA)
            gt = k_lag
            st = sb("st", [P, 4, 6], where=pt)
            spare = sb("spare_b", [P, 1], where=pt)
            ag = sb("ag", [P, 4, 2], where=pt)
            rs = sb("rs", [P, 4, 2], where=pt)
            half_n = sb("half_n", [P, 1], where=pt)
            w16 = sb("w16", [P, 2, 2, PAIRS], where=pt)
            tw = sb("tw", [P, 4, PAIRS], where=pt)
            pl = Place(nc, base + 96 * KB)
            wv_bits = sb("wv_bits", [P, KD, WA], I32, where=Place(nc, pl.at))
            wv = [sb("wv_high", [P, KD, WA], F32R, where=pl), sb("wv_low", [P, KD, WA], F32R, where=Place(nc, base))]
            x_bits = sb("x_bits", [P, KD, P], I32, where=pl)
            x_high, x_low = sb("x_high", [P, 2, KD, P], F32R, where=pl), sb("x_low", [P, KD, SEQ], F32R, where=Place(nc, base + 16 * KB))
            TB = K // 8
            tb = sb("tb", [P, 4, PAIRS, TB], where=pl)
            assert pl.at <= base + 128 * KB
            xs_bits = sb("xs_bits", [P, KD, NS], I32, where=Place(nc, pt.at))
            xs_part = [sb(f"xs_{n}", [P, KD, NS], F32R, where=pt) for n in ("high", "low")]
            gs_row, bs8 = mixs[:, 1, :], sb("bs8", [NS, WA], where=pt)
            w00 = sb("w00", [NS, 2, HA], where=pt)
            vs = sb("vs", [NS, WA], where=pt)
            assert pt.at <= Place.END - G * NS * 4
            pv = [ph.enter_context(nc.psum_tensor(f"pv{i}", [P, WA], F32)) for i in range(2)]
            pg = [ph.enter_context(nc.psum_tensor(f"pg{i}", [P, HA, P], F32)) for i in range(2)]
            pw = ph.enter_context(nc.psum_tensor("pw", [P, HA, P], F32))
            pr = ph.enter_context(nc.psum_tensor("pr", [P, HA, P], F32))
            psv = ph.enter_context(nc.psum_tensor("psv", [NS, WA], F32))
            pmt = ph.enter_context(nc.psum_tensor("pmt", [P, 4 * NS], F32))
            (ws_in, row_in, col_in, smp_in, ones_set, w_turned, w_copied, w_masked, rowsum, gate_b_set, v_prod, v_gelu,
             var_set, rstd_set, v_norm, gate_prod, gated, toep_in, bdch, vs_prod, vs_gelu, vs_var, vs_rstd, vs_set,
             mixa_set, vs_stored, tables_set, us_zero, us_in,
             wv_masked, wv_low, wv_low_dve, wv_high, x_masked, x_low_set, x_high_set, xs_masked, xs_low_set, xs_high_set) = sems("""ws_in row_in col_in smp_in ones_set w_turned w_copied w_masked rowsum
             gate_b_set v_prod v_gelu var_set rstd_set v_norm gate_prod gated toep_in bdch vs_prod vs_gelu vs_var
             vs_rstd vs_set mixa_set vs_stored tables_set us_zero us_in
             wv_masked wv_low wv_low_dve wv_high x_masked x_low_set x_high_set xs_masked xs_low_set xs_high_set""")
            LAG = 3
            block = ph.enter_context(nc.Block())

            @block.sync
            def _(sp):
                sp.dma_start(wsr, a["w_s"][0].rearrange("h l m -> l h m")).then_inc(ws_in, 16)
                sp.dma_start(bs_row[:], bass.AP(tensor=a["b_s"].tensor, offset=0,
                             ap=[[0, P], [P, HA], [1, P]])).then_inc(row_in, 16)
                sp.dma_start(gs_row, bass.AP(tensor=a["ln_v_g"].tensor, offset=0, ap=[[0, NS], [1, WA]])).then_inc(smp_in, 16)
                sp.dma_start(bs8[:], bass.AP(tensor=a["ln_v_b"].tensor, offset=0, ap=[[0, NS], [1, WA]])).then_inc(smp_in, 16)
                sp.dma_start(g_col[:], bass.AP(tensor=a["ln_v_g"].tensor, offset=0, ap=[[1, P], [P, HA]])).then_inc(col_in, 16)
                sp.dma_start(b_col[:], bass.AP(tensor=a["ln_v_b"].tensor, offset=0, ap=[[1, P], [P, HA]])).then_inc(col_in, 16)
                sp.dma_start(w00[:, 0, :], bass.AP(tensor=a["w_s"].tensor, offset=0, ap=[[0, NS], [P * P, HA]])).then_inc(smp_in, 16)
                sp.dma_start(w00[:, 1, :], bass.AP(tensor=a["b_s"].tensor, offset=0, ap=[[0, NS], [P, HA]])).then_inc(smp_in, 16)
                sp.wait_ge(us_zero, 1)
                for n in range(NS):
                    sp.dma_start(us1[P - Q:P, :, n], us_dram[n].rearrange("(g q) -> q g", q=Q)).then_inc(us_in, 16)
                sp.wait_ge(v_prod, CH)
                sp.wait_ge(tables_set, 1)
                for j in range(L):
                    sp.dma_start(toep[:, j, :], k_dram[(L - 1 - j) * Q:(L - 1 - j) * Q + P, :]).then_inc(toep_in, 16)
                sp.wait_ge(us_in, NS * 16)
                for p in range(2):
                    load(sp, p, p)
                sp.wait_ge(vs_set, 1)
                sp.dma_start(o["v_sample"][0, :, 0, :], vs[:]).then_inc(vs_stored, 16)
                sp.wait_ge(vs_stored, 16)
                sp.wait_ge(toep_in, L * 16)

            @block.gpsimd
            def _(gp):
                def x_lows(c):
                    gp.wait_ge(x_masked, c + 1)
                    cols = bass.ds(c * P, P)
                    gp.tensor_tensor(x_low[:, :, cols], xt[:, :, cols], x_bits[:].bitcast(F32),
                                     ALU.subtract).then_inc(x_low_set, 1)

                x_lows(0)
                for k in range(1, KD, 2):
                    gp.wait_ge(wv_masked, k + 1)
                    gp.tensor_tensor(wv[1][:, k, :], w_xs[:, k, :], wv_bits[:, k, :].bitcast(F32), ALU.subtract).then_inc(wv_low, 1)
                x_lows(1)
                gp.wait_ge(xs_masked, 1)
                gp.tensor_tensor(xs_part[1][:], xts[:], xs_bits[:].bitcast(F32), ALU.subtract).then_inc(xs_low_set, 1)
                gp.memset(us1[:], 0.0).then_inc(us_zero, 1)
                gp.memset(ones[:], 1.0).then_inc(ones_set, 1)
                gp.memset(half_n[:], -0.5).then_inc(ones_set, 1)
                x_lows(2)
                gp.wait_ge(w_copied, 1)
                gp.affine_select(out=wst[:], in_=wst[:], compare_op=ALU.is_ge, fill=0.0, base=0,
                                 pattern=[[0, HA], [1, P]], channel_multiplier=-1).then_inc(w_masked, 1)
                gp.wait_ge(ones_set, 2)

                def root(c, b):
                    gp.wait_ge(var_set, c + 1)
                    gp.tensor_tensor(rs[:, b, 1:2], rs[:, b, 0:1], half_n[:], ALU.pow).then_inc(rstd_set, 1)

                root(0, 0)
                x_lows(3)
                root(1, 1)
                x_lows(4)
                root(2, 2)
                root(3, 3)
                with gp.Fori(0, CH // 4 - 2) as i:
                    for b in range(4):
                        x_lows(i * 4 + 5 + b)
                        root(i * 4 + 4 + b, b)
                for b in range(4):
                    if b < 3:
                        x_lows(CH - 3 + b)
                    root(CH - 4 + b, b)
                gp.wait_ge(vs_var, 1)
                gp.tensor_tensor(rs[0:NS, 0, 1:2], rs[0:NS, 0, 0:1], half_n[0:NS], ALU.pow).then_inc(vs_rstd, 1)

            @block.scalar
            def _(act):
                def x_highs(c, b):
                    act.wait_ge(x_masked, c + 1)
                    nc.scalar.copy(x_high[:, b % 2], x_bits[:].bitcast(F32)).then_inc(x_high_set, 1)

                def gelu(c, b, first):
                    act.wait_ge(v_prod, c + 1)
                    if not first:
                        act.wait_ge(v_norm, c - 3)
                    nc.scalar.activation(vg[:, b, :], pv[b % 2][:, :], ACT.Gelu_apprx_tanh).then_inc(v_gelu, 1)

                x_highs(0, 0)
                for k in range(KD):
                    act.wait_ge((wv_low_dve, wv_low)[k % 2], k // 2 + 1)
                    nc.scalar.copy(wv[0][:, k, :], wv_bits[:, k, :].bitcast(F32)).then_inc(wv_high, 1)
                x_highs(1, 1)
                act.wait_ge(xs_low_set, 1)
                nc.scalar.copy(xs_part[0][:], xs_bits[:].bitcast(F32)).then_inc(xs_high_set, 1)
                for b in range(4):
                    gelu(b, b, True)
                    if b == 1:
                        act.wait_ge(w_turned, 1)
                        nc.scalar.copy(wst[:], pw[:, :, :]).then_inc(w_copied, 1)
                    x_highs(b + 2, b)
                with act.Fori(1, CH // 4 - 1) as i:
                    for b in range(4):
                        gelu(i * 4 + b, b, False)
                        x_highs(i * 4 + b + 2, b)
                for b in range(4):
                    gelu(CH - 4 + b, b, False)
                    if b < 2:
                        x_highs(CH - 2 + b, b)
                act.wait_ge(vs_prod, 1)
                nc.scalar.activation(vs[:], psv[:, :], ACT.Gelu_apprx_tanh).then_inc(vs_gelu, 1)

            @block.vector
            def _(dve):
                v = nc.vector
                ch = Chain(dve, bdch)

                def mask(c):
                    if c:
                        dve.wait_ge(x_low_set, c)
                        dve.wait_ge(x_high_set, c)
                    v.tensor_scalar(x_bits[:], xt[:, :, c * P:(c + 1) * P].bitcast(I32), HIGH, None,
                                    ALU.bitwise_and).then_inc(x_masked, 1)

                mask(0)
                for k in range(KD):
                    v.tensor_scalar(wv_bits[:, k, :], w_xs[:, k, :].bitcast(I32), HIGH, None, ALU.bitwise_and).then_inc(wv_masked, 1)
                    if k % 2 == 0:
                        dve.wait_ge(wv_masked, k + 1)
                        v.tensor_tensor(wv[1][:, k, :], w_xs[:, k, :], wv_bits[:, k, :].bitcast(F32), ALU.subtract).then_inc(wv_low_dve, 1)
                mask(1)
                v.tensor_scalar(xs_bits[:], xts[:].bitcast(I32), HIGH, None, ALU.bitwise_and).then_inc(xs_masked, 1)
                def square(xr, xi, yr, yi):
                    ch.mark(v.tensor_tensor(tw[:, 0], xr, xr, ALU.mult))
                    ch.mark(v.tensor_tensor(tw[:, 1], xi, xi, ALU.mult))
                    ch.mark(v.tensor_tensor(tw[:, 2], xr, xi, ALU.mult))
                    ch.settle()
                    ch.mark(v.tensor_tensor(yr, tw[:, 0], tw[:, 1], ALU.subtract))
                    ch.mark(v.tensor_scalar(yi, tw[:, 2], 2.0, None, ALU.mult))
                    ch.settle()
                    unit_length(yr, yi)

                def unit_length(yr, yi):
                    ch.mark(v.tensor_tensor(tw[:, 0], yr, yr, ALU.mult))
                    ch.mark(v.tensor_tensor(tw[:, 1], yi, yi, ALU.mult))
                    ch.settle()
                    ch(v.tensor_tensor(tw[:, 0], tw[:, 0], tw[:, 1], ALU.add))
                    ch(v.tensor_scalar(tw[:, 0], tw[:, 0], -0.5, 1.5, ALU.mult, ALU.add))
                    ch.mark(v.tensor_tensor(yr, yr, tw[:, 0], ALU.mult))
                    ch.mark(v.tensor_tensor(yi, yi, tw[:, 0], ALU.mult))
                    ch.settle()

                def table_step(n, part=0):
                    src = (unit[:, 0, :], unit[:, 1, :]) if n == 0 else (w16[:, n % 2, 0, :], w16[:, n % 2, 1, :])
                    if n >= 4:
                        have, at = 1 << (n - 4), part * TB
                        m = min(have, TB)
                        sh = [P, PAIRS, m]
                        br, bi = (x.unsqueeze(2).broadcast_to(sh) for x in src)
                        t = [tb[:, k, :, 0:m] for k in range(4)]
                        ar, ai = cos_k[:, :, at:at + m], sin_k[:, :, at:at + m]
                        for k, (x, y) in enumerate([(ar, br), (ai, bi), (ar, bi), (ai, br)]):
                            ch.mark(v.tensor_tensor(t[k], x, y, ALU.mult))
                        ch.settle()
                        ch.mark(v.tensor_tensor(cos_k[:, :, have + at:have + at + m], t[0], t[1], ALU.subtract))
                        ch.mark(v.tensor_tensor(sin_k[:, :, have + at:have + at + m], t[2], t[3], ALU.add))
                        ch.settle()
                    if n < STEPS - 1 and (n < 4 or at + m == have):
                        square(*src, w16[:, (n + 1) % 2, 0, :], w16[:, (n + 1) % 2, 1, :])

                STEPS = 4 + K.bit_length() - 1
                ch.mark(v.memset(cos_k[:, :, 0:1], 1.0))
                ch.mark(v.memset(sin_k[:, :, 0:1], 0.0))
                ch.settle()
                table_step(0)
                table_step(1)
                mask(2)
                table_step(2)
                def normalise(src, n, b, var, rstd, ready, out):
                    ch.mark(v.bn_stats(st[0:n, b, :], src))
                    ch.settle()
                    v.memset(spare[:], 0.0)
                    ch(v.bn_aggr(ag[0:n, b, :], st[0:n, b, :]))
                    v.tensor_scalar(rs[0:n, b, 0:1], ag[0:n, b, 1:2], EPS, None, ALU.add).then_inc(var, 1)
                    dve.wait_ge(rstd, ready)
                    return v.tensor_scalar(out, src, ag[0:n, b, 0:1], rs[0:n, b, 1:2], ALU.subtract, ALU.mult)

                def norm_tile(c, b, first=False):
                    dve.wait_ge(v_gelu, c + 1)
                    if not first:
                        dve.wait_ge(gate_prod, c - 3)
                    normalise(vg[:, b, :], P, b, var_set, rstd_set, c + 1, vn[:, b, :]).then_inc(v_norm, 1)

                def gate_tile(c, b):
                    dve.wait_ge(gate_prod, c + 1)
                    for h in range(HA):
                        ch.mark(v.scalar_tensor_tensor(gt[:, b % 2, h * P:(h + 1) * P], pg[b % 2][:, h, :], g_col[:, h:h + 1],
                                                       gate_b[:, h, :], ALU.mult, ALU.add))
                    ch.settle()
                    part = ya[:, :, bass.ds(c * P, P)]
                    v.tensor_tensor(part, gt[:, b % 2, :].rearrange("p (h l) -> p h l", h=HA), part, ALU.mult).then_inc(gated, 1)

                norm_tile(0, 0, True)
                mask(3)
                table_step(3)
                norm_tile(1, 1, True)
                mask(4)
                table_step(4)
                dve.wait_ge(rowsum, 1)
                dve.wait_ge(row_in, 16)
                dve.wait_ge(col_in, 32)
                for h in range(HA):
                    v.scalar_tensor_tensor(gate_b[:, h, :], pr[:, h, :], b_col[:, h:h + 1], bs_row[:, h, :],
                                           ALU.mult, ALU.add).then_inc(gate_b_set, 1)
                dve.wait_ge(gate_b_set, HA)
                norm_tile(2, 2, True)
                table_step(5)
                norm_tile(3, 3, True)
                rest = [(n, part) for n in range(6, STEPS) for part in range(max(1, (1 << (n - 4)) // TB))]
                assert len(rest) <= CH - 4
                for c in range(CH - 4):
                    if c + 5 < CH:
                        mask(c + 5)
                    gate_tile(c, c % 4)
                    if c < len(rest):
                        table_step(*rest[c])
                    norm_tile(c + 4, c % 4)
                v.memset(tw[:, 3], 0.0).then_inc(tables_set, 1)
                dve.wait_ge(vs_gelu, 1)
                dve.wait_ge(smp_in, 64)
                ch(normalise(vs[:], NS, 0, vs_var, vs_rstd, 1, vs[:]))
                ch(v.tensor_tensor(vs[:], vs[:], gs_row, ALU.mult))
                v.tensor_tensor(vs[:], vs[:], bs8[:], ALU.add).then_inc(vs_set, 1)
                dve.wait_ge(vs_set, 1)
                for h in range(HA):
                    ch.mark(v.tensor_scalar(mixs[:, 0, h * P:(h + 1) * P], vs[:, h * P:(h + 1) * P],
                                            w00[:, 0, h:h + 1], w00[:, 1, h:h + 1], ALU.mult, ALU.add))
                ch.settle()
                v.tensor_tensor(mixs[:, 0, :], mixs[:, 0, :], us[:, 0, :], ALU.mult).then_inc(mixa_set, 1)
                for c in range(CH - 4, CH):
                    gate_tile(c, c % 4)
                dve.wait_ge(w_turned, 2)
                v.tensor_copy(mixs_t[:, 0:FT, :], pmt[:, :].rearrange("p (f s) -> p f s", s=NS)).then_inc(mixa_set, 1)

            @block.tensor
            def _(pe):
                t = nc.tensor
                def gate(c):
                    pe.wait_ge(v_norm, c + 1)
                    if c >= 2:
                        pe.wait_ge(gated, c - 1)
                    for h in range(HA):
                        mm = t.matmul(pg[c % 2][:, h, :], vn[:, c % 4, h * P:(h + 1) * P], wst[:, h, :], start=True, stop=True)
                    mm.then_inc(gate_prod, 1)

                for c in range(CH + LAG):
                    if c == 2:
                        pe.wait_ge(ws_in, 16)
                        for h in range(HA):
                            mm = t.transpose(pw[:, h, :], wsr[:, h, :], ident[:])
                        mm.then_inc(w_turned, 1)
                        pe.wait_ge(xs_high_set, 1)
                        for k in range(KD):
                            for x, w in PARTS:
                                mm = t.matmul(psv[:, :], xs_part[x][:, k, :], wv[w][:, k, :], start=(k == 0 and x + w == 0),
                                              stop=(k == KD - 1 and x == 1))
                        mm.then_inc(vs_prod, 1)
                    if c < CH:
                        if c >= 2:
                            pe.wait_ge(v_gelu, c - 1)
                        pe.wait_ge(x_high_set, c + 1)
                        pe.wait_ge(x_low_set, c + 1)
                        for k in range(KD):
                            if c == 0:
                                pe.wait_ge(wv_high, k + 1)
                            for x, w in PARTS:
                                lhs = x_low[:, k, c * P:(c + 1) * P] if x else x_high[:, c % 2, k, :]
                                mm = t.matmul(pv[c % 2][:, :], lhs, wv[w][:, k, :], start=(k == 0 and x + w == 0),
                                              stop=(k == KD - 1 and x == 1))
                        mm.then_inc(v_prod, 1)
                    if c == 2:
                        pe.wait_ge(w_masked, 1)
                        pe.wait_ge(ones_set, 2)
                        t.matmul(pr[:, :, :].rearrange("p h l -> p (h l)"), ones[:], wst[:].rearrange("p h l -> p (h l)"),
                                 start=True, stop=True).then_inc(rowsum, 1)
                    if c >= LAG:
                        gate(c - LAG)
                pe.wait_ge(mixa_set, 1)
                for f in range(FT):
                    mm = t.transpose(pmt[:, f * NS:(f + 1) * NS], mixs[:, 0, f * P:(f + 1) * P], ident[0:NS, 0:NS])
                mm.then_inc(w_turned, 1)


        yb = sb("yb", [P, FT, SEQ], where=Place(nc, base))
        w_out = sb("w_out", [P, KD, D], where=Place(nc, base + 32 * KB))
        w_out_in = nc.alloc_semaphore("w_out_in")
        with phase() as ph:
            ps_ = Place(nc, base + 64 * KB)
            smat = sq[:, :, 0, :].rearrange("p s (h r c) -> p s h r c", h=2, r=2)
            qmat = sq[:, :, 1, :].rearrange("p s (r c) -> p s r c", r=2)
            hst = sb("hst", [P, 2, 2, K + 1], where=ps_)
            pt = Place(nc, base + 128 * KB)
            ytok = sb("ytok", [P, L, 8, Q], where=pt)
            pt.at = base + 144 * KB
            h_rows = sb("h_rows", [NS, 2, G * N], where=Place(nc, base + 128 * KB))
            rot = sb("rot", [P, 8, K], where=pt)
            sg = sb("sg", [P, 2, SUP], where=ps_)
            bus = sb("bus", [P, 2, PAIRS, NS], where=pt)
            h0 = sb("h0", [P, 2, PAIRS, NS], where=ps_)
            ts = sb("ts", [P, 4, PAIRS, NS], where=ps_)
            ys_row = sb("ys_row", [NS, WA], where=ps_)
            assert ps_.at <= base + 80 * KB
            fin = sb("fin", [P, 2, PAIRS], where=pt)
            fin_t = sb("fin_t", [PAIRS, 2, P], where=pt)
            wglu = sb("wglu", [P, FT, Q], where=pt)
            wbd = k_lag[:, 0, :].rearrange("p (f g q) -> p f g q", f=FT, g=8)
            bglu = sb("bglu", [P, FT], where=pt)
            d8 = k_lag[0:NS, 1, :]
            yts = sb("yts", [P, 2, FT, NS], where=pt)
            pst = [ph.enter_context(nc.psum_tensor(f"p_state{i}", [P, 2, P + NS], F32)) for i in range(2)]
            py = [[ph.enter_context(nc.psum_tensor(f"p_y{i}{g}", [P, 2, L, Q], F32)) for g in range(2)] for i in range(2)]
            ptr = [ph.enter_context(nc.psum_tensor(f"p_turn{i}", [P, 4, P], F32)) for i in range(2)]
            pgl = [py[1][g][:].rearrange("p g j q -> p (g j q)") for g in range(2)]
            (wg_in, wg_set, col_in, s_prod, y_prod, w_rot, h_set, bus_set, y_gelu, y_turned, yb_set,
             glu_prod, glu_sig, glu_set, cdch, h0_in, h0_turned, h0_set, hs_set, ys_prod, ys_set, ys_gelu, ys_turned,
             ys_copied, gs_prod, gs_sig, mix_set, st_turned, st_copied, out_stored, fin_set, fin_turned,
             fin_copied, v_zero) = sems("""wg_in wg_set c_col_in s_prod y_prod w_rot h_set bus_set
             y_gelu y_turned yb_set glu_prod glu_sig glu_set cdch h0_in h0_turned h0_set hs_set ys_prod ys_set ys_gelu
             ys_turned ys_copied gs_prod gs_sig mix_set st_turned st_copied out_stored fin_set fin_turned fin_copied
             v_zero""")
            QUADS = PAIRS // 4
            psy = py[0][0][0:NS].rearrange("p g j q -> p (g j q)")
            block = ph.enter_context(nc.Block())

            @block.sync
            def _(sp):
                for p in range(2, PS):
                    load(sp, p, p)
                with sp.Fori(0, PAIRS // PS - 1) as i:
                    for b in range(PS):
                        sp.wait_ge(y_prod, i * PS + b + 1)
                        load(sp, i * PS + PS + b, b)
                sp.wait_ge(y_turned, 4 * QUADS)
                sp.dma_start(h_rows[:, 0, :], a["state_ssm_re"][0].rearrange("s g n -> s (g n)")).then_inc(h0_in, 16)
                sp.dma_start(h_rows[:, 1, :], a["state_ssm_im"][0].rearrange("s g n -> s (g n)")).then_inc(h0_in, 16)
                sp.wait_ge(y_prod, PAIRS)
                sp.dma_start(w_out[:], a["w_out"][0].rearrange("(k p) n -> p k n", p=P)).then_inc(w_out_in, 16)
                sp.wait_ge(fin_copied, 1)
                sp.dma_start(o["re_prompt"][0, 0].rearrange("(c g) n -> c (g n)", g=2), fin_t[:, 0, :]).then_inc(out_stored, 16)
                sp.dma_start(o["im_prompt"][0, 0].rearrange("(c g) n -> c (g n)", g=2), fin_t[:, 1, :]).then_inc(out_stored, 16)
                sp.wait_ge(st_copied, 8)
                sp.dma_start(o["re_sample"][0].rearrange("s g n -> s (g n)"), h_rows[:, 0, :]).then_inc(out_stored, 16)
                sp.dma_start(o["im_sample"][0].rearrange("s g n -> s (g n)"), h_rows[:, 1, :]).then_inc(out_stored, 16)
                sp.wait_ge(out_stored, 64)

            @block.gpsimd
            def _(gp):
                gp.dma_start(wglu[:], bass.AP(tensor=a["w_glu"].tensor, offset=0,
                             ap=[[Q, P], [P * Q, FT], [1, Q]])).then_inc(wg_in, 16)
                gp.dma_start(bglu[:], bass.AP(tensor=a["b_glu"].tensor, offset=0, ap=[[1, P], [P, FT]])).then_inc(col_in, 16)
                gp.dma_start(d8, bass.AP(tensor=a["ssm_d"].tensor, offset=0, ap=[[0, NS], [1, WA]])).then_inc(col_in, 16)
                gp.wait_ge(wg_in, 16)
                gp.tensor_copy(wbd, wglu[:].unsqueeze(2).broadcast_to([P, FT, 8, Q])).then_inc(wg_set, 1)
                gp.wait_ge(wg_set, 1)
                gp.affine_select(out=wbd, in_=wbd, compare_op=ALU.is_ge, fill=0.0, base=0,
                                 pattern=[[0, FT], [-Q, 8], [0, Q]], channel_multiplier=1).then_inc(wg_set, 1)
                gp.wait_ge(wg_set, 2)
                gp.affine_select(out=wbd, in_=wbd, compare_op=ALU.is_ge, fill=0.0, base=Q - 1,
                                 pattern=[[0, FT], [Q, 8], [0, Q]], channel_multiplier=-1).then_inc(wg_set, 1)

            @block.scalar
            def _(act):
                def quad(i):
                    for b in range(4):
                        act.wait_ge(y_prod, i * 4 + b + 1)
                        for g in range(2):
                            nc.scalar.activation(ytok[:, :, 2 * b + g, :], py[b % 2][g][:, 0],
                                                 ACT.Gelu_apprx_tanh).then_inc(y_gelu, 1)
                    for j in range(4):
                        act.wait_ge(y_turned, i * 4 + j + 1)
                        nc.scalar.copy(yb[:, i, :].rearrange("p (k j) -> p j k", j=L)[:, 4 * j:4 * j + 4, :],
                                       ptr[j % 2][:, :, :]).then_inc(yb_set, 1)

                with act.Fori(0, QUADS) as i:
                    quad(i)
                act.wait_ge(col_in, 32)
                for n in range(4 * FT):
                    act.wait_ge(glu_prod, n + 1)
                    if n >= 2:
                        act.wait_ge(glu_set, n - 1)
                    nc.scalar.activation(sg[:, n % 2, :], pgl[n % 2], ACT.Sigmoid, bias=bglu[:, n // 4:n // 4 + 1]).then_inc(glu_sig, 1)
                act.wait_ge(ys_set, 1)
                nc.scalar.activation(mixs[:, 1, :], ys_row[:, 0:WA], ACT.Gelu_apprx_tanh).then_inc(ys_gelu, 1)
                act.wait_ge(ys_turned, 1)
                nc.scalar.copy(yts[:, 0], pst[1][:, 0, 0:FT * NS].rearrange("p (f s) -> p f s", s=NS)).then_inc(ys_copied, 1)
                act.wait_ge(gs_prod, 1)
                for f in range(FT):
                    nc.scalar.activation(yts[:, 1, f, :], pst[1][:, 0, 64 + f * NS:64 + (f + 1) * NS], ACT.Sigmoid,
                                         bias=bglu[:, f:f + 1]).then_inc(gs_sig, 1)

            @block.vector
            def _(dve):
                v = nc.vector
                ch = Chain(dve, cdch)
                for b in range(2):
                    ch.mark(v.memset(hst[:, b, :, 0:1], 0.0))
                ch.settle()

                def scan_pair(pair, b, first):
                    dve.wait_ge(s_prod, pair + 1)
                    c, s = cos_k[:, pair, :], sin_k[:, pair, :]
                    sr, si = pst[b][:, 0, 0:K], pst[b][:, 1, 0:K]
                    t = [rot[:, k, :] for k in range(8)]
                    for k, (x, y) in enumerate([(c, sr), (s, si), (c, si), (s, sr)]):
                        ch.mark(v.tensor_tensor(t[k], x, y, ALU.mult))
                    v.tensor_copy(bus[:, :, pair, :], pst[b][:, :, K:K + NS]).then_inc(bus_set, 1)
                    ch.settle()
                    ch.mark(v.tensor_tensor(t[4], t[0], t[1], ALU.add))
                    v.tensor_tensor(t[5], t[2], t[3], ALU.subtract).then_inc(w_rot, 1)
                    ch.settle()
                    dve.wait_ge(w_rot, pair + 1)
                    decay = r16[:, pair:pair + 1] if isinstance(pair, int) else r16[:, bass.ds(pair, 1)]
                    decay = decay.broadcast_to([P, K])
                    ch.mark(v.tensor_tensor_scan(t[6], decay, t[4], 0.0, ALU.mult, ALU.add))
                    ch.mark(v.tensor_tensor_scan(t[7], decay, t[5], 0.0, ALU.mult, ALU.add))
                    ch.settle()
                    for k, (x, y) in enumerate([(c, t[6]), (s, t[7]), (c, t[7]), (s, t[6])]):
                        ch.mark(v.tensor_tensor(t[k], x, y, ALU.mult))
                    ch.settle()
                    if not first:
                        dve.wait_ge(y_prod, pair - 1)
                    ch.mark(v.tensor_tensor(hst[:, b, 0, 1:K + 1], t[0], t[1], ALU.subtract))
                    v.tensor_tensor(hst[:, b, 1, 1:K + 1], t[2], t[3], ALU.add).then_inc(h_set, 1)
                    ch.settle()
                    dve.wait_ge(h_set, pair + 1)
                    fp = fin[:, :, pair:pair + 1] if isinstance(pair, int) else fin[:, :, bass.ds(pair, 1)]
                    ch(v.tensor_copy(fp, hst[:, b, :, K:K + 1]))

                for b in range(2):
                    scan_pair(b, b, True)
                with dve.Fori(1, PAIRS // 2) as i:
                    ch.enter(i - 1, 26)
                    for b in range(2):
                        scan_pair(i * 2 + b, b, False)
                    ch.leave(PAIRS // 2 - 1)
                v.memset(rot[:, 0, :], 0.0).then_inc(fin_set, 1)
                dve.wait_ge(fin_turned, 1)
                v.tensor_copy(fin_t[:], ptr[0][0:PAIRS, 0:2, :]).then_inc(fin_copied, 1)
                for n in range(4 * FT):
                    dve.wait_ge(glu_sig, n + 1)
                    part = yb[:, n // 4, (n % 4) * SUP:(n % 4 + 1) * SUP]
                    v.tensor_tensor(part, part, sg[:, n % 2, :], ALU.mult).then_inc(glu_set, 1)
                dve.wait_ge(bus_set, PAIRS)
                dve.wait_ge(h0_turned, 1)
                v.tensor_copy(h0[:], ptr[1][:, :, :].rearrange("p a b -> p (a b)")[:, 0:2 * PAIRS * NS]
                              .rearrange("p (r c s) -> p r c s", r=2, c=PAIRS)).then_inc(h0_set, 1)
                dve.wait_ge(h0_set, 1)
                sh = [P, PAIRS, NS]
                lr, li = (x[:, 1, :].unsqueeze(2).broadcast_to(sh) for x in (p_re, p_im))
                for k, (x, y) in enumerate([(lr, h0[:, 0]), (li, h0[:, 1]), (lr, h0[:, 1]), (li, h0[:, 0])]):
                    ch.mark(v.tensor_tensor(ts[:, k], x, y, ALU.mult))
                ch.settle()
                ch.mark(v.tensor_tensor(ts[:, 0], ts[:, 0], ts[:, 1], ALU.subtract))
                ch.mark(v.tensor_tensor(ts[:, 2], ts[:, 2], ts[:, 3], ALU.add))
                ch.settle()
                v.tensor_tensor(h0[:, 0], ts[:, 0], bus[:, 0], ALU.add).then_inc(hs_set, 1)
                v.tensor_tensor(h0[:, 1], ts[:, 2], bus[:, 1], ALU.add).then_inc(hs_set, 1)
                dve.wait_ge(col_in, 32)
                ch(v.tensor_tensor(ys_row[:], d8, us[:, 1, :], ALU.mult))
                dve.wait_ge(ys_prod, 1)
                v.tensor_tensor(ys_row[:], psy[:, :], ys_row[:], ALU.add).then_inc(ys_set, 1)
                for n in range(8):
                    dve.wait_ge(st_turned, n + 1)
                    v.tensor_copy(h_rows[:, n // 4, (n % 4) * 512:(n % 4 + 1) * 512],
                                  ptr[n % 2][0:NS].rearrange("p a b -> p (a b)")).then_inc(st_copied, 1)
                dve.wait_ge(gs_sig, FT)
                v.tensor_tensor(mixs_t[:, FT:KD, :], yts[:, 0], yts[:, 1], ALU.mult).then_inc(mix_set, 1)

            @block.tensor
            def _(pe):
                t = nc.tensor

                def states(pair, slot, first, count):
                    b = slot % 2
                    pe.wait_ge(pair_in[slot], count * 96)
                    if not first:
                        pe.wait_ge(w_rot, pair - 1)
                        pe.wait_ge(bus_set, pair - 1)
                    for r in range(2):
                        for g in range(2):
                            lhs = [smat[:, slot, h, r, g * N:(g + 1) * N] for h in range(2)]
                            dst = pst[b][g * N:(g + 1) * N, r, :]
                            for h in range(2):
                                t.matmul(dst[:, 0:K], lhs[h], umat[:, slot, h, g, 0:K], start=(h == 0), stop=(h == 1))
                            mm = t.matmul(dst[:, K:K + NS], lhs[1], umat[:, slot, 1, g, K:K + NS], start=True, stop=True)
                    mm.then_inc(s_prod, 1)

                def outputs(pair, slot, first):
                    b = slot % 2
                    if not first:
                        pe.wait_ge(y_gelu, pair * 2 - 2)
                    for g in range(2):
                        dst = py[b][g][:, 0]
                        col = (pair * 2 + g) * Q
                        t.matmul(dst, umat[:, slot, 0, g, 0:K], toep[:, :, bass.ds(col, Q)], start=True, stop=False)
                        t.matmul(dst[:, HALF:L, :], umat[:, slot, 1, g, 0:K], toep[:, 0:HALF, bass.ds(col, Q)],
                                 start=False, stop=False)
                    pe.wait_ge(h_set, pair + 1)
                    for r in range(2):
                        for g in range(2):
                            rows = slice(g * N, (g + 1) * N)
                            mm = t.matmul(py[b][g][:, 0].rearrange("p j q -> p (j q)"), hst[rows, b, r, 0:K],
                                          qmat[rows, slot, r, :], start=False, stop=(r == 1))
                    mm.then_inc(y_prod, 1)

                def quad(i, first, last):
                    for b in range(4):
                        if not (last and b == 3):
                            states(i * 4 + b + 1, (b + 1) % PS, first and b == 0, i + (b + 1) // PS + 1)
                        outputs(i * 4 + b, b, first and b < 2)
                    pe.wait_ge(y_gelu, i * 8 + 8)
                    for j in range(L):
                        if j % 4 == 0 and not (first and j < 8):
                            pe.wait_ge(yb_set, i * 4 + j // 4 - 1)
                        mm = t.transpose(ptr[j // 4 % 2][:, j % 4, :], ytok[:, j].rearrange("p g q -> p (g q)"), ident[:])
                        if j % 4 == 3:
                            mm.then_inc(y_turned, 1)

                states(0, 0, True, 1)
                quad(0, True, False)
                with pe.Fori(1, QUADS - 1) as i:
                    quad(i, False, False)
                quad(QUADS - 1, False, True)
                pe.wait_ge(fin_set, 1)
                pe.wait_ge(yb_set, 4 * QUADS)
                for r in range(2):
                    mm = t.transpose(ptr[0][0:PAIRS, r, :], fin[:, r, :], ident[:])
                mm.then_inc(fin_turned, 1)
                pe.wait_ge(wg_set, 3)
                for n in range(4 * FT):
                    if n >= 2:
                        pe.wait_ge(glu_sig, n - 1)
                    f = n // 4
                    t.matmul(pgl[n % 2], wbd[:, f].rearrange("p g q -> p (g q)"), yb[:, f, (n % 4) * SUP:(n % 4 + 1) * SUP],
                             start=True, stop=True).then_inc(glu_prod, 1)
                pe.wait_ge(h0_in, 32)
                flat = ptr[1][:, :, :].rearrange("p a b -> p (a b)")
                for r in range(2):
                    for c in range(PAIRS):
                        mm = t.transpose(flat[:, (r * PAIRS + c) * NS:(r * PAIRS + c + 1) * NS],
                                         h_rows[:, r, c * P:(c + 1) * P], ident[0:NS, 0:NS])
                mm.then_inc(h0_turned, 1)
                pe.wait_ge(hs_set, 2)
                for c in range(PAIRS):
                    dst = psy[:, c * 2 * Q:(c + 1) * 2 * Q]
                    t.matmul(dst, h0[:, 0, c, :], cb_re[:, c].rearrange("p h q -> p (h q)"), start=True, stop=False)
                    mm = t.matmul(dst, h0[:, 1, c, :], cb_im[:, c].rearrange("p h q -> p (h q)"), start=False, stop=True)
                mm.then_inc(ys_prod, 1)
                pe.wait_ge(fin_copied, 1)
                for n in range(8):
                    if n >= 2:
                        pe.wait_ge(st_copied, n - 1)
                    for c in range(4):
                        mm = t.transpose(ptr[n % 2][0:NS, c, :], h0[:, n // 4, (n % 4) * 4 + c, :], ident[:])
                    mm.then_inc(st_turned, 1)
                pe.wait_ge(ys_gelu, 1)
                for f in range(FT):
                    mm = t.transpose(pst[1][:, 0, f * NS:(f + 1) * NS], mixs[:, 1, f * P:(f + 1) * P], ident[0:NS, 0:NS])
                mm.then_inc(ys_turned, 1)
                pe.wait_ge(ys_copied, 1)
                for f in range(FT):
                    mm = t.matmul(pst[1][:, 0, 64 + f * NS:64 + (f + 1) * NS], wbd[:, f].rearrange("p g q -> p (g q)"),
                                  yts[:, 0, f, :], start=True, stop=True)
                mm.then_inc(gs_prod, 1)

        TILES = CH + 1
        late = Place(nc, base + 153 * KB)
        scores = sb("scores", [P, TILES, E], where=late)
        w_slots = sb("w_slots", [P, 4, 3 * KD * FF], where=Place(nc, base + 53 * KB))
        with phase() as ph:
            pt = Place(nc, base + 64 * KB)
            z = sb("z", [P, 2, D], where=pt)
            x1 = sb("x1", [P, 2, D], where=pt)
            ax1 = sb("ax1", [P, 2, D], where=pt)
            x1t = sb("x1t", [P, 2, KD, P], where=pt)
            mix_bits = sb("mix_bits", [P, 2, KD, P], I32, where=Place(nc, pt.at))
            mixt = [sb(f"mixt_{n}", [P, 2, KD, P], F32R, where=pt) for n in ("high", "low")]
            wo_bits = sb("w_out_bits", [P, KD, D], I32, where=Place(nc, pt.at))
            wo = [sb("w_out_high", [P, KD, D], F32R, where=pt), sb("w_out_low", [P, KD, D], F32R, where=Place(nc, base + 32 * KB))]
            g1_row, b1_row = sb("g1_row", [P, D], where=pt), sb("b1_row", [P, D], where=pt)
            w_r = sb("w_r", [P, KD, E], where=pt)
            st = sb("st1", [P, 2, 2, 6], where=pt)
            spare = sb("spare_d", [P, 1], where=pt)
            ag = sb("ag1", [P, 2, 2], where=pt)
            rs = sb("rs1", [P, 2, 2], where=pt)
            neg_half = sb("neg_half", [P, 1], where=pt)
            assert pt.at <= base + 153 * KB, pt.at - base
            po = [[ph.enter_context(nc.psum_tensor(f"p_out{i}{n}", [P, SUP], F32)) for n in range(2)] for i in range(2)]
            ptr = [ph.enter_context(nc.psum_tensor(f"p_x1t{i}", [P, 4, P], F32)) for i in range(2)]
            prt = ph.enter_context(nc.psum_tensor("p_router", [P, E], F32))
            (row_in, half_set, wo_low, wo_low_dve, wo_high, wo_masked, mix_masked, mix_high, mix_low, o_prod, z_set, var_set, rstd_set, x1_set, ax1_set, x1_turned, x1t_act,
             x1t_dve, r_prod, r_set, sc_zero, ddch) = sems("""row1_in half_set wo_low wo_low_dve wo_high wo_masked mix_masked mix_high mix_low o_prod z_set var1_set
             rstd1_set x1_set ax1_set x1_turned x1t_act x1t_dve r_prod r_set sc_zero ddch""")
            z_in = [phase_sem(f"z_in{i}") for i in range(2)]
            x1_stored = [phase_sem(f"x1_stored{i}") for i in range(2)]
            ax1_stored = [phase_sem(f"ax1_stored{i}") for i in range(2)]

            def mixer(c):
                if isinstance(c, int) and c == CH:
                    return mixs_t[:, 0:FT, :], mixs_t[:, FT:KD, :]
                return ya[:, :, bass.ds(c * P, P)], yb[:, :, bass.ds(c * P, P)]

            block = ph.enter_context(nc.Block())

            @block.sync
            def _(sp):
                for b in range(2):
                    sp.dma_start(z[:, b, :], a["x_prompt"][0, b * P:(b + 1) * P, :]).then_inc(z_in[b], 16)
                for dst, name in ((g1_row, "ln1_g"), (b1_row, "ln1_b")):
                    sp.dma_start(dst[:], bass.AP(tensor=a[name].tensor, offset=0, ap=[[0, P], [1, D]])).then_inc(row_in, 16)
                sp.dma_start(w_r[:], a["w_router"].rearrange("(k p) e -> p k e", p=P)).then_inc(row_in, 16)

                def stores(c, b):
                    rows = bass.ds(c * P, P)
                    sp.wait_ge(x1_set, c + 1)
                    sp.dma_start(x1_dram[rows, :], x1[:, b, :]).then_inc(x1_stored[b], 16)
                    sp.wait_ge(ax1_set, c + 1)
                    sp.dma_start(acc_dram[rows, :], ax1[:, b, :]).then_inc(ax1_stored[b], 16)

                with sp.Fori(0, CH // 2 - 1) as i:
                    for b in range(2):
                        sp.wait_ge(x1_set, i * 2 + b + 1)
                        sp.dma_start(z[:, b, :], a["x_prompt"][0, bass.ds((i * 2 + 2 + b) * P, P), :]).then_inc(z_in[b], 16)
                        stores(i * 2 + b, b)
                sp.wait_ge(x1_set, CH - 1)
                sp.dma_start(z[0:NS, 0, :], a["x_sample"][:, 0, :]).then_inc(z_in[0], 16)
                for b in range(2):
                    stores(CH - 2 + b, b)
                sp.wait_ge(x1_set, CH + 1)
                sp.dma_start(x1_dram[SEQ:, :], x1[0:NS, 0, :]).then_inc(x1_stored[0], 16)
                sp.wait_ge(ax1_set, CH + 1)
                sp.dma_start(acc_dram[SEQ:SEQ + NS, :], ax1[0:NS, 0, :]).then_inc(ax1_stored[0], 16)
                sp.dma_start(acc_dram[SEQ + NS:, :], ax1[:, 1, :]).then_inc(ax1_stored[1], 16)
                for s in (x1_stored, ax1_stored):
                    sp.wait_ge(s[0], (CH // 2 + 1) * 16)
                sp.wait_ge(x1_stored[1], CH // 2 * 16)
                sp.wait_ge(ax1_stored[1], (CH // 2 + 1) * 16)

            @block.gpsimd
            def _(gp):
                gp.memset(scores[:], 0.0).then_inc(sc_zero, 1)
                gp.memset(neg_half[:], -0.5).then_inc(half_set, 1)
                gp.wait_ge(half_set, 1)

                def low(c, b, n=P):
                    gp.wait_ge(mix_masked, c * 2 + 2)
                    for h, src in enumerate(mixer(c)):
                        part = slice(h * FT, (h + 1) * FT)
                        gp.tensor_tensor(mixt[1][:, b, part, 0:n], src, mix_bits[:, b, part, 0:n].bitcast(F32),
                                         ALU.subtract).then_inc(mix_low, 1)

                def root(c, b, n=P):
                    gp.wait_ge(var_set, c + 1)
                    gp.tensor_tensor(rs[0:n, b, 1:2], rs[0:n, b, 0:1], neg_half[0:n], ALU.pow).then_inc(rstd_set, 1)

                low(0, 0)
                for k in range(1, KD, 2):
                    gp.wait_ge(wo_masked, k + 1)
                    gp.tensor_tensor(wo[1][:, k, :], w_out[:, k, :], wo_bits[:, k, :].bitcast(F32), ALU.subtract).then_inc(wo_low, 1)
                low(1, 1)
                with gp.Fori(0, CH // 2 - 1) as i:
                    for b in range(2):
                        low(i * 2 + 2 + b, b)
                        root(i * 2 + b, b)
                low(CH, 0, NS)
                for b in range(2):
                    root(CH - 2 + b, b)
                root(CH, 0, NS)

            @block.scalar
            def _(act):
                def high(c, b, n=P):
                    act.wait_ge(mix_low, c * 2 + 2)
                    nc.scalar.copy(mixt[0][:, b, :, 0:n], mix_bits[:, b, :, 0:n].bitcast(F32)).then_inc(mix_high, 1)

                def tile(c, b, half, n=P):
                    act.wait_ge(x1_set, c + 1)
                    if half is not None:
                        act.wait_ge(ax1_stored[b], half * 16)
                    nc.scalar.mul(ax1[0:n, b, :], x1[0:n, b, :], ALPHA).then_inc(ax1_set, 1)
                    act.wait_ge(x1_turned, c + 1)
                    if half is not None:
                        act.wait_ge(r_prod, c - 1)
                    nc.scalar.copy(x1t[:, b, 0:4, 0:n], ptr[0][:, :, 0:n]).then_inc(x1t_act, 1)

                def score(c, n=P):
                    act.wait_ge(r_prod, c + 1)
                    nc.scalar.activation(scores[0:n, c, :], prt[0:n, :], ACT.Sigmoid).then_inc(r_set, 1)

                act.wait_ge(sc_zero, 1)
                high(0, 0)
                for k in range(KD):
                    act.wait_ge((wo_low_dve, wo_low)[k % 2], k // 2 + 1)
                    nc.scalar.copy(wo[0][:, k, :], wo_bits[:, k, :].bitcast(F32)).then_inc(wo_high, 1)
                high(1, 1)
                high(2, 0)
                tile(0, 0, None)
                high(3, 1)
                tile(1, 1, None)
                score(0)
                with act.Fori(1, CH // 2 - 1) as i:
                    for b in range(2):
                        high(i * 2 + 2 + b, b)
                        tile(i * 2 + b, b, i)
                        score(i * 2 + b - 1)
                high(CH, 0, NS)
                for b in range(2):
                    tile(CH - 2 + b, b, CH // 2 - 1)
                    score(CH - 3 + b)
                tile(CH, 0, CH // 2, NS)
                score(CH - 1)
                score(CH, NS)

            @block.vector
            def _(dve):
                v = nc.vector
                ch = Chain(dve, ddch)

                def mask(c, b, first, n=P):
                    if not first:
                        dve.wait_ge(o_prod, c - 1)
                    for h, src in enumerate(mixer(c)):
                        v.tensor_scalar(mix_bits[:, b, h * FT:(h + 1) * FT, 0:n], src.bitcast(I32), HIGH, None,
                                        ALU.bitwise_and).then_inc(mix_masked, 1)

                def norm(c, b, first, half, n=P):
                    dve.wait_ge(z_in[b], (half + 1) * 16)
                    dve.wait_ge(o_prod, c + 1)
                    for m in range(2):
                        cols = slice(m * SUP, (m + 1) * SUP)
                        v.scalar_tensor_tensor(z[0:n, b, cols], z[0:n, b, cols], ALPHA, po[b][m][0:n, :], ALU.mult,
                                               ALU.add).then_inc(z_set, 1)
                    dve.wait_ge(z_set, c * 2 + 2)
                    for m in range(2):
                        ch.mark(v.bn_stats(st[0:n, b, m, :], z[0:n, b, m * SUP:(m + 1) * SUP]))
                    ch.settle()
                    v.memset(spare[:], 0.0)
                    ch(v.bn_aggr(ag[0:n, b, :], st[0:n, b]))
                    v.tensor_scalar(rs[0:n, b, 0:1], ag[0:n, b, 1:2], EPS, None, ALU.add).then_inc(var_set, 1)
                    if not first:
                        dve.wait_ge(x1_stored[b], half * 16)
                        dve.wait_ge(ax1_set, c - 1)
                        dve.wait_ge(x1_turned, c - 1)
                    ch(v.scalar_tensor_tensor(z[0:n, b, :], z[0:n, b, :], ag[0:n, b, 0:1], g1_row[0:n, :], ALU.subtract, ALU.mult))
                    dve.wait_ge(rstd_set, c + 1)
                    v.scalar_tensor_tensor(x1[0:n, b, :], z[0:n, b, :], rs[0:n, b, 1:2], b1_row[0:n, :], ALU.mult,
                                           ALU.add).then_inc(x1_set, 1)

                def turn(c, b, first=False, n=P):
                    dve.wait_ge(x1_turned, c + 1)
                    if not first:
                        dve.wait_ge(r_prod, c - 1)
                    v.tensor_copy(x1t[:, b, 4:8, 0:n], ptr[1][:, :, 0:n]).then_inc(x1t_dve, 1)

                mask(0, 0, True)
                dve.wait_ge(w_out_in, 16)
                for k in range(KD):
                    v.tensor_scalar(wo_bits[:, k, :], w_out[:, k, :].bitcast(I32), HIGH, None,
                                    ALU.bitwise_and).then_inc(wo_masked, 1)
                    if k % 2 == 0:
                        dve.wait_ge(wo_masked, k + 1)
                        v.tensor_tensor(wo[1][:, k, :], w_out[:, k, :], wo_bits[:, k, :].bitcast(F32), ALU.subtract).then_inc(wo_low_dve, 1)
                mask(1, 1, True)
                dve.wait_ge(row_in, 48)
                for b in range(2):
                    mask(2 + b, b, False)
                    norm(b, b, True, 0)
                    if b:
                        turn(0, 0, True)
                for b in range(2):
                    mask(4 + b, b, False)
                    norm(2 + b, b, False, 1)
                    turn(1 + b, 1 - b, b == 0)
                with dve.Fori(2, CH // 2 - 1) as i:
                    ch.enter(i - 2, 8)
                    for b in range(2):
                        mask(i * 2 + 2 + b, b, False)
                        norm(i * 2 + b, b, False, i)
                        turn(i * 2 + b - 1, (b + 1) % 2)
                    ch.leave(CH // 2 - 3)
                mask(CH, 0, False, NS)
                for b in range(2):
                    norm(CH - 2 + b, b, False, CH // 2 - 1)
                    turn(CH - 3 + b, (b + 1) % 2)
                norm(CH, 0, False, CH // 2, NS)
                turn(CH - 1, 1)
                turn(CH, 0, False, NS)

            @block.tensor
            def _(pe):
                t = nc.tensor

                def out(c, b, first, start=False, n=P):
                    pe.wait_ge(mix_high, c + 1)
                    if not first:
                        pe.wait_ge(z_set, c * 2 - 2)
                    for m in range(2):
                        for k in range(KD):
                            if start and m == 0:
                                pe.wait_ge(wo_high, k + 1)
                            for x, w in PARTS:
                                mm = t.matmul(po[b][m][0:n, :], mixt[x][:, b, k, 0:n], wo[w][:, k, m * SUP:(m + 1) * SUP],
                                              start=(k == 0 and x + w == 0), stop=(k == KD - 1 and x == 1))
                    mm.then_inc(o_prod, 1)

                def turn(c, b, first, n=P):
                    pe.wait_ge(x1_set, c + 1)
                    if not first:
                        pe.wait_ge(x1t_act, c)
                        pe.wait_ge(x1t_dve, c)
                    for k in range(KD):
                        mm = t.transpose(ptr[k // 4][:, k % 4, 0:n], x1[0:n, b, k * P:(k + 1) * P], ident[0:n, 0:n])
                    mm.then_inc(x1_turned, 1)

                def router(c, b, first, n=P):
                    pe.wait_ge(x1t_act, c + 1)
                    pe.wait_ge(x1t_dve, c + 1)
                    if not first:
                        pe.wait_ge(r_set, c)
                    for k in range(KD):
                        mm = t.matmul(prt[0:n, :], x1t[:, b, k, 0:n], w_r[:, k, :], start=(k == 0), stop=(k == KD - 1))
                    mm.then_inc(r_prod, 1)

                pe.wait_ge(row_in, 48)
                out(0, 0, True, True)
                out(1, 1, True)
                turn(0, 0, True)
                out(2, 0, False)
                turn(1, 1, False)
                router(0, 0, True)
                out(3, 1, False)
                turn(2, 0, False)
                router(1, 1, False)
                with pe.Fori(2, CH // 2) as i:
                    for b in range(2):
                        out(i * 2 + b, b, False)
                        turn(i * 2 + b - 1, (b + 1) % 2, False)
                        router(i * 2 + b - 2, b, False)
                out(CH, 0, False, n=NS)
                turn(CH - 1, 1, False)
                router(CH - 2, 0, False)
                turn(CH, 0, False, NS)
                router(CH - 1, 1, False)
                router(CH, 0, False, NS)

        ROWS = SEQ + NS
        NT = (2 * ROWS + E * (P - 1)) // P
        GS = 4
        NT += -NT % GS
        BIG = 1e30
        with phase() as ph:
            pt = Place(nc, base)
            def tmp(name, shape, dt=F32):
                return sb(name, shape, dt, where=pt)

            bi, m1, oh1, oh2, msk, tot, pos, bas = (tmp(n, [P, TILES, E]) for n in
                                                    ("bi", "m1", "oh1", "oh2", "msk", "tot", "pos", "bas"))
            tot_e, inc_e, reset = (tmp(n, [P, E, TILES]) for n in ("tot_e", "inc_e", "reset"))
            pairs6 = tmp("pairs6", [P, TILES * EG, 6])
            gs, gq = tmp("gs", [P, TILES, EG]), tmp("gq", [P, TILES, EG])
            red, s1, s2, den, gw1, gw2 = (tmp(n, [P, TILES]) for n in ("red", "s1", "s2", "den", "gw1", "gw2"))
            rowf, tilef, gate_k = (tmp(n, [P, 2, TILES]) for n in ("rowf", "tilef", "gate_k"))
            posi, posj = tmp("posi", [P, TILES], I32), tmp("posj", [P, TILES], I32)
            w4, w16_, i48, i128 = tmp("w4", [P, EG]), tmp("w16r", [P, E]), tmp("i48", [P, NT]), tmp("i128", [P, P])
            thr, id1, valid, padrow = tmp("thr", [P, TILES]), tmp("id1", [P, TILES]), tmp("valid", [P, TILES]), tmp("padrow", [P, 1])
            below, ones2 = tmp("below", [P, P]), tmp("ones2", [P, P])
            rb = tmp("rb", [P, E])
            nt, te, ones_e = tmp("nt", [P, E]), tmp("te", [P, E]), tmp("ones_e", [P, E])
            cmp_, tix, tfl, tsl = tmp("cmp", [P, NT, E]), tmp("tix", [P, NT]), tmp("tfl", [P, NT]), tmp("tsl", [P, NT])
            lst, pad = tmp("lst", [P, NT]), tmp("pad", [P, NT])
            tilehot = tmp("tilehot", [P, 2, TILES, 2, NT])
            assert pt.at <= base + 35 * KB, pt.at - base
            rowhot = sb("rowhot", [P, 2, TILES, P], where=Place(nc, base + 35 * KB))
            gates = sb("gates", [P, NT], where=late)
            g_idx, s_idx = sb("g_idx", [P, NT], U32, where=late), sb("s_idx", [P, NT], U32, where=late)
            tab = sb("tab", [P, 2, NT], I32, where=late)
            tab_e = sb("tab_e", [P, E], I32, where=late)
            spare, nothing = sb("spare_e", [P, 1], where=late), sb("nothing", [P, 1], where=late)
            gi, si = sb("gi", [P, GS], U32, where=late), sb("si", [P, 2], U32, where=late)
            pt = Place(nc, base)
            xgt = sb("xgt", [P, 2, KD, P], where=pt)
            yo = sb("yo", [P, 2, D], where=pt)
            sl = sb("sl", [P, 2, FF], where=pt)
            hh = sb("hh", [P, 2, FF], where=pt)
            ht = sb("ht", [P, 2, 2, P], where=pt)
            pt = Place(nc, base + 35 * KB)
            xg = sb("xg", [P, GS, D], where=pt)
            assert pt.at <= base + 53 * KB
            pg = [ph.enter_context(nc.psum_tensor(f"p_gu{i}", [P, 2, FF], F32)) for i in range(2)]
            pt_x = [ph.enter_context(nc.psum_tensor(f"p_xt{i}", [P, 4, P], F32)) for i in range(2)]
            pt_h = ph.enter_context(nc.psum_tensor("p_ht", [P, 2, P], F32))
            pd = [ph.enter_context(nc.psum_tensor(f"p_d{i}", [P, SUP], F32)) for i in range(2)]
            p_ls = ph.enter_context(nc.psum_tensor("p_list", [P, 2, NT], F32))
            (nothing_set, consts, rb_in, oh_set, cnt_prod, tables_set, hot_set, list_prod, lists_set, w_dma, weights_ready,
             edch, gi_set, si_set, x_turned, xt_act, xt_dve, gu_prod, silu_set, h_set, h_turned, ht_set, d_prod, yo_act,
             yo_dve, added, te_set) = sems("""nothing_set consts rb_in oh_set cnt_prod tables_set2 hot_set list_prod
             lists_set w_dma weights_ready edch gi_set si_set xg_turned xg_act xg_dve gu_prod silu_set hh_set h_turned
             ht_set d_prod yo_act yo_dve added te_set""")
            xg_in = [phase_sem(f"xg_in{i}") for i in range(GS)]
            block = ph.enter_context(nc.Block())

            @block.sync
            def _(sp):
                def load(e, slot):
                    for n, (name, at) in enumerate((("w_gate", 0), ("w_up", KD * FF), ("w_down", 2 * KD * FF))):
                        sp.dma_start(w_slots[:, slot, at:at + KD * FF],
                                     a[name][0, e].rearrange("(p k) f -> p (k f)", p=P)).then_inc(w_dma, 16)

                for e in range(4):
                    load(e, 3 - e)
                sp.wait_ge(w_dma, 4 * 48)
                sp.sem_inc(weights_ready, 4)
                sp.wait_ge(te_set, 1)
                with sp.Fori(1, E // 4) as i:
                    for b in range(4):
                        free = sp.value_load(tab_e[0:1, bass.ds(i * 4 + b - 4, 1)], min_val=1, max_val=NT + 1)
                        sp.wait_ge(d_prod, free)
                        load(i * 4 + b, 3 - b)
                        sp.wait_ge(w_dma, (i * 4 + b + 1) * 48)
                        sp.sem_inc(weights_ready, 1)

            @block.gpsimd
            def _(gp):
                io = dict(allow_small_or_imprecise_dtypes=True)
                gp.dma_start(rb[:], bass.AP(tensor=a["router_bias"].tensor, offset=0, ap=[[0, P], [1, E]])).then_inc(rb_in, 16)
                gp.iota(w4[:], [[-1, EG]], base=EG, channel_multiplier=0, **io).then_inc(consts, 1)
                gp.iota(w16_[:], [[-1, E]], base=E, channel_multiplier=0, **io).then_inc(consts, 1)
                gp.iota(i48[:], [[1, NT]], base=0, channel_multiplier=0, **io).then_inc(consts, 1)
                gp.iota(i128[:], [[1, P]], base=0, channel_multiplier=0, **io).then_inc(consts, 1)
                gp.iota(thr[:], [[P, TILES]], base=0, channel_multiplier=0, **io).then_inc(consts, 1)
                gp.iota(id1[:], [[P, TILES]], base=1, channel_multiplier=1, **io).then_inc(consts, 1)
                gp.iota(padrow[:], [[0, 1]], base=ROWS + 1, channel_multiplier=1, **io).then_inc(consts, 1)
                gp.memset(valid[:], 1.0).then_inc(consts, 1)
                gp.memset(ones2[:], 1.0).then_inc(consts, 1)
                gp.memset(ones_e[:], 1.0).then_inc(consts, 1)
                gp.memset(reset[:], 1.0).then_inc(consts, 1)
                gp.wait_ge(consts, 11)
                gp.memset(nothing[:], 0.0).then_inc(nothing_set, 1)
                gp.wait_ge(nothing_set, 1)
                gp.memset(reset[:, :, 0:1], 0.0).then_inc(consts, 1)
                gp.affine_select(out=valid[:, CH:CH + 1], in_=valid[:, CH:CH + 1], compare_op=ALU.is_ge, fill=0.0,
                                 base=NS - 1, pattern=[[0, 1]], channel_multiplier=-1).then_inc(consts, 1)
                gp.affine_select(out=below[:], in_=ones2[:], compare_op=ALU.is_gt, fill=0.0, base=0,
                                 pattern=[[1, P]], channel_multiplier=-1).then_inc(consts, 1)


                def gather(i, b, first):
                    if not first:
                        gp.wait_ge(xg_in[b], (i - b) * (16 // GS))
                        gp.wait_ge(x_turned, i - GS + 1)
                    gp.tensor_copy(gi[:, b:b + 1], g_idx[:, bass.ds(i, 1)]).then_inc(gi_set, 1)
                    gp.wait_ge(gi_set, i + 1)
                    gp.tensor_tensor(spare[:], nothing[:], nothing[:], ALU.add)
                    gp.indirect_dma_start(xg[:, b, :], None, x1_dram,
                                          bass.IndirectOffsetOnAxis(ap=gi[:, b:b + 1], axis=0)).then_inc(xg_in[b], 16)

                def add(i, b, first):
                    if not first:
                        gp.wait_ge(added, i * 16)
                    gp.tensor_copy(si[:, b:b + 1], s_idx[:, bass.ds(i, 1)]).then_inc(si_set, 1)
                    gp.wait_ge(si_set, i + 1)
                    gp.wait_ge(yo_act, i + 1)
                    gp.wait_ge(yo_dve, i + 1)
                    gp.tensor_tensor(spare[:], nothing[:], nothing[:], ALU.add)
                    gp.indirect_dma_start(acc_dram, bass.IndirectOffsetOnAxis(ap=si[:, b:b + 1], axis=0),
                                          yo[:, b, :], None, compute_op=ALU.add).then_inc(added, 16)

                gp.wait_ge(lists_set, 1)
                for b in range(GS):
                    gather(b, b, True)
                for b in range(GS):
                    gather(GS + b, b, False)
                    add(b, b % 2, b == 0)
                with gp.Fori(1, NT // GS - 1) as i:
                    for b in range(GS):
                        gather(i * GS + GS + b, b, False)
                        add(i * GS + b, b % 2, False)
                for b in range(GS):
                    add(NT - GS + b, b % 2, False)
                gp.wait_ge(added, NT * 16)

            @block.vector
            def _(dve):
                v = nc.vector
                ch = Chain(dve, edch)
                tt, ts, stt, rd = v.tensor_tensor, v.tensor_scalar, v.scalar_tensor_tensor, v.tensor_reduce
                dve.wait_ge(consts, 14)
                dve.wait_ge(rb_in, 16)
                full = [P, TILES, E]
                ch(tt(bi[:], scores[:], rb[:].unsqueeze(1).broadcast_to(full), ALU.add))
                q4 = bi[:].rearrange("p t (g e) -> p (t g) e", e=EG)
                ch.mark(tt(pairs6[:, :, 0:3], q4[:, :, 0:3], q4[:, :, 1:4], ALU.add))
                ch.mark(tt(pairs6[:, :, 3:5], q4[:, :, 0:2], q4[:, :, 2:4], ALU.add))
                ch.mark(tt(pairs6[:, :, 5:6], q4[:, :, 0:1], q4[:, :, 3:4], ALU.add))
                ch.settle()
                ch(rd(gs[:].rearrange("p t g -> p (t g)"), pairs6[:], axis=AX, op=ALU.max))

                def first_max(x, weight, out, n):
                    sh = [P, TILES, n]
                    ch(rd(red[:], x, axis=AX, op=ALU.max))
                    ch(tt(out, x, red[:].unsqueeze(2).broadcast_to(sh), ALU.is_equal))
                    ch(tt(out, out, weight[:].unsqueeze(1).broadcast_to(sh), ALU.mult))
                    ch(rd(red[:], out, axis=AX, op=ALU.max))
                    ch(tt(out, out, red[:].unsqueeze(2).broadcast_to(sh), ALU.is_equal))

                first_max(gs[:], w4, gq[:], EG)
                by_group = [P, TILES, EG, E // EG]
                m4, b4 = (x[:].rearrange("p t (g e) -> p t g e", e=EG) for x in (m1, bi))
                ch(tt(m4, b4, gq[:].unsqueeze(3).broadcast_to(by_group), ALU.mult))
                ch(ts(gq[:], gq[:], BIG, -BIG, ALU.mult, ALU.add))
                ch(tt(m4, m4, gq[:].unsqueeze(3).broadcast_to(by_group), ALU.add))
                first_max(m1[:], w16_, oh1[:], E)
                ch(stt(m1[:], oh1[:], -2 * BIG, m1[:], ALU.mult, ALU.add))
                first_max(m1[:], w16_, oh2[:], E)
                vb = valid[:].unsqueeze(2).broadcast_to(full)
                for oh, s in ((oh1, s1), (oh2, s2)):
                    ch(tt(oh[:], oh[:], vb, ALU.mult))
                    ch(tt(msk[:], oh[:], scores[:], ALU.mult))
                    ch(rd(s[:], msk[:], axis=AX, op=ALU.add))
                ch(tt(den[:], s1[:], s2[:], ALU.add))
                ch(tt(den[:], den[:], valid[:], ALU.subtract))
                ch(ts(den[:], den[:], 1.0, None, ALU.add))
                ch(v.reciprocal(den[:], den[:]))
                ch(tt(gate_k[:, 0, :], s1[:], den[:], ALU.mult))
                ch(tt(gate_k[:, 1, :], s2[:], den[:], ALU.mult))
                tt(msk[:], oh1[:], oh2[:], ALU.add).then_inc(oh_set, 1)
                dve.wait_ge(cnt_prod, 1)
                cnt = pd[1][:, 0:TILES * E].rearrange("p (t e) -> p t e", e=E)
                pre = pd[0][:, 0:TILES * E].rearrange("p (t e) -> p t e", e=E)
                ch(v.tensor_copy(tot_e[:].rearrange("p e t -> p t e"), cnt))
                flat = "p e t -> p (e t)"
                ch(v.tensor_tensor_scan(inc_e[:].rearrange(flat), reset[:].rearrange(flat), tot_e[:].rearrange(flat), 0.0,
                                        ALU.mult, ALU.add))
                by_e = [P, E, TILES]
                ch(tt(reset[:], inc_e[:, :, TILES - 1:TILES].broadcast_to(by_e), thr[:].unsqueeze(1).broadcast_to(by_e), ALU.is_gt))
                ch(rd(nt[:], reset[:], axis=AX, op=ALU.add))
                ch(v.tensor_tensor_scan(te[:], ones_e[:], nt[:], 0.0, ALU.mult, ALU.add))
                ts(tab_e[:], te[:], 1.0, None, ALU.add).then_inc(te_set, 1)
                ch(tt(nt[:], te[:], nt[:], ALU.subtract))
                ch(tt(inc_e[:], inc_e[:], tot_e[:], ALU.subtract))
                ch(stt(inc_e[:], nt[:].unsqueeze(2).broadcast_to(by_e), float(P), inc_e[:], ALU.mult, ALU.add))
                ch(tt(pos[:], pre, inc_e[:].rearrange("p e t -> p t e"), ALU.add))
                for k, oh in enumerate((oh1, oh2)):
                    ch(tt(m1[:], oh[:], pos[:], ALU.mult))
                    ch(rd(red[:], m1[:], axis=AX, op=ALU.add))
                    ch(v.tensor_copy(posi[:], red[:]))
                    ch(ts(posj[:], posi[:], P - 1, None, ALU.bitwise_and))
                    ch(v.tensor_copy(rowf[:, k, :], posj[:]))
                    ch(ts(posj[:], posi[:], 7, None, ALU.logical_shift_right))
                    ch(v.tensor_copy(tilef[:, k, :], posj[:]))
                    ch(tt(gate_k[:, k, :], gate_k[:, k, :], valid[:], ALU.mult))
                ch(tt(id1[:], id1[:], valid[:], ALU.mult))
                by_t = [P, NT, E]
                ch(tt(cmp_[:], te[:].unsqueeze(1).broadcast_to(by_t), i48[:].unsqueeze(2).broadcast_to(by_t), ALU.is_le))
                ch(rd(tix[:], cmp_[:], axis=AX, op=ALU.add))
                ch(ts(tix[:], tix[:], float(E - 1), None, ALU.min))
                ch(ts(tfl[:], tix[:], 4.0, None, ALU.is_ge))
                for j in (8.0, 12.0):
                    ch(stt(tfl[:], tix[:], j, tfl[:], ALU.is_ge, ALU.add))
                ch(stt(tsl[:], tfl[:], 4.0, tix[:], ALU.mult, ALU.subtract))
                ch(ts(tsl[:], tsl[:], 3.0, None, ALU.add))
                v.tensor_copy(tab[:, 0, :], tsl[:]).then_inc(te_set, 1)
                ts(tab[:, 1, :], tix[:], 1.0, None, ALU.add).then_inc(te_set, 1)

                for k in range(2):
                    sh, st_ = [P, TILES, P], [P, TILES, NT]
                    ch.mark(tt(rowhot[:, k], i128[:].unsqueeze(1).broadcast_to(sh), rowf[:, k, :].unsqueeze(2).broadcast_to(sh),
                               ALU.is_equal))
                    hot = tilehot[:, k, :, 0, :]
                    ch(tt(hot, i48[:].unsqueeze(1).broadcast_to(st_), tilef[:, k, :].unsqueeze(2).broadcast_to(st_), ALU.is_equal))
                    ch(tt(tilehot[:, k, :, 1, :], hot, gate_k[:, k, :].unsqueeze(2).broadcast_to(st_), ALU.mult))
                    ch.settle()
                    tt(hot, hot, id1[:].unsqueeze(2).broadcast_to(st_), ALU.mult).then_inc(hot_set, 1)
                dve.wait_ge(list_prod, 1)
                ch(ts(lst[:], p_ls[:, 0, :], -1.0, None, ALU.add))
                ch(v.tensor_copy(gates[:], p_ls[:, 1, :]))
                ch(ts(pad[:], lst[:], 0.0, None, ALU.max))
                ch(v.tensor_copy(g_idx[:], pad[:]))
                ch(ts(pad[:], lst[:], 0.0, padrow[:, 0:1], ALU.is_lt, ALU.mult))
                ch(tt(pad[:], lst[:], pad[:], ALU.add))
                v.tensor_copy(s_idx[:], pad[:]).then_inc(lists_set, 1)
                dve.wait_ge(lists_set, 1)

                def turn(i, b):
                    dve.wait_ge(x_turned, i + 1)
                    v.tensor_copy(xgt[:, b, 4:8, :], pt_x[1][:, :, :]).then_inc(xt_dve, 1)

                def hidden(i, b, first):
                    dve.wait_ge(silu_set, i + 1)
                    if not first:
                        dve.wait_ge(h_turned, i - 1)
                    v.scalar_tensor_tensor(hh[:, b, :], pg[b][:, 1, :], gates[:, bass.ds(i, 1)], sl[:, b, :], ALU.mult,
                                           ALU.mult).then_inc(h_set, 1)

                def tail(i, b, first):
                    dve.wait_ge(h_turned, i + 1)
                    v.tensor_copy(ht[:, b], pt_h[:, :, :]).then_inc(ht_set, 1)

                def result(i, b, first):
                    dve.wait_ge(d_prod, i + 2)
                    if not first:
                        dve.wait_ge(added, i * 16 - 16)
                    v.tensor_copy(yo[:, b, SUP:D], pd[1][:, :]).then_inc(yo_dve, 1)

                def step(i, b, first, last):
                    if not (first and b == 0):
                        tail(i - 1, 1 - b, False)
                    hidden(i, b, first)
                    if not last:
                        turn(i + 1, 1 - b)
                    if not (first and b == 0):
                        result(i - 1, 1 - b, first)

                turn(0, 0)
                for b in range(2):
                    step(b, b, True, False)
                with dve.Fori(1, NT // 2 - 1) as i:
                    for b in range(2):
                        step(i * 2 + b, b, False, False)
                for b in range(2):
                    step(NT - 2 + b, b, False, b == 1)
                tail(NT - 1, 1, False)
                result(NT - 1, 1, False)

            @block.scalar
            def _(act):
                def turn_b(i, b):
                    act.wait_ge(x_turned, i + 1)
                    nc.scalar.copy(xgt[:, b, 0:4, :], pt_x[0][:, :, :]).then_inc(xt_act, 1)

                def step(i, b, first, last):
                    act.wait_ge(gu_prod, i + 1)
                    if not first:
                        act.wait_ge(h_set, i - 1)
                    nc.scalar.activation(sl[:, b, :], pg[b][:, 0, :], ACT.Silu).then_inc(silu_set, 1)
                    if not last:
                        turn_b(i + 1, 1 - b)
                    if not (first and b == 0):
                        result(i - 1, 1 - b, first)

                def result(i, b, first):
                    act.wait_ge(d_prod, i + 2)
                    if not first:
                        act.wait_ge(added, i * 16 - 16)
                    nc.scalar.copy(yo[:, b, 0:SUP], pd[0][:, :]).then_inc(yo_act, 1)

                act.wait_ge(lists_set, 1)
                turn_b(0, 0)
                for b in range(2):
                    step(b, b, True, False)
                with act.Fori(1, NT // 2 - 1) as i:
                    for b in range(2):
                        step(i * 2 + b, b, False, False)
                for b in range(2):
                    step(NT - 2 + b, b, False, b == 1)
                result(NT - 1, 1, False)

            @block.tensor
            def _(pe):
                t = nc.tensor
                pe.sem_inc(d_prod, 1)
                pe.wait_ge(oh_set, 1)
                flat = msk[:].rearrange("p t e -> p (t e)")
                t.matmul(pd[0][:, 0:TILES * E], below[:], flat, start=True, stop=True)
                t.matmul(pd[1][:, 0:TILES * E], ones2[:], flat, start=True, stop=True).then_inc(cnt_prod, 1)

                for k in range(2):
                    pe.wait_ge(hot_set, k + 1)
                    for c in range(TILES):
                        mm = t.matmul(p_ls[:, :, :].rearrange("p a b -> p (a b)"), rowhot[:, k, c, :],
                                      tilehot[:, k, c].rearrange("p a b -> p (a b)"), start=(k == 0 and c == 0),
                                      stop=(k == 1 and c == TILES - 1))
                mm.then_inc(list_prod, 1)

                def turn(i, b, first):
                    pe.wait_ge(xg_in[b], (i - b) * (16 // GS) + 16)
                    if not first:
                        pe.wait_ge(xt_act, i)
                        pe.wait_ge(xt_dve, i)
                    for k in range(KD):
                        mm = t.transpose(pt_x[k // 4][:, k % 4, :], xg[:, b, k:D:KD], ident[:])
                    mm.then_inc(x_turned, 1)

                def gate_up(i, b, first):
                    expert = pe.value_load(tab[0:1, 1, bass.ds(i, 1)], min_val=1, max_val=E)
                    slot = pe.value_load(tab[0:1, 0, bass.ds(i, 1)], min_val=0, max_val=3)
                    pe.wait_ge(weights_ready, expert)
                    pe.wait_ge(xt_act, i + 1)
                    pe.wait_ge(xt_dve, i + 1)
                    if not first:
                        pe.wait_ge(h_set, i - 1)
                    w = w_slots[:, slot, 0:2 * KD * FF].rearrange("p (m k f) -> p k m f", m=2, k=KD)
                    for k in range(KD):
                        mm = t.matmul(pg[b][:, :, :], xgt[:, b, k, :], w[:, k], start=(k == 0), stop=(k == KD - 1))
                    mm.then_inc(gu_prod, 1)

                def turn_hidden(i, b, first):
                    pe.wait_ge(h_set, i + 1)
                    if not first:
                        pe.wait_ge(ht_set, i)
                    for k in range(2):
                        mm = t.transpose(pt_h[:, k, :], hh[:, b, k:FF:2], ident[:])
                    mm.then_inc(h_turned, 1)

                def down(i, b, first):
                    slot = pe.value_load(tab[0:1, 0, bass.ds(i, 1)], min_val=0, max_val=3)
                    pe.wait_ge(ht_set, i + 1)
                    if not first:
                        pe.wait_ge(yo_act, i)
                        pe.wait_ge(yo_dve, i)
                    w = w_slots[:, slot, 2 * KD * FF:].rearrange("p (k n) -> p k n", k=2)
                    for m in range(2):
                        for k in range(2):
                            mm = t.matmul(pd[m][:, :], ht[:, b, k, :], w[:, k, m * SUP:(m + 1) * SUP], start=(k == 0), stop=(k == 1))
                    mm.then_inc(d_prod, 1)

                def step(i, g, start=False, last=False):
                    b, begun = g % 2, not (start and g == 0)
                    gate_up(i, b, start and g < 2)
                    if begun:
                        turn_hidden(i - 1, 1 - b, start and g < 2)
                    if not last:
                        turn(i + 1, (g + 1) % GS, False)
                    if begun:
                        down(i - 1, 1 - b, start and g < 2)

                pe.wait_ge(te_set, 3)
                turn(0, 0, True)
                for g in range(GS):
                    step(g, g, start=True)
                with pe.Fori(1, NT // GS - 1) as i:
                    for g in range(GS):
                        step(i * GS + g, g)
                for g in range(GS):
                    step(NT - GS + g, g, last=(g == GS - 1))
                turn_hidden(NT - 1, 1, False)
                down(NT - 1, 1, False)

        with phase() as ph:
            pt = Place(nc, base)
            SL = 4
            zi = sb("zi", [P, SL, D], where=pt)
            zo = sb("zo", [P, SL, D], where=pt)
            g2_row, b2_row = sb("g2_row", [P, D], where=pt), sb("b2_row", [P, D], where=pt)
            st = sb("st2", [P, SL, 2, 6], where=pt)
            ag = sb("ag2", [P, SL, 2], where=pt)
            rs = sb("rs2", [P, SL, 2], where=pt)
            nh, spare = sb("nh", [P, 1], where=pt), sb("spare_g", [P, 1], where=pt)
            (row_in, nh_set, var_set, rstd_set, centred, scaled, out_set, gdch) = sems("""row2_in nh_set var2_set rstd2_set centred
             scaled out_set gdch""")
            acc_in = [phase_sem(f"acc_in{i}") for i in range(SL)]
            y_stored = [phase_sem(f"y_stored{i}") for i in range(SL)]
            block = ph.enter_context(nc.Block())

            @block.sync
            def _(sp):
                for dst, name in ((g2_row, "ln2_g"), (b2_row, "ln2_b")):
                    sp.dma_start(dst[:], bass.AP(tensor=a[name].tensor, offset=0, ap=[[0, P], [1, D]])).then_inc(row_in, 16)
                for b in range(SL):
                    sp.dma_start(zi[:, b, :], acc_dram[b * P:(b + 1) * P, :]).then_inc(acc_in[b], 16)
                with sp.Fori(0, CH // SL - 1) as i:
                    for b in range(SL):
                        sp.wait_ge(scaled, i * SL + b + 1)
                        sp.dma_start(zi[:, b, :], acc_dram[bass.ds((i * SL + SL + b) * P, P), :]).then_inc(acc_in[b], 16)
                sp.wait_ge(scaled, CH - SL + 1)
                sp.dma_start(zi[0:NS, 0, :], acc_dram[SEQ:SEQ + NS, :]).then_inc(acc_in[0], 16)

            @block.scalar
            def _(act):
                def scale(c, b, turn, n=P):
                    act.wait_ge(centred, c + 1)
                    act.wait_ge(rstd_set, c + 1)
                    if not (isinstance(turn, int) and turn == 0):
                        act.wait_ge(y_stored[b], turn * 16)
                    nc.scalar.mul(zo[0:n, b, :], zi[0:n, b, :], rs[0:n, b, 1:2]).then_inc(scaled, 1)

                def store(c, b):
                    act.wait_ge(out_set, c + 1)
                    act.dma_start(o["y_prompt"][0, bass.ds(c * P, P), :], zo[:, b, :]).then_inc(y_stored[b], 16)

                for b in range(SL):
                    scale(b, b, 0)
                    if b > 1:
                        store(b - 2, b - 2)
                with act.Fori(1, CH // SL) as i:
                    for b in range(SL):
                        store(i * SL + b - 2, (b - 2) % SL)
                        scale(i * SL + b, b, i)
                store(CH - 2, SL - 2)
                scale(CH, 0, CH // SL, NS)
                store(CH - 1, SL - 1)
                act.wait_ge(out_set, CH + 1)
                act.dma_start(o["y_sample"][:, 0, :], zo[0:NS, 0, :]).then_inc(y_stored[0], 16)
                act.wait_ge(y_stored[0], (CH // SL + 1) * 16)
                for b in range(1, SL):
                    act.wait_ge(y_stored[b], CH // SL * 16)

            @block.gpsimd
            def _(gp):
                gp.memset(nh[:], -0.5).then_inc(nh_set, 1)
                gp.wait_ge(nh_set, 1)
                gp.wait_ge(row_in, 32)

                def root(c, b, n=P):
                    gp.wait_ge(var_set, c + 1)
                    gp.tensor_tensor(rs[0:n, b, 1:2], rs[0:n, b, 0:1], nh[0:n], ALU.pow).then_inc(rstd_set, 1)

                def shift(c, b, n=P):
                    gp.wait_ge(scaled, c + 1)
                    gp.tensor_tensor(zo[0:n, b, :], zo[0:n, b, :], b2_row[0:n, :], ALU.add).then_inc(out_set, 1)

                for b in range(SL):
                    root(b, b)
                    if b:
                        shift(b - 1, b - 1)
                with gp.Fori(1, CH // SL) as i:
                    for b in range(SL):
                        root(i * SL + b, b)
                        shift(i * SL + b - 1, (b - 1) % SL)
                root(CH, 0, NS)
                shift(CH - 1, SL - 1)
                shift(CH, 0, NS)

            @block.vector
            def _(dve):
                v = nc.vector
                ch = Chain(dve, gdch)

                def norm(c, b, turn, n=P):
                    dve.wait_ge(acc_in[b], (turn + 1) * 16)
                    for m in range(2):
                        ch.mark(v.bn_stats(st[0:n, b, m, :], zi[0:n, b, m * SUP:(m + 1) * SUP]))
                    ch.settle()
                    v.memset(spare[:], 0.0)
                    ch(v.bn_aggr(ag[0:n, b, :], st[0:n, b]))
                    if not (isinstance(turn, int) and turn == 0):
                        dve.wait_ge(scaled, c - SL + 1)
                    v.tensor_scalar(rs[0:n, b, 0:1], ag[0:n, b, 1:2], EPS, None, ALU.add).then_inc(var_set, 1)
                    v.scalar_tensor_tensor(zi[0:n, b, :], zi[0:n, b, :], ag[0:n, b, 0:1], g2_row[0:n, :], ALU.subtract,
                                           ALU.mult).then_inc(centred, 1)

                dve.wait_ge(row_in, 32)
                for b in range(SL):
                    norm(b, b, 0)
                with dve.Fori(1, CH // SL) as i:
                    ch.enter(i - 1, 3 * SL)
                    for b in range(SL):
                        norm(i * SL + b, b, i)
                    ch.leave(CH // SL - 1)
                norm(CH, 0, CH // SL, NS)


INS = ["x_prompt", "x_sample", "state_ssm_re", "state_ssm_im", "w_in", "w_out", "ln_v_g", "ln_v_b", "w_s", "b_s",
       "ssm_a_re", "ssm_a_im", "ssm_log_dt", "ssm_b_re", "ssm_b_im", "ssm_c_re", "ssm_c_im", "ssm_d", "w_glu",
       "b_glu", "ln1_g", "ln1_b", "ln2_g", "ln2_b", "w_router", "router_bias", "w_gate", "w_up", "w_down"]
OUTS = [("y_prompt", (1, SEQ, D)), ("y_sample", (NS, 1, D)), ("re_prompt", (1, 1, G, N)), ("im_prompt", (1, 1, G, N)),
        ("re_sample", (1, NS, G, N)), ("im_sample", (1, NS, G, N)), ("v_sample", (1, NS, 1, WA))]


def kernel(**inputs):
    import numpy as np
    from concourse import bacc
    from concourse.bass_utils import run_bass_kernel_spmd

    nc = bacc.Bacc("TRN2", target_bir_lowering=False, num_devices=1)
    arrays = {f"in_{n}": np.ascontiguousarray(inputs[n]) for n in INS}
    a = {n: nc.dram_tensor(f"in_{n}", arrays[f"in_{n}"].shape, F32, kind="ExternalInput").ap() for n in INS}
    o = {n: nc.dram_tensor(f"out_{n}", shape, F32, kind="ExternalOutput").ap() for n, shape in OUTS}
    hybrid_step(nc, a, o)
    r = run_bass_kernel_spmd(nc, [arrays], core_ids=[0])
    return tuple(r.results[0][f"out_{n}"] for n, _ in OUTS)
```
